# Optimizing a Trainium2 kernel written in Bass

```python
import jax
import jax.numpy as jnp
from jax import lax
import numpy as np

D_MODEL = 1024
BATCH = 1
SEQ = 1024
DEPTH = 1

FOX_HEADS = 8
FOX_HEAD_DIM = 64
FOX_WIDTH = FOX_HEADS * FOX_HEAD_DIM
Q_BLOCK = 128
RWKV_HEADS = 8
RWKV_HEAD_DIM = 64
RWKV_WIDTH = RWKV_HEADS * RWKV_HEAD_DIM
DECAY_LORA = 64
AAA_LORA = 64
GATE_LORA = 128
LN_X_EPS = 64e-5
N_BRANCHES = 2
SHIFT_WIDTH = 3 * RWKV_WIDTH + DECAY_LORA + AAA_LORA + GATE_LORA
IN_SPLITS = [FOX_WIDTH, 2 * FOX_WIDTH, 3 * FOX_WIDTH, 3 * FOX_WIDTH + FOX_HEADS,
             3 * FOX_WIDTH + FOX_HEADS + SHIFT_WIDTH]
D_IN = 3 * FOX_WIDTH + FOX_HEADS + SHIFT_WIDTH + N_BRANCHES * D_MODEL
RWKV_SPLITS = [RWKV_WIDTH, 2 * RWKV_WIDTH, 3 * RWKV_WIDTH, 3 * RWKV_WIDTH + DECAY_LORA,
               3 * RWKV_WIDTH + DECAY_LORA + AAA_LORA]
N_GROUPS = 4
EXPERTS_PER_GROUP = 8
N_EXPERTS = N_GROUPS * EXPERTS_PER_GROUP
TOP_K = 2
D_EXPERT = 512
MOE_BLOCK = 128
NORM_EPS = 1e-6

kernel_name = 'fox_rwkv7_hmoe_adaln_block'

def rms_norm(x, g):
    xf = x.astype(jnp.float32)
    y = xf * lax.rsqrt(jnp.mean(xf * xf, axis=-1, keepdims=True) + NORM_EPS)
    return (y * g.astype(jnp.float32)).astype(x.dtype)

def token_shift(p, mu):
    prev = jnp.pad(p, ((0, 0), (1, 0), (0, 0)))[:, :-1]
    return p + (prev - p) * mu

def fox_attention(q, k, v, log_f):
    b, s, _ = q.shape
    nqb = s // Q_BLOCK
    scale = FOX_HEAD_DIM ** -0.5
    qh = q.reshape(b, nqb, Q_BLOCK, FOX_HEADS, FOX_HEAD_DIM).transpose(1, 0, 3, 2, 4)
    kh = k.reshape(b, s, FOX_HEADS, FOX_HEAD_DIM).transpose(0, 2, 1, 3)
    vh = v.reshape(b, s, FOX_HEADS, FOX_HEAD_DIM).transpose(0, 2, 1, 3)
    cum = jnp.cumsum(log_f, axis=1).transpose(0, 2, 1)
    cum_q = cum.reshape(b, FOX_HEADS, nqb, Q_BLOCK).transpose(2, 0, 1, 3)
    k_pos = jnp.arange(s)

    def block(args):
        q_blk, c_blk, i = args
        logits = jnp.einsum('bhqd,bhkd->bhqk', q_blk, kh).astype(jnp.float32) * scale
        logits = logits + c_blk[..., None] - cum[:, :, None, :]
        q_pos = i * Q_BLOCK + jnp.arange(Q_BLOCK)
        logits = jnp.where(k_pos[None, :] <= q_pos[:, None], logits, -jnp.inf)
        probs = jax.nn.softmax(logits, axis=-1).astype(vh.dtype)
        return jnp.einsum('bhqk,bhkd->bhqd', probs, vh)

    o = lax.map(block, (qh, cum_q, jnp.arange(nqb)))
    return o.transpose(1, 0, 3, 2, 4).reshape(b, s, FOX_WIDTH)

def rwkv7_scan(r, w, k, v, a_vec, b_vec):
    b, s, h, n = r.shape
    xs = tuple(t.astype(jnp.float32).transpose(1, 0, 2, 3) for t in (r, w, k, v, a_vec, b_vec))
    state0 = jnp.zeros((b, h, n, n), jnp.float32)

    def step(state, inp):
        r_t, w_t, k_t, v_t, a_t, b_t = inp
        sa = jnp.einsum('bhij,bhj->bhi', state, a_t)
        state = (state * w_t[:, :, None, :] + sa[..., None] * b_t[:, :, None, :]
                 + v_t[..., None] * k_t[:, :, None, :])
        return state, jnp.einsum('bhij,bhj->bhi', state, r_t)

    _, y = lax.scan(step, state0, xs)
    return y.transpose(1, 0, 2, 3)

def rwkv7_branch(p, w0, w2, a0, a2, g2, k_k, k_a, r_k, ln_g, ln_b):
    b, s, _ = p.shape
    r, k, v, wd, ad, gd = jnp.split(p, RWKV_SPLITS, axis=-1)
    log_w = -jax.nn.softplus(-(w0 + jnp.tanh(wd) @ w2).astype(jnp.float32)) - 0.5
    decay = jnp.exp(-jnp.exp(log_w))
    a = jax.nn.sigmoid(a0 + ad @ a2)
    g = jax.nn.sigmoid(gd) @ g2
    heads = lambda t: t.reshape(b, s, RWKV_HEADS, RWKV_HEAD_DIM)
    kk = heads(k * k_k).astype(jnp.float32)
    kk = kk / jnp.maximum(jnp.sqrt(jnp.sum(kk * kk, axis=-1, keepdims=True)), 1e-12)
    k = k * (1.0 + (a - 1.0) * k_a)
    rh, kh, vh, ah = heads(r), heads(k), heads(v), heads(a)
    y = rwkv7_scan(rh, heads(decay), kh, vh, -kk, kk * ah)
    mu = jnp.mean(y, axis=-1, keepdims=True)
    var = jnp.mean(jnp.square(y - mu), axis=-1, keepdims=True)
    yn = ((y - mu) * lax.rsqrt(var + LN_X_EPS)).reshape(b, s, RWKV_WIDTH) * ln_g + ln_b
    bonus = jnp.sum((rh * kh * r_k).astype(jnp.float32), axis=-1, keepdims=True) * vh.astype(jnp.float32)
    out = (yn + bonus.reshape(b, s, RWKV_WIDTH)) * g
    return out.astype(p.dtype)

def hier_moe(h, rg_w, rg_b, re_w, re_b, w1, w3, w2):
    t, d = h.shape
    hf = h.astype(jnp.float32)
    group_prob = jax.nn.softmax(hf @ rg_w.astype(jnp.float32) + rg_b, axis=-1)
    g_p, g_idx = lax.top_k(group_prob, 1)
    exp_logits = (hf @ re_w.astype(jnp.float32) + re_b).reshape(t, N_GROUPS, EXPERTS_PER_GROUP)
    sel = exp_logits[jnp.arange(t), g_idx[:, 0]]
    e_p, e_idx = lax.top_k(jax.nn.softmax(sel, axis=-1), TOP_K)
    weights = g_p * e_p / jnp.sum(e_p, axis=-1, keepdims=True)
    expert_id = g_idx * EXPERTS_PER_GROUP + e_idx

    m = t * TOP_K
    flat_e = expert_id.reshape(m)
    flat_w = weights.reshape(m)
    flat_tok = jnp.arange(m) // TOP_K
    order = jnp.argsort(flat_e)
    e_s, tok_s, w_s = flat_e[order], flat_tok[order], flat_w[order]
    counts = jnp.bincount(flat_e, length=N_EXPERTS)
    padded = (counts + MOE_BLOCK - 1) // MOE_BLOCK * MOE_BLOCK
    seg_start = jnp.cumsum(counts) - counts
    pad_end = jnp.cumsum(padded)
    pad_start = pad_end - padded
    dest = pad_start[e_s] + (jnp.arange(m) - seg_start[e_s])
    n_blocks = -(-m // MOE_BLOCK) + N_EXPERTS
    rows = n_blocks * MOE_BLOCK
    row_tok = jnp.full((rows,), t, jnp.int32).at[dest].set(tok_s.astype(jnp.int32))
    row_w = jnp.zeros((rows,), h.dtype).at[dest].set(w_s.astype(h.dtype))
    blk_e = jnp.minimum(jnp.searchsorted(pad_end, jnp.arange(n_blocks) * MOE_BLOCK, side='right'),
                        N_EXPERTS - 1)
    h_pad = jnp.concatenate([h, jnp.zeros((1, d), h.dtype)], axis=0)
    x_in = h_pad[row_tok].reshape(n_blocks, MOE_BLOCK, d)

    def expert_block(args):
        xb, e = args
        return (jax.nn.silu(xb @ w1[e]) * (xb @ w3[e])) @ w2[e]

    out = lax.map(expert_block, (x_in, blk_e)).reshape(rows, d)
    y = jax.ops.segment_sum(out * row_w[:, None], row_tok, num_segments=t + 1)
    return y[:t]

def setup_inputs(seed: int = 0) -> dict:
    key = jax.random.key(seed)
    ks = jax.random.split(key, 32)
    L, D = DEPTH, D_MODEL

    def nrm(i, shape, scale):
        return scale * jax.random.normal(ks[i], shape, jnp.float32)

    def uni(i, shape, lo, hi):
        return jax.random.uniform(ks[i], shape, jnp.float32, lo, hi)

    return {
        'x': nrm(0, (BATCH, SEQ, D), 1.0),
        'c': nrm(1, (BATCH, D), 1.0),
        'ada_w': nrm(2, (L, D, 6 * D), 0.5 * D ** -0.5),
        'ada_b': nrm(3, (L, 6 * D), 0.02),
        'norm1_g': 1.0 + nrm(4, (L, D), 0.02),
        'w_in': nrm(5, (L, D, D_IN), D ** -0.5),
        'fox_forget_b': uni(6, (L, FOX_HEADS), 1.0, 5.0),
        'shift_mu': uni(7, (L, SHIFT_WIDTH), 0.0, 1.0),
        'rwkv_w0': uni(8, (L, RWKV_WIDTH), -6.0, -1.0),
        'rwkv_w2': nrm(9, (L, DECAY_LORA, RWKV_WIDTH), 0.5 * DECAY_LORA ** -0.5),
        'rwkv_a0': nrm(10, (L, RWKV_WIDTH), 0.1),
        'rwkv_a2': nrm(11, (L, AAA_LORA, RWKV_WIDTH), AAA_LORA ** -0.5),
        'rwkv_g2': nrm(12, (L, GATE_LORA, RWKV_WIDTH), GATE_LORA ** -0.5),
        'rwkv_k_k': 0.85 + nrm(13, (L, RWKV_WIDTH), 0.02),
        'rwkv_k_a': 1.0 + nrm(14, (L, RWKV_WIDTH), 0.02),
        'rwkv_r_k': nrm(15, (L, RWKV_HEADS, RWKV_HEAD_DIM), 0.1),
        'ln_x_g': 1.0 + nrm(16, (L, RWKV_WIDTH), 0.02),
        'ln_x_b': nrm(17, (L, RWKV_WIDTH), 0.02),
        'w_out_fox': nrm(18, (L, FOX_WIDTH, D), FOX_WIDTH ** -0.5),
        'w_out_rwkv': nrm(19, (L, RWKV_WIDTH, D), RWKV_WIDTH ** -0.5),
        'w_o': nrm(20, (L, D, D), D ** -0.5),
        'norm2_g': 1.0 + nrm(21, (L, D), 0.02),
        'router_group_w': nrm(22, (L, D, N_GROUPS), D ** -0.5),
        'router_group_b': nrm(23, (L, N_GROUPS), 0.01),
        'router_expert_w': nrm(24, (L, D, N_EXPERTS), D ** -0.5),
        'router_expert_b': nrm(25, (L, N_EXPERTS), 0.01),
        'exp_w1': nrm(26, (L, N_EXPERTS, D, D_EXPERT), D ** -0.5),
        'exp_w3': nrm(27, (L, N_EXPERTS, D, D_EXPERT), D ** -0.5),
        'exp_w2': nrm(28, (L, N_EXPERTS, D_EXPERT, D), D_EXPERT ** -0.5),
        'final_g': 1.0 + nrm(29, (D,), 0.02),
    }

def reference(x, c, ada_w, ada_b, norm1_g, w_in, fox_forget_b, shift_mu, rwkv_w0, rwkv_w2,
              rwkv_a0, rwkv_a2, rwkv_g2, rwkv_k_k, rwkv_k_a, rwkv_r_k, ln_x_g, ln_x_b,
              w_out_fox, w_out_rwkv, w_o, norm2_g, router_group_w, router_group_b,
              router_expert_w, router_expert_b, exp_w1, exp_w3, exp_w2, final_g):
    b, s, d = x.shape
    for l in range(DEPTH):
        mod = jax.nn.silu(c) @ ada_w[l] + ada_b[l]
        shift1, scale1, gate1, shift2, scale2, gate2 = [m[:, None, :] for m in jnp.split(mod, 6, axis=-1)]

        h = rms_norm(x, norm1_g[l]) * (1.0 + scale1) + shift1
        p = h @ w_in[l]
        q, k, v, f_logit, p_rwkv, gate_logit = jnp.split(p, IN_SPLITS, axis=-1)
        log_f = jax.nn.log_sigmoid((f_logit + fox_forget_b[l]).astype(jnp.float32))
        o_fox = fox_attention(q, k, v, log_f)
        o_rwkv = rwkv7_branch(token_shift(p_rwkv, shift_mu[l]), rwkv_w0[l], rwkv_w2[l], rwkv_a0[l],
                              rwkv_a2[l], rwkv_g2[l], rwkv_k_k[l], rwkv_k_a[l], rwkv_r_k[l],
                              ln_x_g[l], ln_x_b[l])
        g_fox, g_rwkv = jnp.split(jax.nn.sigmoid(gate_logit), N_BRANCHES, axis=-1)
        merged = g_fox * (o_fox @ w_out_fox[l]) + g_rwkv * (o_rwkv @ w_out_rwkv[l])
        x = x + gate1 * (merged @ w_o[l])

        h2 = rms_norm(x, norm2_g[l]) * (1.0 + scale2) + shift2
        y = hier_moe(h2.reshape(b * s, d), router_group_w[l], router_group_b[l], router_expert_w[l],
                     router_expert_b[l], exp_w1[l], exp_w3[l], exp_w2[l])
        x = x + gate2 * y.reshape(b, s, d)
    return rms_norm(x, final_g)


_drawn_inputs = setup_inputs


def setup_inputs(seed=0):
    import zlib

    import numpy as np

    out = dict(_drawn_inputs(seed))
    spreads = {}
    factors = {'ada_b': 3.023,
     'norm1_g': 8.0,
     'rwkv_w2': 64.0,
     'rwkv_a0': 8.0,
     'rwkv_k_k': 64.0,
     'rwkv_k_a': 8.0,
     'ln_x_g': 64.0,
     'ln_x_b': 64.0,
     'norm2_g': 41.032,
     'router_group_b': 64.0,
     'router_expert_b': 64.0,
     'final_g': 8.913,
     'fox_forget_b': 8.0,
     'rwkv_w0': 8.0,
     'w_out_fox': 4.354}
    for name, (base, spread) in spreads.items():
        noise = np.random.default_rng([zlib.crc32(name.encode()), seed]).standard_normal(out[name].shape)
        drawn = base * np.exp(spread * noise) if base else spread * noise
        out[name] = jnp.asarray(drawn.astype(out[name].dtype))
    for name, factor in factors.items():
        out[name] = (out[name] * factor).astype(out[name].dtype)
    return out
```

```python
from contextlib import ExitStack

import numpy as np

import concourse.bass as bass
from concourse import mybir

F32 = mybir.dt.float32
I32 = mybir.dt.int32
ALU = mybir.AluOpType
ACT = mybir.ActivationFunctionType
AX = mybir.AxisListType

P = 128
D = 1024
S = 1024
TT = S // P
KT = D // P
H = 8
HD = 64
W = H * HD
NC5 = 512
LORA = 64
GLORA = 128
SHIFT = 3 * W + 2 * LORA + GLORA
COL_V = 2 * W
COL_F = 3 * W
COL_R = COL_F + H
COL_G = COL_R + SHIFT
CHUNK = 64
G, EPG = 4, 8
E = G * EPG
FE = 512
NEG = -1.0e30
EPS = 1e-6
LN_EPS = 64e-5
EXPM05 = float(np.exp(-0.5))
OVERFLOW_BLOCKS = 2 * S // P
BLOCKS = E + OVERFLOW_BLOCKS
ROWS = BLOCKS * P
LASTING = ("w13_in0", "w13_in1", "w2_in0", "w2_in1")
SOFTWARE_DMA = ("x_in0", "x_in1", "g1_in", "fb_in", "wf_in", "g2_in", "zrow_out", "mu_in", "x_mid_out0", "x_mid_out1",
                "h_mid_out0", "h_mid_out1", "table_zero", "scattered", "x_in_e0", "x_in_e1", "y_out0", "y_out1",
                "cb_rows_in0", "cb_rows_in1", "cb_rows_in2")


class Signals:

    POOL = 100

    def __init__(self, nc, ctx):
        self.nc = nc
        self.pool = [ctx.enter_context(nc.semaphore(f"stage_{i}")) for i in range(self.POOL)]
        self.lasting = {n: ctx.enter_context(nc.semaphore(n)) for n in LASTING + SOFTWARE_DMA}
        self.names = {}

    def __call__(self, name):
        if name in self.lasting:
            return self.lasting[name]
        return self.pool[self.names.setdefault(name, len(self.names))]

    def next_stage(self, stage):
        used = [self.pool[i].num for i in range(len(self.names))]
        self.names = {}
        assert used == list(range(used[0], used[0] + len(used)))
        with self.nc.Block(f"{stage}_cleared") as block:
            @block.gpsimd
            def _(pool):
                pool.sem_clear(range(used[0], used[0] + len(used)))


class Link:

    def __init__(self, eng, sem, start=0):
        self.eng, self.sem, self.n = eng, sem, start

    def __call__(self, ins):
        self.n += 1
        ins.then_inc(self.sem, 1)
        self.eng.wait_ge(self.sem, self.n)


def project(nc, sig, bank, const, keep, ins, dram):
    ident, ones_row = const["ident"], const["ones_row"]
    q_t, k_t, v_tok, ncum = keep["q_t"], keep["k_t"], keep["v_tok"], keep["ncum"]
    mod_bc = keep["mod_bc"]
    ada = ins["ada_w"][0].rearrange("(p k) n -> p k n", k=KT)
    w_in = ins["w_in"][0].rearrange("(k p) n -> p k n", p=P)
    chunks = [("ada", ada[:, :, j * NC5:(j + 1) * NC5]) for j in range(4)]
    chunks += [("qk", w_in[:, :, j * NC5:(j + 1) * NC5]) for j in range(2)]
    chunks += [("v", w_in[:, :, COL_V:COL_V + NC5])]
    chunks += [("rwkv", w_in[:, :, COL_R + j:COL_R + min(j + NC5, SHIFT)]) for j in range(0, SHIFT, NC5)]
    chunks += [("gate", w_in[:, :, COL_G + j:COL_G + j + NC5]) for j in range(0, 2 * D, NC5)]
    chunks += [("ada", ada[:, :, j * NC5:(j + 1) * NC5]) for j in range(4, 12)]
    RING = 3
    first_fill, fills = [], 0
    for kind, _ in chunks:
        first_fill.append(fills)
        fills += 0 if kind == "ada" else 8
    with ExitStack() as ctx:
        sb = lambda name, shape: ctx.enter_context(nc.sbuf_tensor(name, shape, F32))
        ring = sb("w_ring", [P, RING, KT, NC5])
        x_in = sb("x_in", [P, 2, D])
        sq = mod_bc[:, 0, :]
        h_t = sb("h_t", [P, KT, S])
        mod_row = sb("mod_row", [1, 6 * D])
        stage = sb("stage", [P, 3, NC5])
        c_col = sb("c_col", [P, KT])
        c_sig = sb("c_sig", [P, KT])
        g1_col = sb("g1_col", [P, KT])
        shift_col = sb("shift_col", [P, KT])
        scale_col = sb("scale_col", [P, KT])
        ss = sb("ss", [P, TT])
        w_f = sb("w_f", [P, KT, H])
        f_b = sb("f_b", [H, 1])
        f_nb = sb("f_nb", [H, 1])
        f_abs = x_in[0:H, 0, :]
        f_min = sq[0:H, :]
        block = ctx.enter_context(nc.Block("project"))

        @block.sync
        def _(sp):
            sp.dma_start(c_col[:], ins["c"][0].rearrange("(p k) -> p k", k=KT)).then_inc(sig("c_in"), 16)
            sp.dma_start(mod_row[:], ins["ada_b"]).then_inc(sig("adab_in"), 16)
            for j, (kind, src) in enumerate(chunks):
                if j >= RING:
                    sp.wait_ge(sig("chunk_used"), j - RING + 1)
                sp.dma_start(ring[:, j % RING, :, 0:src.shape[2]], src).then_inc(sig(f"chunk_in{j % RING}"), 16)

        @block.gpsimd
        def _(pool):
            for t in range(2):
                pool.dma_start(x_in[:, t, :], ins["x"][0, t * P:(t + 1) * P, :]).then_inc(sig(f"x_in{t}"), 16)
            pool.dma_start(g1_col[:], ins["norm1_g"][0].rearrange("(k p) -> p k", p=P), allow_slow_non_contiguous=True).then_inc(sig("g1_in"), 16)
            pool.dma_start(f_b[:], ins["fox_forget_b"][0].rearrange("(h a) -> h a", a=1)).then_inc(sig("fb_in"), 16)
            pool.dma_start(w_f[:], w_in[:, :, COL_F:COL_R]).then_inc(sig("wf_in"), 16)
            pool.dma_start(mod_bc[:, 4, :], ins["norm2_g"].partition_broadcast(P).rearrange("p a n -> p (a n)")).then_inc(sig("g2_in"), 16)
            nc.gpsimd.memset(sq[0:1, :], 0.0).then_inc(sig("zrow"), 1)
            pool.wait_ge(sig("zrow"), 1)
            pool.dma_start(dram["p_rwkv"][0:1, 0:D], sq[0:1, :]).then_inc(sig("zrow_out"), 16)
            pool.dma_start(dram["p_rwkv"][0:1, D:SHIFT], sq[0:1, 0:SHIFT - D]).then_inc(sig("zrow_out"), 16)
            for t in range(TT):
                pool.wait_ge(sig("x_ms"), t + 1)
                nc.gpsimd.tensor_tensor(ss[:, t:t + 1], ss[:, t:t + 1], const["neghalf"][:, 0:1], ALU.pow).then_inc(sig("x_rstd"), 1)
                if 1 <= t < TT - 1:
                    pool.wait_ge(sig("xn_transposed"), t)
                    pool.dma_start(x_in[:, (t + 1) % 2, :], ins["x"][0, (t + 1) * P:(t + 2) * P, :]).then_inc(sig(f"x_in{(t + 1) % 2}"), 16)

        @block.vector
        def _(dve):
            link = Link(dve, sig("dve_link_a"))
            dve.wait_ge(sig("c_in"), 16)
            dve.wait_ge(sig("c_sig"), 1)
            nc.vector.tensor_tensor(c_sig[:], c_sig[:], c_col[:], ALU.mult).then_inc(sig("c_silu"), 1)

            def mod_chunk(j):
                dve.wait_ge(sig("mod_full"), j + 1)
                dst = mod_row[0:1, j * NC5:(j + 1) * NC5]
                nc.vector.tensor_tensor(dst, bank[j % 2][0:1, 0:NC5], dst, ALU.add).then_inc(sig("mod_row"), 1)

            dve.wait_ge(sig("adab_in"), 16)
            for j in range(4):
                mod_chunk(j)
            dve.wait_ge(sig("mod_cols"), 1)
            dve.wait_ge(sig("g1_in"), 16)
            nc.vector.tensor_copy(shift_col[:], bank[2][:, 0:KT]).then_inc(sig("cols_ready"), 1)
            nc.vector.scalar_tensor_tensor(out=scale_col[:], in0=bank[2][:, KT:2 * KT], scalar=1.0, in1=g1_col[:],
                                           op0=ALU.add, op1=ALU.mult).then_inc(sig("cols_ready"), 1)
            dve.wait_ge(sig("cols_ready"), 2)
            for t in range(TT):
                dve.wait_ge(sig("x_ss"), t + 1)
                nc.vector.tensor_scalar(ss[:, t:t + 1], ss[:, t:t + 1], 1.0 / D, EPS, ALU.mult, ALU.add).then_inc(sig("x_ms"), 1)
                dve.wait_ge(sig("x_rstd"), t + 1)
                nc.vector.tensor_scalar(x_in[:, t % 2, :], x_in[:, t % 2, :], ss[:, t:t + 1], None, ALU.mult).then_inc(sig("xn_ready"), 1)
                dve.wait_ge(sig("xn_transposed"), t + 1)
                for k in range(KT // 2):
                    nc.vector.tensor_scalar(h_t[:, k, t * P:(t + 1) * P], bank[4 + 2 * (t % 2)][:, k * P:(k + 1) * P],
                                            scale_col[:, k:k + 1], shift_col[:, k:k + 1], ALU.mult, ALU.add).then_inc(sig("h_dve"), 1)
            dve.wait_ge(sig("fb_in"), 16)
            for half in range(2):
                cols = slice(half * NC5, (half + 1) * NC5)
                dve.wait_ge(sig("f_absd"), half + 1)
                nc.vector.tensor_scalar(f_min[:, cols], bank[half][0:H, :], f_b[:], 0.0, ALU.add, ALU.min).then_inc(sig("f_min"), 1)
            dve.wait_ge(sig("f_ln"), 2)
            dve.wait_ge(sig("f_min"), 2)
            link(nc.vector.tensor_tensor(f_min, f_abs, f_min, ALU.subtract))
            link(nc.vector.memset(f_abs, 1.0))
            nc.vector.tensor_tensor_scan(ncum[:], f_abs, f_min, 0.0, ALU.mult, ALU.add).then_inc(sig("ncum"), 1)
            for j in range(4, 12):
                mod_chunk(j)
            dve.wait_ge(sig("g2_in"), 16)
            dve.wait_ge(sig("bc_evac"), 8)
            nc.vector.scalar_tensor_tensor(out=mod_bc[:, 2, :], in0=mod_bc[:, 2, :], scalar=1.0, in1=mod_bc[:, 4, :],
                                           op0=ALU.add, op1=ALU.mult).then_inc(sig("a2_ready"), 1)
            dve.wait_ge(sig("a2_ready"), 1)

        @block.scalar
        def _(act):
            act.wait_ge(sig("c_in"), 16)
            nc.scalar.activation(c_sig[:], c_col[:], ACT.Sigmoid).then_inc(sig("c_sig"), 1)
            act.wait_ge(sig("zrow_out"), 32)
            for t in range(TT):
                act.wait_ge(sig(f"x_in{t % 2}"), 16 * (t // 2 + 1))
                if t >= 1:
                    act.wait_ge(sig("x_ss"), t)
                nc.scalar.activation(sq, x_in[:, t % 2, :], ACT.Square, accum_out=ss[:, t:t + 1]).then_inc(sig("x_ss"), 1)
                act.wait_ge(sig("cols_ready"), 2)
                act.wait_ge(sig("xn_transposed"), t + 1)
                for k in range(KT // 2, KT):
                    nc.scalar.activation(h_t[:, k, t * P:(t + 1) * P], bank[5 + 2 * (t % 2)][:, (k - 4) * P:(k - 3) * P],
                                         ACT.Identity, scale=scale_col[:, k:k + 1], bias=shift_col[:, k:k + 1]).then_inc(sig("h_act"), 1)
            act.wait_ge(sig("fb_in"), 16)
            for half in range(2):
                cols = slice(half * NC5, (half + 1) * NC5)
                act.wait_ge(sig("f_full"), half + 1)
                nc.scalar.activation(f_abs[:, cols], bank[half][0:H, :], ACT.Abs, bias=f_b[:]).then_inc(sig("f_absd"), 1)
            act.wait_ge(sig("f_absd"), 2)
            nc.scalar.activation(f_abs, f_abs, ACT.Exp, scale=-1.0).then_inc(sig("f_exp"), 1)
            act.wait_ge(sig("f_exp"), 1)
            nc.scalar.activation(f_abs, f_abs, ACT.Ln, bias=1.0).then_inc(sig("f_ln"), 1)
            nc.scalar.activation(f_nb[:], f_b[:], ACT.Copy).then_inc(sig("f_ln"), 1)
            staged = 0
            for j, (kind, src) in enumerate(chunks):
                if kind == "ada":
                    continue
                n = src.shape[2]
                for i in range(8):
                    fill = first_fill[j] + i
                    ps = bank[2 + fill % 4]
                    if kind in ("rwkv", "gate") and staged >= 3:
                        act.wait_ge(sig(f"staged_out{staged % 3}"), 16 * (staged // 3))
                    act.wait_ge(sig("proj_full"), fill + 1)
                    if kind == "qk":
                        dst = (q_t, k_t)[j - 4][:, i // 2, (i % 2) * NC5:(i % 2 + 1) * NC5]
                        nc.scalar.activation(dst, ps[:], ACT.Copy).then_inc(sig("proj_evac"), 1)
                    elif kind == "v":
                        nc.scalar.activation(v_tok[:, i, :], ps[:], ACT.Copy).then_inc(sig("proj_evac"), 1)
                    else:
                        buf = stage[:, staged % 3, 0:n]
                        nc.scalar.activation(buf, ps[:, 0:n], ACT.Copy if kind == "rwkv" else ACT.Sigmoid).then_inc(sig("proj_evac"), 1)
                        act.wait_ge(sig("proj_evac"), fill + 1)
                        if kind == "rwkv":
                            dst = dram["p_rwkv"][1 + i * P:1 + (i + 1) * P, (j - 7) * NC5:(j - 7) * NC5 + n]
                        else:
                            dst = dram["gates"][i * P:(i + 1) * P, (j - 11) * NC5:(j - 10) * NC5]
                        act.dma_start(dst, buf).then_inc(sig(f"staged_out{staged % 3}"), 16)
                        staged += 1
            for i in range(8):
                act.wait_ge(sig("bc_full"), i + 1)
                nc.scalar.activation(mod_bc[:, i // 2, (i % 2) * NC5:(i % 2 + 1) * NC5], bank[2 + i % 2][:], ACT.Copy).then_inc(sig("bc_evac"), 1)
            for b in range(3):
                act.wait_ge(sig(f"staged_out{b}"), 16 * ((staged + 2 - b) // 3))

        @block.tensor
        def _(pe):
            def mod_chunk(j, n):
                pe.wait_ge(sig(f"chunk_in{j % RING}"), 16 * (j // RING + 1))
                if n >= 2:
                    pe.wait_ge(sig("mod_row"), n - 1)
                for k in range(KT):
                    last = nc.tensor.matmul(bank[n % 2][0:1, :], c_sig[:, k:k + 1], ring[:, j % RING, k, :],
                                            start=(k == 0), stop=(k == KT - 1))
                last.then_inc(sig("mod_full"), 1)
                pe.wait_ge(sig("mod_full"), n + 1)
                nc.tensor.nop().then_inc(sig("chunk_used"), 1)

            pe.wait_ge(sig("c_silu"), 1)
            for j in range(4):
                mod_chunk(j, j)
            pe.wait_ge(sig("mod_row"), 4)
            for i in range(2 * KT):
                last = nc.tensor.matmul(bank[2][:, i:i + 1], mod_row[0:1, i * P:(i + 1) * P], ones_row[0:1, 0:1],
                                        start=True, stop=True)
            last.then_inc(sig("mod_cols"), 1)
            for t in range(TT):
                pe.wait_ge(sig("xn_ready"), t + 1)
                if t >= 2:
                    pe.wait_ge(sig("h_dve"), 4 * (t - 1))
                    pe.wait_ge(sig("h_act"), 4 * (t - 1))
                for k in range(KT):
                    last = nc.tensor.transpose(bank[4 + 2 * (t % 2) + k // 4][:, (k % 4) * P:(k % 4 + 1) * P],
                                               x_in[:, t % 2, k * P:(k + 1) * P], ident[:])
                last.then_inc(sig("xn_transposed"), 1)
            pe.wait_ge(sig("h_dve"), 4 * TT)
            pe.wait_ge(sig("h_act"), 4 * TT)
            pe.wait_ge(sig("wf_in"), 16)
            for half in range(2):
                for k in range(KT):
                    last = nc.tensor.matmul(bank[half][0:H, :], w_f[:, k, :], h_t[:, k, half * NC5:(half + 1) * NC5],
                                            start=(k == 0), stop=(k == KT - 1))
                last.then_inc(sig("f_full"), 1)
            for j, (kind, src) in enumerate(chunks[:15]):
                if kind == "ada":
                    continue
                n = src.shape[2]
                pe.wait_ge(sig(f"chunk_in{j % RING}"), 16 * (j // RING + 1))
                for i in range(8):
                    fill = first_fill[j] + i
                    if fill >= 4:
                        pe.wait_ge(sig("proj_evac"), fill - 3)
                    ps = bank[2 + fill % 4]
                    for k in range(KT):
                        if kind == "qk":
                            lhs = ring[:, j % RING, k, (i // 2) * P:(i // 2 + 1) * P]
                            rhs = h_t[:, k, (i % 2) * NC5:(i % 2 + 1) * NC5]
                        else:
                            lhs = h_t[:, k, i * P:(i + 1) * P]
                            rhs = ring[:, j % RING, k, 0:n]
                        last = nc.tensor.matmul(ps[:, 0:rhs.shape[1]], lhs, rhs, start=(k == 0), stop=(k == KT - 1))
                    last.then_inc(sig("proj_full"), 1)
                pe.wait_ge(sig("proj_full"), fill + 1)
                nc.tensor.nop().then_inc(sig("chunk_used"), 1)
            pe.wait_ge(sig("f_ln"), 2)
            pe.wait_ge(sig("f_min"), 2)
            for n in range(4, 12):
                mod_chunk(n + 11, n)
            pe.wait_ge(sig("mod_row"), 12)
            pe.wait_ge(sig("proj_evac"), fills)
            for i in range(8):
                if i >= 2:
                    pe.wait_ge(sig("bc_evac"), i - 1)
                nc.tensor.matmul(bank[2 + i % 2][:], ones_row[0:1, :], mod_row[0:1, (4 + i) * NC5:(5 + i) * NC5],
                                 start=True, stop=True).then_inc(sig("bc_full"), 1)


def attend(nc, sig, bank, const, keep, dram):
    q_t, k_t, v_tok, ncum, o_fox = (keep[n] for n in ("q_t", "k_t", "v_tok", "ncum", "o_fox"))
    psum = const["psum"]
    items = [(h, t) for h in range(H) for t in range(TT)]
    with ExitStack() as ctx:
        sb = lambda name, shape: ctx.enter_context(nc.sbuf_tensor(name, shape, F32))
        pick = sb("pick", [H, H, P])
        causal = sb("causal", [P, P])
        gate_bias = sb("gate_bias", [P, 2, S])
        logits = sb("att_logits", [P, 2, S])
        probs = sb("att_probs", [P, 2, S])
        probs_t = sb("att_probs_t", [P, 2, S])
        neg_max = sb("neg_max", [P, len(items)])
        row_sum = sb("row_sum", [P, len(items)])
        zeros = sb("zeros", [P, D])
        block = ctx.enter_context(nc.Block("attend"))

        def scores(n):
            return psum[:, (n % 2) * 2 * NC5:(n % 2 + 1) * 2 * NC5]

        @block.sync
        def _(sp):
            sp.wait_ge(sig("zeros"), 1)
            sp.dma_start(dram["expert_rows"][E * P:ROWS, :].rearrange("(j p) n -> p j n", p=P),
                         zeros[:].unsqueeze(1).to_broadcast([P, OVERFLOW_BLOCKS, D])).then_inc(sig("zeros_out"), 16)
            sp.wait_ge(sig("zeros_out"), 16)

        @block.gpsimd
        def _(pool):
            nc.gpsimd.memset(zeros[:], 0.0).then_inc(sig("zeros"), 1)
            nc.gpsimd.memset(pick[:], 0.0).then_inc(sig("att_const"), 1)
            nc.gpsimd.memset(causal[:], 0.0).then_inc(sig("att_const"), 1)
            pool.wait_ge(sig("att_const"), 2)
            nc.gpsimd.affine_select(out=pick[:], in_=pick[:], compare_op=ALU.not_equal, fill=1.0, base=0,
                                    pattern=[[-1, H], [0, P]], channel_multiplier=1).then_inc(sig("att_const"), 1)
            nc.gpsimd.affine_select(out=causal[:], in_=causal[:], compare_op=ALU.is_ge, fill=NEG, base=0,
                                    pattern=[[-1, P]], channel_multiplier=1).then_inc(sig("att_const"), 1)

        @block.tensor
        def _(pe):
            def bias_half(h, half):
                if 2 * h + half >= 1:
                    pe.wait_ge(sig("bias_rows"), 2 * h + half)
                nc.tensor.matmul(bank[5][:], pick[:, h, :], ncum[:, half * NC5:(half + 1) * NC5],
                                 start=True, stop=True).then_inc(sig("bias_full"), 1)

            def score(n):
                h, t = items[n]
                if n >= 2:
                    pe.wait_ge(sig("scores_read"), n - 1)
                rows = slice((h % 2) * HD, (h % 2 + 1) * HD)
                for lo in range(0, (t + 1) * P, NC5):
                    hi = min(lo + NC5, (t + 1) * P)
                    last = nc.tensor.matmul(scores(n)[:, lo:hi], q_t[rows, h // 2, t * P:(t + 1) * P],
                                            k_t[rows, h // 2, lo:hi], start=True, stop=True)
                last.then_inc(sig("scores_full"), 1)

            def flip(n):
                h, t = items[n]
                pe.wait_ge(sig("probs"), n + 1)
                if n >= 1:
                    pe.wait_ge(sig("probs_t"), n)
                if t == 4 and h + 1 < H:
                    pe.wait_ge(sig("bias_rows"), 2 * (h + 2))
                for k in range(t + 1):
                    last = nc.tensor.transpose(psum[:, 4 * NC5 + k * P:4 * NC5 + (k + 1) * P],
                                               probs[:, n % 2, k * P:(k + 1) * P], const["ident"][:])
                last.then_inc(sig("flipped"), 1)

            def mix(n):
                h, t = items[n]
                pe.wait_ge(sig("probs_t"), n + 1)
                if n >= 2:
                    pe.wait_ge(sig("fox_out"), n - 1)
                for k in range(t + 1):
                    last = nc.tensor.matmul(bank[6 + n % 2][:, 0:HD], probs_t[:, n % 2, k * P:(k + 1) * P],
                                            v_tok[:, k, h * HD:(h + 1) * HD], start=(k == 0), stop=(k == t))
                last.then_inc(sig("mixed"), 1)

            pe.wait_ge(sig("att_const"), 4)
            bias_half(0, 0)
            bias_half(0, 1)
            score(0)
            for n in range(len(items)):
                if n + 1 < len(items):
                    score(n + 1)
                flip(n)
                h, t = items[n]
                if t in (1, 2) and h + 1 < H:
                    bias_half(h + 1, t - 1)
                if n >= 1:
                    mix(n - 1)
            mix(len(items) - 1)

        @block.scalar
        def _(act):
            def bias_half(h, half):
                act.wait_ge(sig("bias_full"), 2 * h + half + 1)
                if h >= 2:
                    act.wait_ge(sig("scores_read"), TT * (h - 1))
                nc.scalar.activation(gate_bias[:, h % 2, half * NC5:(half + 1) * NC5], bank[5][:], ACT.Copy).then_inc(sig("bias_rows"), 1)

            def evacuate(n):
                t = items[n][1]
                act.wait_ge(sig("flipped"), n + 1)
                if n >= 2:
                    act.wait_ge(sig("mixed"), n - 1)
                cols = (t + 1) * P
                nc.scalar.activation(probs_t[:, n % 2, 0:cols], psum[:, 4 * NC5:4 * NC5 + cols], ACT.Copy).then_inc(sig("probs_t"), 1)

            bias_half(0, 0)
            bias_half(0, 1)
            for n, (h, t) in enumerate(items):
                act.wait_ge(sig("neg_max"), n + 1)
                if n >= 2:
                    act.wait_ge(sig("flipped"), n - 1)
                cols = (t + 1) * P
                nc.scalar.activation(probs[:, n % 2, 0:cols], logits[:, n % 2, 0:cols], ACT.Exp,
                                     bias=neg_max[:, n:n + 1], accum_out=row_sum[:, n:n + 1]).then_inc(sig("probs"), 1)
                if n >= 1:
                    evacuate(n - 1)
                if t in (1, 2) and h + 1 < H:
                    bias_half(h + 1, t - 1)
            evacuate(len(items) - 1)

        @block.vector
        def _(dve):
            def finish(n):
                h, t = items[n]
                dve.wait_ge(sig("probs"), n + 1)
                nc.vector.reciprocal(row_sum[:, n:n + 1], row_sum[:, n:n + 1]).then_inc(sig("row_scale"), 1)
                dve.wait_ge(sig("mixed"), n + 1)
                dve.wait_ge(sig("row_scale"), n + 1)
                nc.vector.tensor_scalar(o_fox[:, t, h * HD:(h + 1) * HD], bank[6 + n % 2][:, 0:HD],
                                        row_sum[:, n:n + 1], None, ALU.mult).then_inc(sig("fox_out"), 1)

            dve.wait_ge(sig("att_const"), 4)
            for n, (h, t) in enumerate(items):
                cols = (t + 1) * P
                lg = logits[:, n % 2, :]
                dve.wait_ge(sig("scores_full"), n + 1)
                dve.wait_ge(sig("bias_rows"), 2 * (h + 1))
                if n >= 2:
                    dve.wait_ge(sig("probs"), n - 1)
                nc.vector.scalar_tensor_tensor(out=lg[:, 0:cols], in0=scores(n)[:, 0:cols], scalar=HD ** -0.5,
                                               in1=gate_bias[:, h % 2, 0:cols], op0=ALU.mult, op1=ALU.add).then_inc(sig("scores_read"), 1)
                dve.wait_ge(sig("scores_read"), n + 1)
                nc.vector.tensor_tensor(lg[:, t * P:cols], lg[:, t * P:cols], causal[:], ALU.add).then_inc(sig("masked"), 1)
                dve.wait_ge(sig("masked"), n + 1)
                nc.vector.tensor_reduce(neg_max[:, n:n + 1], lg[:, 0:cols], AX.X, ALU.max, negate=True).then_inc(sig("neg_max"), 1)
                if n >= 2:
                    finish(n - 2)
            finish(len(items) - 2)
            finish(len(items) - 1)


def recur(nc, sig, bank, const, keep, ins, dram):
    ident = const["ident"]
    o_rwkv = keep["o_rwkv"]
    LEVELS = [2, 4, 8, 16, 32]
    with ExitStack() as ctx:
        sb = lambda name, shape: ctx.enter_context(nc.sbuf_tensor(name, shape, F32))
        cur = sb("rw_cur", [P, 2, SHIFT])
        prev = sb("rw_prev", [P, SHIFT])
        mu_bc = sb("mu_bc", [P, SHIFT])
        names = ["rwkv_w0", "rwkv_a0", "rwkv_k_k", "rwkv_k_a", "rwkv_r_k", "ln_x_g", "ln_x_b"]
        rows = sb("rw_rows", [P, len(names), W])
        w0, a0, k_k, k_a, r_k, ln_g, ln_b = (rows[:, i, :] for i in range(len(names)))
        lora_w = sb("lora_w", [P, W])
        gate_w = sb("gate_w", [P, W])
        in_chunk = sb("in_chunk", [P, 2])
        tri = sb("tri", [P, 4, P])
        low = sb("low", [P, P])
        off_t = sb("off_t", [P, 6, P])
        off_1 = sb("off_1", [P, P])
        lora = sb("lora", [P, 2 * P])
        lora_t = sb("lora_t", [P, 2 * P])
        gate = sb("rw_gate", [P, W])
        sw = sb("sw", [P, W])
        aa = sb("aa", [P, W])
        p_in = sb("p_in", [P, W])
        p_inv = sb("p_inv", [P, W])
        p_ex = sb("p_ex", [P, W])
        p_end = sb("p_end", [CHUNK, H, 2])
        kk = sb("kk", [P, W])
        kp = sb("kp", [P, W])
        tmp = sb("rw_tmp", [P, W])
        norm = sb("rw_norm", [P, H])
        bonus = sb("bonus", [P, H])
        tm = sb("tm", [P, 4, W])
        fm = sb("fm", [HD, H, 4, P])
        gram = sb("gram", [P, H, 4 * P])
        a_low = sb("a_low", [P, H, P])
        inv = sb("inv", [P, H, P])
        inv_t = sb("inv_t", [P, H, P])
        a_off = sb("a_off", [P, 2, H, P])
        grow = sb("grow", [P, H, P])
        xv = sb("xv", [P, W])
        u = sb("u", [P, W])
        w_t = sb("w_t", [HD, H, P])
        sa = sb("sa", [P, W])
        state = sb("state", [HD, 2, W])
        y = sb("rw_y", [P, W])
        block = ctx.enter_context(nc.Block("recur"))

        def heads(ap, n=HD):
            return ap.rearrange("p (h d) -> p h d", d=n)

        @block.sync
        def _(sp):
            for i, n in enumerate(names):
                src = ins[n] if n != "rwkv_r_k" else ins[n].rearrange("l h d -> l (h d)")
                sp.dma_start(rows[:, i, :], src.partition_broadcast(P).rearrange("p a n -> p (a n)")).then_inc(sig("rows_in"), 16)
            sp.dma_start(lora_w[0:LORA, :], ins["rwkv_w2"][0]).then_inc(sig("rows_in"), 16)
            sp.dma_start(lora_w[LORA:2 * LORA, :], ins["rwkv_a2"][0]).then_inc(sig("rows_in"), 16)
            sp.dma_start(gate_w[:], ins["rwkv_g2"][0]).then_inc(sig("rows_in"), 16)
            for t in range(TT):
                if t >= 2:
                    sp.wait_ge(sig("tile_done"), t - 1)
                sp.dma_start(cur[:, t % 2, :], dram["p_rwkv"][1 + t * P:1 + (t + 1) * P, :]).then_inc(sig("cur_in"), 16)
                if t >= 1:
                    sp.wait_ge(sig("shifted"), t)
                sp.dma_start(prev[:], dram["p_rwkv"][t * P:(t + 1) * P, :]).then_inc(sig("prev_in"), 16)

        @block.gpsimd
        def _(pool):
            link = Link(pool, sig("pool_link_r"))

            def select(ap, pattern, cm, base, op, fill=0.0):
                link(nc.gpsimd.affine_select(out=ap, in_=ap, compare_op=op, fill=fill, base=base,
                                             pattern=pattern, channel_multiplier=cm))

            pool.dma_start(mu_bc[:], ins["shift_mu"].partition_broadcast(P).rearrange("p a n -> p (a n)")).then_inc(sig("mu_in"), 16)
            for m in (tri, low, off_t, off_1, in_chunk):
                link(nc.gpsimd.memset(m[:], 1.0))
            link(nc.gpsimd.memset(state[:], 0.0))
            for m in [in_chunk[:]]:
                select(m, [[-CHUNK, 2]], 1, 0, ALU.is_ge)
                select(m, [[CHUNK, 2]], -1, CHUNK - 1, ALU.is_ge)
            for i in range(4):
                m = tri[:, i, :].rearrange("p (c t) -> p c t", c=2)
                select(m, [[-CHUNK, 2], [0, CHUNK]], 1, 0, ALU.is_ge)
                select(m, [[CHUNK, 2], [0, CHUNK]], -1, CHUNK - 1, ALU.is_ge)
                select(m, [[CHUNK, 2], [1, CHUNK]], -1, 0, ALU.is_ge if i % 2 else ALU.is_gt)
            m = low[:].rearrange("p (c t) -> p c t", c=2)
            select(m, [[-CHUNK, 2], [0, CHUNK]], 1, 0, ALU.is_ge)
            select(m, [[CHUNK, 2], [0, CHUNK]], -1, CHUNK - 1, ALU.is_ge)
            select(m, [[-CHUNK, 2], [-1, CHUNK]], 1, 0, ALU.is_gt)
            for i in range(6):
                n = 1 << i
                m = off_t[:, i, :].rearrange("p (b u v) -> p b u v", u=2, v=n)
                select(m, [[0, P // (2 * n)], [1, 2], [0, n]], 0, -1, ALU.is_ge)
                select(m, [[-2 * n, P // (2 * n)], [0, 2], [0, n]], 1, 0, ALU.is_ge)
                select(m, [[2 * n, P // (2 * n)], [0, 2], [0, n]], -1, n - 1, ALU.is_ge)
            m = off_1[:].rearrange("p (b u) -> p b u", u=2)
            select(m, [[0, P // 2], [-1, 2]], 0, 0, ALU.is_ge)
            select(m, [[-2, P // 2], [0, 2]], 1, -1, ALU.is_equal)
            nc.gpsimd.nop().then_inc(sig("masks"), 1)

            def shift(t):
                if t == 0:
                    pool.wait_ge(sig("mu_in"), 16)
                pool.wait_ge(sig("cur_in"), 16 * (t + 1))
                pool.wait_ge(sig("prev_in"), 16 * (t + 1))
                c = cur[:, t % 2, :]
                link(nc.gpsimd.tensor_tensor(prev[:], prev[:], c, ALU.subtract))
                link(nc.gpsimd.tensor_tensor(prev[:], prev[:], mu_bc[:], ALU.mult))
                nc.gpsimd.tensor_tensor(c, c, prev[:], ALU.add).then_inc(sig("shifted"), 1)

            shift(0)
            for t in range(TT):
                pool.wait_ge(sig("kk_ss"), t + 1)
                nc.gpsimd.tensor_tensor(norm[:], norm[:], const["neghalf"][:], ALU.pow).then_inc(sig("kk_rn"), 1)
                if t + 1 < TT:
                    shift(t + 1)
                pool.wait_ge(sig("gram"), H * (t + 1))
                for i, n in enumerate(LEVELS):
                    if i >= 2:
                        pool.wait_ge(sig("grow_full"), 2 * (len(LEVELS) * t + i - 1))
                    elif t >= 1:
                        pool.wait_ge(sig("grow_full"), 2 * len(LEVELS) * t)
                    nc.gpsimd.tensor_tensor(a_off[:, i % 2], gram[:, :, 0:P],
                                            off_t[:, i + 1, :].unsqueeze(1).to_broadcast([P, H, P]), ALU.mult).then_inc(sig("a_off"), 1)
                pool.wait_ge(sig("y_var"), t + 1)
                nc.gpsimd.tensor_tensor(norm[:], norm[:], const["neghalf"][:], ALU.pow).then_inc(sig("y_rstd"), 1)

        @block.scalar
        def _(act):
            for t in range(TT):
                c = cur[:, t % 2, :]
                act.wait_ge(sig("shifted"), t + 1)
                nc.scalar.activation(lora[:, 0:LORA], c[:, 3 * W:3 * W + LORA], ACT.Tanh).then_inc(sig("lora"), 1)
                nc.scalar.activation(lora[:, LORA:2 * LORA], c[:, 3 * W + LORA:3 * W + 2 * LORA], ACT.Copy).then_inc(sig("lora"), 1)
                nc.scalar.activation(lora[:, P:2 * P], c[:, 3 * W + 2 * LORA:SHIFT], ACT.Tanh, scale=0.5).then_inc(sig("lora"), 1)
                act.wait_ge(sig("lora_flipped"), t + 1)
                nc.scalar.activation(lora_t[:], bank[0][:, 0:2 * P], ACT.Copy).then_inc(sig("lora_t"), 1)
                act.wait_ge(sig("z_biased"), t + 1)
                nc.scalar.activation(sw[:], sw[:], ACT.Tanh, scale=0.5).then_inc(sig("z_tanh"), 1)
                act.wait_ge(sig("a_biased"), t + 1)
                nc.scalar.activation(aa[:], aa[:], ACT.Tanh, scale=0.5).then_inc(sig("a_tanh"), 1)
                act.wait_ge(sig("g_full"), t + 1)
                nc.scalar.activation(gate[:], bank[3], ACT.Copy).then_inc(sig("gate"), 1)
                act.wait_ge(sig("decay_sums"), t + 1)
                nc.scalar.activation(p_in[:], bank[1], ACT.Exp, scale=-EXPM05).then_inc(sig("p_in"), 1)
                nc.scalar.activation(p_inv[:], bank[1], ACT.Exp, scale=EXPM05).then_inc(sig("p_inv"), 1)
                nc.scalar.activation(p_ex[:], bank[2], ACT.Exp, scale=-EXPM05).then_inc(sig("p_ex"), 1)
                nc.scalar.activation(p_end[:].rearrange("p h c -> p (h c)"), bank[3][0:CHUNK, 0:2 * H], ACT.Exp,
                                     scale=-EXPM05).then_inc(sig("p_end"), 1)
                for h in range(H):
                    act.wait_ge(sig("fm_full"), H * t + h + 1)
                    nc.scalar.activation(fm[:, h].rearrange("p a t -> p (a t)"), bank[4 + h % 4][0:HD, :], ACT.Copy).then_inc(sig("fm"), 1)
                for i in range(len(LEVELS)):
                    for g in range(2):
                        n = 2 * (len(LEVELS) * t + i) + g
                        act.wait_ge(sig("inv_full"), n + 1)
                        hs = slice(4 * g, 4 * g + 4)
                        if i < len(LEVELS) - 1:
                            nc.scalar.activation(inv[:, hs].rearrange("p h s -> p (h s)"), bank[g], ACT.Copy).then_inc(sig("inv"), 1)
                        nc.scalar.activation(inv_t[:, hs].rearrange("p h s -> p (h s)"), bank[2 + g], ACT.Copy).then_inc(sig("inv_t"), 1)
                act.wait_ge(sig("xv_full"), t + 1)
                nc.scalar.activation(xv[:], bank[6], ACT.Copy).then_inc(sig("xv"), 1)
                act.wait_ge(sig("w_full"), t + 1)
                for g in range(2):
                    nc.scalar.activation(w_t[:, 4 * g:4 * g + 4].rearrange("p h s -> p (h s)"), bank[g][0:HD, :], ACT.Copy).then_inc(sig("w_t"), 1)
                act.wait_ge(sig("u_full"), t + 1)
                nc.scalar.activation(u[:], bank[7], ACT.Copy).then_inc(sig("u"), 1)
                act.wait_ge(sig("y_state_full"), 2 * (t + 1))
                nc.scalar.activation(y[:], bank[5], ACT.Copy).then_inc(sig("y_state"), 1)

        @block.tensor
        def _(pe):
            pe.wait_ge(sig("masks"), 1)
            pe.wait_ge(sig("rows_in"), 16 * 10)
            for t in range(TT):
                c = cur[:, t % 2, :]
                v = c[:, 2 * W:3 * W]
                pe.wait_ge(sig("lora"), 3 * (t + 1))
                pe.wait_ge(sig("lora_sig"), t + 1)
                if t >= 1:
                    pe.wait_ge(sig("y_sum"), t)
                for i in range(2):
                    last = nc.tensor.transpose(bank[0][:, i * P:(i + 1) * P], lora[:, i * P:(i + 1) * P], ident[:])
                last.then_inc(sig("lora_flipped"), 1)
                pe.wait_ge(sig("lora_t"), t + 1)
                nc.tensor.matmul(bank[1], lora_t[0:LORA, 0:P], lora_w[0:LORA, :], start=True, stop=True).then_inc(sig("z_full"), 1)
                nc.tensor.matmul(bank[2], lora_t[LORA:P, 0:P], lora_w[LORA:P, :], start=True, stop=True).then_inc(sig("a_full"), 1)
                nc.tensor.matmul(bank[3], lora_t[:, P:2 * P], gate_w[:], start=True, stop=True).then_inc(sig("g_full"), 1)
                pe.wait_ge(sig("sw"), t + 1)
                pe.wait_ge(sig("a_biased"), t + 1)
                pe.wait_ge(sig("gate"), t + 1)
                nc.tensor.matmul(bank[1], tri[:, 1, :], sw[:], start=True, stop=True)
                nc.tensor.matmul(bank[2], tri[:, 0, :], sw[:], start=True, stop=True)
                for h in range(H):
                    last = nc.tensor.matmul(bank[3][0:HD, 2 * h:2 * h + 2], sw[:, h * HD:(h + 1) * HD], in_chunk[:],
                                            start=True, stop=True)
                last.then_inc(sig("decay_sums"), 1)
                pe.wait_ge(sig("tm"), 4 * (t + 1))
                for h in range(H):
                    if h >= 4:
                        pe.wait_ge(sig("fm"), H * t + h - 3)
                    for i in range(4):
                        last = nc.tensor.transpose(bank[4 + h % 4][0:HD, i * P:(i + 1) * P], tm[:, i, h * HD:(h + 1) * HD], ident[:])
                    last.then_inc(sig("fm_full"), 1)
                pe.wait_ge(sig("p_end"), t + 1)
                for h in range(H):
                    pe.wait_ge(sig("fm"), H * t + h + 1)
                    if h >= 2:
                        pe.wait_ge(sig("gram"), H * t + h - 1)
                    ar = fm[:, h, 0:2, :].rearrange("p a t -> p (a t)")
                    nc.tensor.matmul(bank[h % 2][:, 0:2 * P], fm[:, h, 2, :], ar, start=True, stop=True)
                    nc.tensor.matmul(bank[h % 2][:, 2 * P:4 * P], fm[:, h, 3, :], ar, start=True, stop=True)
                    nc.tensor.matmul(bank[2 + h // 4][:, (h % 4) * P:(h % 4 + 1) * P], fm[:, h, 0, :], fm[:, h, 2, :],
                                     start=True, stop=True).then_inc(sig("gram_full"), 1)
                pe.wait_ge(sig("fm"), H * (t + 1))
                for i in range(len(LEVELS)):
                    for g in range(2):
                        n = 2 * (len(LEVELS) * t + i) + g
                        if i == 0:
                            pe.wait_ge(sig("inv_first"), 2 * (t + 1))
                        else:
                            pe.wait_ge(sig("inv"), 2 * ((len(LEVELS) - 1) * t + i - 1) + g + 1)
                            pe.wait_ge(sig("inv_t"), n - 1)
                            pe.wait_ge(sig("grow"), n - 1)
                        pe.wait_ge(sig("a_off"), len(LEVELS) * t + i + 1)
                        for h in range(4):
                            last = nc.tensor.matmul(bank[4 + g][:, h * P:(h + 1) * P], a_off[:, i % 2, 4 * g + h, :],
                                                    inv[:, 4 * g + h, :], start=True, stop=True)
                        last.then_inc(sig("grow_full"), 1)
                    for g in range(2):
                        n = 2 * (len(LEVELS) * t + i) + g
                        pe.wait_ge(sig("grow"), n + 1)
                        for h in range(4):
                            cols = slice(h * P, (h + 1) * P)
                            if i < len(LEVELS) - 1:
                                nc.tensor.matmul(bank[g][:, cols], inv_t[:, 4 * g + h, :], grow[:, 4 * g + h, :], start=True, stop=True)
                            last = nc.tensor.matmul(bank[2 + g][:, cols], grow[:, 4 * g + h, :], inv_t[:, 4 * g + h, :], start=True, stop=True)
                        last.then_inc(sig("inv_full"), 1)
                for h in range(H):
                    hc = slice(h * HD, (h + 1) * HD)
                    last = nc.tensor.matmul(bank[6][:, hc], gram[:, h, 2 * P:3 * P], v[:, hc], start=True, stop=True)
                last.then_inc(sig("xv_full"), 1)
                pe.wait_ge(sig("inv_t"), 2 * len(LEVELS) * (t + 1))
                for h in range(H):
                    last = nc.tensor.matmul(bank[h // 4][0:HD, (h % 4) * P:(h % 4 + 1) * P], tm[:, 0, h * HD:(h + 1) * HD],
                                            inv_t[:, h, :], start=True, stop=True)
                last.then_inc(sig("w_full"), 1)
                pe.wait_ge(sig("xv"), t + 1)
                for h in range(H):
                    hc = slice(h * HD, (h + 1) * HD)
                    last = nc.tensor.matmul(bank[7][:, hc], inv_t[:, h, :], xv[:, hc], start=True, stop=True)
                last.then_inc(sig("u_full"), 1)
                pe.wait_ge(sig("w_t"), 2 * (t + 1))
                for ch in range(2):
                    n = 2 * t + ch
                    tok = slice(ch * CHUNK, (ch + 1) * CHUNK)
                    if n >= 1:
                        pe.wait_ge(sig("state"), n)
                    for h in range(H):
                        hc = slice(h * HD, (h + 1) * HD)
                        last = nc.tensor.matmul(bank[4][tok, hc], w_t[:, h, tok], state[:, ch, hc], start=True, stop=True)
                    last.then_inc(sig("sa_full"), 1)
                    for h in range(H):
                        hc = slice(h * HD, (h + 1) * HD)
                        last = nc.tensor.matmul(bank[5][tok, hc], fm[:, h, 1, tok], state[:, ch, hc], start=True, stop=True)
                    last.then_inc(sig("y_state_full"), 1)
                    pe.wait_ge(sig("sa"), n + 1)
                    if ch == 0:
                        pe.wait_ge(sig("u"), t + 1)
                    for h in range(H):
                        hc = slice(h * HD, (h + 1) * HD)
                        nc.tensor.matmul(bank[6 + ch][0:HD, hc], tm[tok, 2, hc], sa[tok, hc], start=True, stop=False)
                        last = nc.tensor.matmul(bank[6 + ch][0:HD, hc], tm[tok, 3, hc], v[tok, hc], start=False, stop=True)
                    last.then_inc(sig("state_full"), 1)
                for h in range(H):
                    hc = slice(h * HD, (h + 1) * HD)
                    nc.tensor.matmul(bank[0][:, hc], gram[:, h, P:2 * P], sa[:, hc], start=True, stop=False)
                    last = nc.tensor.matmul(bank[0][:, hc], gram[:, h, 3 * P:4 * P], v[:, hc], start=False, stop=True)
                last.then_inc(sig("y_full"), 1)

        @block.vector
        def _(dve):
            link = Link(dve, sig("dve_link_r"))

            def mark(ins, name, count):
                ins.then_inc(sig(name), 1)
                dve.wait_ge(sig(name), count)

            ident_h = ident[:].unsqueeze(1).to_broadcast([P, 4, P])
            dve.wait_ge(sig("masks"), 1)
            dve.wait_ge(sig("rows_in"), 16 * 10)
            for t in range(TT):
                c = cur[:, t % 2, :]
                r, k, v = (c[:, i * W:(i + 1) * W] for i in range(3))
                tt, stt, ts = nc.vector.tensor_tensor, nc.vector.scalar_tensor_tensor, nc.vector.tensor_scalar
                dve.wait_ge(sig("lora"), 3 * (t + 1))
                ts(lora[:, P:2 * P], lora[:, P:2 * P], 0.5, 0.5, ALU.mult, ALU.add).then_inc(sig("lora_sig"), 1)
                link(tt(kk[:], k, k_k, ALU.mult))
                link(tt(tmp[:], kk[:], kk[:], ALU.mult))
                link(nc.vector.tensor_reduce(norm[:], heads(tmp[:]), AX.X, ALU.add))
                ts(norm[:], norm[:], 1e-24, None, ALU.max).then_inc(sig("kk_ss"), 1)
                dve.wait_ge(sig("z_full"), t + 1)
                tt(sw[:], bank[1], w0, ALU.add).then_inc(sig("z_biased"), 1)
                dve.wait_ge(sig("a_full"), t + 1)
                tt(aa[:], bank[2], a0, ALU.add).then_inc(sig("a_biased"), 1)
                dve.wait_ge(sig("kk_rn"), t + 1)
                link(tt(heads(kk[:]), heads(kk[:]), norm[:].unsqueeze(2).to_broadcast([P, H, HD]), ALU.mult))
                dve.wait_ge(sig("z_tanh"), t + 1)
                mark(ts(sw[:], sw[:], 0.5, 0.5, ALU.mult, ALU.add), "sw", t + 1)
                dve.wait_ge(sig("a_tanh"), t + 1)
                link(ts(aa[:], aa[:], 0.5, 0.5, ALU.mult, ALU.add))
                link(stt(out=kp[:], in0=aa[:], scalar=1.0, in1=k_a, op0=ALU.subtract, op1=ALU.mult))
                link(stt(out=kp[:], in0=kp[:], scalar=1.0, in1=k, op0=ALU.add, op1=ALU.mult))
                link(tt(aa[:], aa[:], kk[:], ALU.mult))
                link(tt(tmp[:], r, kp[:], ALU.mult))
                link(tt(tmp[:], tmp[:], r_k, ALU.mult))
                link(nc.vector.tensor_reduce(bonus[:], heads(tmp[:]), AX.X, ALU.add))
                dve.wait_ge(sig("p_ex"), t + 1)
                stt(out=tm[:, 0, :], in0=kk[:], scalar=-1.0, in1=p_ex[:], op0=ALU.mult, op1=ALU.mult).then_inc(sig("tm"), 1)
                tt(tm[:, 1, :], r, p_in[:], ALU.mult).then_inc(sig("tm"), 1)
                tt(tm[:, 2, :], aa[:], p_inv[:], ALU.mult).then_inc(sig("tm"), 1)
                tt(tm[:, 3, :], kp[:], p_inv[:], ALU.mult).then_inc(sig("tm"), 1)
                tri_row = tri[:].rearrange("p a t -> p (a t)")
                for h in range(H):
                    dve.wait_ge(sig("gram_full"), H * t + h + 1)
                    tt(gram[:, h, :], bank[h % 2], tri_row, ALU.mult).then_inc(sig("gram"), 1)
                low_h = low[:].unsqueeze(1).to_broadcast([P, 4, P])
                dve.wait_ge(sig("gram"), H * (t + 1))
                for g in range(2):
                    hs = slice(4 * g, 4 * g + 4)
                    link(tt(a_low[:, hs], heads(bank[2 + g], P), low_h, ALU.mult))
                    link(tt(inv[:, hs], a_low[:, hs], off_1[:].unsqueeze(1).to_broadcast([P, 4, P]), ALU.mult))
                    link(tt(inv[:, hs], inv[:, hs], ident_h, ALU.add))
                    link(tt(inv_t[:, hs], gram[:, hs, 0:P], off_t[:, 0, :].unsqueeze(1).to_broadcast([P, 4, P]), ALU.mult))
                    tt(inv_t[:, hs], inv_t[:, hs], ident_h, ALU.add).then_inc(sig("inv_first"), 1)
                for i in range(len(LEVELS)):
                    for g in range(2):
                        n = 2 * (len(LEVELS) * t + i) + g
                        dve.wait_ge(sig("grow_full"), n + 1)
                        tt(grow[:, 4 * g:4 * g + 4], heads(bank[4 + g], P), ident_h, ALU.add).then_inc(sig("grow"), 1)
                dve.wait_ge(sig("u"), t + 1)
                for ch in range(2):
                    n = 2 * t + ch
                    tok = slice(ch * CHUNK, (ch + 1) * CHUNK)
                    dve.wait_ge(sig("sa_full"), n + 1)
                    tt(sa[tok, :], bank[4][tok, :], u[tok, :], ALU.add).then_inc(sig("sa"), 1)
                    dve.wait_ge(sig("state_full"), n + 1)
                    nxt = state[:, 1 - ch, :]
                    link(tt(nxt, bank[6 + ch][0:HD, :], state[:, ch, :], ALU.add))
                    mark(tt(heads(nxt), heads(nxt), p_end[:, :, ch:ch + 1].to_broadcast([CHUNK, H, HD]), ALU.mult), "state", n + 1)
                dve.wait_ge(sig("y_state"), t + 1)
                dve.wait_ge(sig("y_full"), t + 1)
                mark(tt(y[:], bank[0], y[:], ALU.add), "y_sum", t + 1)
                link(nc.vector.tensor_reduce(norm[:], heads(y[:]), AX.X, ALU.add))
                link(ts(norm[:], norm[:], 1.0 / HD, None, ALU.mult))
                link(tt(heads(y[:]), heads(y[:]), norm[:].unsqueeze(2).to_broadcast([P, H, HD]), ALU.subtract))
                link(tt(tmp[:], y[:], y[:], ALU.mult))
                link(nc.vector.tensor_reduce(norm[:], heads(tmp[:]), AX.X, ALU.add))
                ts(norm[:], norm[:], 1.0 / HD, LN_EPS, ALU.mult, ALU.add).then_inc(sig("y_var"), 1)
                link(tt(heads(tmp[:]), heads(v), bonus[:].unsqueeze(2).to_broadcast([P, H, HD]), ALU.mult))
                dve.wait_ge(sig("y_rstd"), t + 1)
                link(tt(heads(y[:]), heads(y[:]), norm[:].unsqueeze(2).to_broadcast([P, H, HD]), ALU.mult))
                link(tt(y[:], y[:], ln_g, ALU.mult))
                link(tt(y[:], y[:], ln_b, ALU.add))
                link(tt(y[:], y[:], tmp[:], ALU.add))
                mark(tt(o_rwkv[:, t, :], y[:], gate[:], ALU.mult), "tile_done", t + 1)


def merge(nc, sig, bank, const, keep, ins, dram):
    ident, psum = const["ident"], const["psum"]
    mod_bc, o_fox, o_rwkv, logits = (keep[n] for n in ("mod_bc", "o_fox", "o_rwkv", "logits"))
    GE = G + E
    with ExitStack() as ctx:
        sb = lambda name, shape: ctx.enter_context(nc.sbuf_tensor(name, shape, F32))
        w_fox = sb("w_fox", [P, W // P, D])
        w_rwkv = sb("w_rwkv", [P, W // P, D])
        w_o = sb("w_o", [P, KT, D])
        w_route = sb("w_route", [P, KT, GE])
        b_route = sb("b_route", [P, GE])
        gates = sb("mg_gates", [P, 2, 2 * D])
        x_in = sb("mg_x", [P, 2, D])
        o_t = sb("mg_o_t", [P, 2 * W // P, P])
        mixed = sb("mg_mixed", [P, 2, D])
        mixed_t = sb("mg_mixed_t", [P, KT, P])
        part = sb("mg_part", [P, D])
        x_mid = sb("mg_x_mid", [P, 2, D])
        h_mid = sb("mg_h_mid", [P, 2, D])
        h_t = sb("mg_h_t", [P, KT, P])
        ms = sb("mg_ms", [P, TT])
        block = ctx.enter_context(nc.Block("merge"))

        @block.sync
        def _(sp):
            sp.dma_start(w_fox[:], ins["w_out_fox"][0].rearrange("(k p) n -> p k n", p=P)).then_inc(sig("mg_w_in"), 16)
            sp.dma_start(w_rwkv[:], ins["w_out_rwkv"][0].rearrange("(k p) n -> p k n", p=P)).then_inc(sig("mg_w_in"), 16)
            for t in range(TT):
                if t >= 2:
                    sp.wait_ge(sig("x_mid"), t - 1)
                sp.dma_start(gates[:, t % 2, :], dram["gates"][t * P:(t + 1) * P, :]).then_inc(sig(f"gates_in{t % 2}"), 16)
                sp.dma_start(x_in[:, t % 2, :], ins["x"][0, t * P:(t + 1) * P, :]).then_inc(sig(f"mg_x_in{t % 2}"), 16)
                if t == 0:
                    sp.dma_start(w_o[:], ins["w_o"][0].rearrange("(k p) n -> p k n", p=P)).then_inc(sig("w_o_in"), 16)
                    sp.dma_start(w_route[:, :, 0:G], ins["router_group_w"][0].rearrange("(k p) n -> p k n", p=P)).then_inc(sig("w_route_in"), 16)
                    sp.dma_start(w_route[:, :, G:GE], ins["router_expert_w"][0].rearrange("(k p) n -> p k n", p=P)).then_inc(sig("w_route_in"), 16)
                    sp.dma_start(b_route[:, 0:G], ins["router_group_b"].partition_broadcast(P).rearrange("p a n -> p (a n)")).then_inc(sig("w_route_in"), 16)
                    sp.dma_start(b_route[:, G:GE], ins["router_expert_b"].partition_broadcast(P).rearrange("p a n -> p (a n)")).then_inc(sig("w_route_in"), 16)

        @block.gpsimd
        def _(pool):
            for t in range(TT):
                pool.wait_ge(sig("mg_ms"), t + 1)
                nc.gpsimd.tensor_tensor(ms[:, t:t + 1], ms[:, t:t + 1], const["neghalf"][:, 0:1], ALU.pow).then_inc(sig("mg_rstd"), 1)
                pool.dma_start(dram["x_mid"][t * P:(t + 1) * P, :], x_mid[:, t % 2, :]).then_inc(sig(f"x_mid_out{t % 2}"), 16)
                pool.wait_ge(sig("h_mid"), t + 1)
                pool.dma_start(dram["h_mid"][t * P:(t + 1) * P, :], h_mid[:, t % 2, :]).then_inc(sig(f"h_mid_out{t % 2}"), 16)
            for b in range(2):
                pool.wait_ge(sig(f"x_mid_out{b}"), 16 * TT // 2)
                pool.wait_ge(sig(f"h_mid_out{b}"), 16 * TT // 2)

        @block.tensor
        def _(pe):
            def flip(src, name, need, count):
                pe.wait_ge(sig(need), count)
                for k in range(KT):
                    last = nc.tensor.transpose(psum[:, k * P:(k + 1) * P], src(k), ident[:])
                last.then_inc(sig(name), 1)

            def branches(t):
                if t >= 3:
                    pe.wait_ge(sig("logits"), t - 2)
                elif t >= 2:
                    pe.wait_ge(sig("mixed_t"), t - 1)
                elif t >= 1:
                    pe.wait_ge(sig("o_t"), t)
                for k in range(2 * W // P):
                    src = o_fox if k < W // P else o_rwkv
                    k4 = k % (W // P)
                    last = nc.tensor.transpose(psum[:, k * P:(k + 1) * P], src[:, t, k4 * P:(k4 + 1) * P], ident[:])
                last.then_inc(sig("o_flipped"), 1)
                pe.wait_ge(sig("o_t"), t + 1)
                if t == 0:
                    pe.wait_ge(sig("mg_w_in"), 32)
                for half in range(2):
                    cols = slice(half * NC5, (half + 1) * NC5)
                    if t >= 1:
                        pe.wait_ge(sig("branches_read"), 2 * (t - 1) + half + 1)
                    for j, w in enumerate((w_fox, w_rwkv)):
                        for k in range(W // P):
                            last = nc.tensor.matmul(bank[2 + 2 * half + j], o_t[:, j * (W // P) + k, :], w[:, k, cols],
                                                    start=(k == 0), stop=(k == W // P - 1))
                    last.then_inc(sig("branches_full"), 1)

            def outward(t):
                flip(lambda k: mixed[:, t % 2, k * P:(k + 1) * P], "mixed_flipped", "mg_mixed", 2 * (t + 1))
                pe.wait_ge(sig("mixed_t"), t + 1)
                if t == 0:
                    pe.wait_ge(sig("w_o_in"), 16)
                if t >= 1:
                    pe.wait_ge(sig("w_o_read"), t)
                for half in range(2):
                    for k in range(KT):
                        last = nc.tensor.matmul(bank[6 + half], mixed_t[:, k, :], w_o[:, k, half * NC5:(half + 1) * NC5],
                                                start=(k == 0), stop=(k == KT - 1))
                last.then_inc(sig("w_o_full"), 1)

            def router(t):
                flip(lambda k: h_mid[:, t % 2, k * P:(k + 1) * P], "h_flipped", "h_mid", t + 1)
                pe.wait_ge(sig("mg_h_t"), t + 1)
                if t == 0:
                    pe.wait_ge(sig("w_route_in"), 64)
                for k in range(KT):
                    last = nc.tensor.matmul(bank[0][:, 0:GE], h_t[:, k, :], w_route[:, k, :], start=(k == 0), stop=(k == KT - 1))
                last.then_inc(sig("logits_full"), 1)

            for s in range(TT + 2):
                if s < TT:
                    branches(s)
                if 1 <= s <= TT:
                    outward(s - 1)
                if s >= 2:
                    if s == TT + 1:
                        pass
                    router(s - 2)

        @block.scalar
        def _(act):
            for s in range(TT + 2):
                if s < TT:
                    act.wait_ge(sig("o_flipped"), s + 1)
                    nc.scalar.activation(o_t[:].rearrange("p k t -> p (k t)"), psum[:, 0:D], ACT.Copy).then_inc(sig("o_t"), 1)
                if 1 <= s <= TT:
                    act.wait_ge(sig("mixed_flipped"), s)
                    nc.scalar.activation(mixed_t[:].rearrange("p k t -> p (k t)"), psum[:, 0:D], ACT.Copy).then_inc(sig("mixed_t"), 1)
                if s >= 2:
                    t = s - 2
                    act.wait_ge(sig("h_flipped"), t + 1)
                    nc.scalar.activation(h_t[:].rearrange("p k t -> p (k t)"), psum[:, 0:D], ACT.Copy).then_inc(sig("mg_h_t"), 1)
                if 1 <= s <= TT:
                    t = s - 1
                    act.wait_ge(sig("x_mid"), t + 1)
                    if t >= 1:
                        act.wait_ge(sig("h_scaled"), t)
                    nc.scalar.activation(part[:], x_mid[:, t % 2, :], ACT.Square, accum_out=ms[:, t:t + 1]).then_inc(sig("mg_ss"), 1)

        @block.vector
        def _(dve):
            link = Link(dve, sig("dve_link_m"))
            tt, stt, ts = nc.vector.tensor_tensor, nc.vector.scalar_tensor_tensor, nc.vector.tensor_scalar

            def gate(t):
                dve.wait_ge(sig(f"gates_in{t % 2}"), 16 * (t // 2 + 1))
                for half in range(2):
                    cols = slice(half * NC5, (half + 1) * NC5)
                    m = mixed[:, t % 2, cols]
                    g = gates[:, t % 2, :]
                    dve.wait_ge(sig("branches_full"), 2 * t + half + 1)
                    if t >= 2:
                        dve.wait_ge(sig("mixed_flipped"), t - 1)
                    tt(m, bank[2 + 2 * half], g[:, cols], ALU.mult).then_inc(sig("fox_gated"), 1)
                    g2 = g[:, D + half * NC5:D + (half + 1) * NC5]
                    tt(g2, bank[3 + 2 * half], g2, ALU.mult).then_inc(sig("branches_read"), 1)
                    dve.wait_ge(sig("branches_read"), 2 * t + half + 1)
                    dve.wait_ge(sig("fox_gated"), 2 * t + half + 1)
                    tt(m, m, g2, ALU.add).then_inc(sig("mg_mixed"), 1)

            def residual(t):
                xm, hm = x_mid[:, t % 2, :], h_mid[:, t % 2, :]
                dve.wait_ge(sig("w_o_full"), t + 1)
                dve.wait_ge(sig(f"mg_x_in{t % 2}"), 16 * (t // 2 + 1))
                if t >= 2:
                    dve.wait_ge(sig(f"x_mid_out{t % 2}"), 16 * (t // 2))
                    dve.wait_ge(sig(f"h_mid_out{t % 2}"), 16 * (t // 2))
                    dve.wait_ge(sig("h_flipped"), t - 1)
                tt(xm, psum[:, 6 * NC5:8 * NC5], mod_bc[:, 0, :], ALU.mult).then_inc(sig("w_o_read"), 1)
                dve.wait_ge(sig("w_o_read"), t + 1)
                tt(xm, xm, x_in[:, t % 2, :], ALU.add).then_inc(sig("x_mid"), 1)
                dve.wait_ge(sig("mg_ss"), t + 1)
                ts(ms[:, t:t + 1], ms[:, t:t + 1], 1.0 / D, EPS, ALU.mult, ALU.add).then_inc(sig("mg_ms"), 1)
                dve.wait_ge(sig("mg_rstd"), t + 1)
                stt(out=hm, in0=xm, scalar=ms[:, t:t + 1], in1=mod_bc[:, 2, :], op0=ALU.mult, op1=ALU.mult).then_inc(sig("h_scaled"), 1)
                dve.wait_ge(sig("h_scaled"), t + 1)
                tt(hm, hm, mod_bc[:, 1, :], ALU.add).then_inc(sig("h_mid"), 1)

            for s in range(TT + 2):
                if s >= 2:
                    t = s - 2
                    dve.wait_ge(sig("logits_full"), t + 1)
                    tt(logits[:, t, :], bank[0][:, 0:GE], b_route[:], ALU.add).then_inc(sig("logits"), 1)
                if s < TT:
                    gate(s)
                if 1 <= s <= TT:
                    residual(s - 1)


def route(nc, sig, bank, const, keep, ins, dram):
    logits, dest, pair_w = keep["logits"], keep["dest"], keep["pair_w"]
    psum = const["psum"]
    BIG = 1024.0
    with ExitStack() as ctx:
        sb = lambda name, shape, dt=F32: ctx.enter_context(nc.sbuf_tensor(name, shape, dt))
        ones = sb("rt_ones", [P, P])
        before = sb("rt_before", [P, P])
        iota_e = sb("iota_e", [P, E])
        iota_g = sb("iota_g", [P, G])
        iota_b = sb("iota_b", [P, OVERFLOW_BLOCKS])
        first_row = sb("first_row", [P, E])
        token = sb("rt_token", [P, TT], I32)
        gmax = sb("rt_gmax", [P, TT])
        gexp = sb("rt_gexp", [P, TT, G])
        gsum = sb("rt_gsum", [P, TT])
        ghot = sb("rt_ghot", [P, TT, G])
        el = sb("rt_el", [P, TT, E])
        best = sb("rt_best", [P, 2, TT])
        hot = sb("rt_hot", [P, 2, TT, E])
        both = sb("rt_both", [P, TT, E])
        tmp = sb("rt_tmp", [P, TT, E])
        idx = sb("rt_idx", [P, TT])
        extra = sb("rt_extra", [P, E])
        extra_end = sb("rt_extra_end", [P, E])
        over_row = sb("rt_over_row", [P, E])
        diff = sb("rt_diff", [P, E])
        ones_e = sb("rt_ones_e", [P, E])
        row = sb("rt_row", [P, TT, E])
        destf = sb("rt_destf", [P, TT])
        table = sb("rt_table", [1, BLOCKS, E])
        tablef = sb("rt_tablef", [1, 1 + BLOCKS])
        zero_i = sb("rt_zero_i", [P, BLOCKS], I32)
        back_i = sb("rt_back_i", [BLOCKS, P], I32)
        back_f = sb("rt_back_f", [BLOCKS, P])
        block = ctx.enter_context(nc.Block("route"))

        def bt(ap, n):
            return ap.unsqueeze(2).to_broadcast([P, TT, n])

        def be(ap, n):
            return ap.unsqueeze(1).to_broadcast([P, TT, n])

        @block.sync
        def _(sp):
            prefetch_weights(nc, sp, sig, keep, ins)
            sp.wait_ge(sig("scattered"), 16 * 2 * TT)
            sp.dma_start(back_i[:], dram["row_token"].rearrange("(b p) a -> b (p a)", p=P)).then_inc(sig("rows_back"), 16)

        @block.gpsimd
        def _(pool):
            link = Link(pool, sig("pool_link_t"))
            nc.gpsimd.memset(zero_i[:], 0).then_inc(sig("rt_zero"), 1)
            link(nc.gpsimd.memset(ones[:], 1.0))
            link(nc.gpsimd.memset(before[:], 1.0))
            link(nc.gpsimd.affine_select(out=before[:], in_=before[:], compare_op=ALU.is_gt, fill=0.0, base=0,
                                         pattern=[[1, P]], channel_multiplier=-1))
            for ap, pattern, cm in ((iota_e, [[1, E]], 0), (iota_g, [[1, G]], 0), (iota_b, [[1, OVERFLOW_BLOCKS]], 0),
                                    (first_row, [[P, E]], 0)):
                link(nc.gpsimd.iota(ap[:], pattern, base=0, channel_multiplier=cm, allow_small_or_imprecise_dtypes=True))
            link(nc.gpsimd.iota(token[:], [[P, TT]], base=0, channel_multiplier=1))
            nc.gpsimd.nop().then_inc(sig("rt_const"), 1)
            pool.wait_ge(sig("rt_zero"), 1)
            pool.dma_start(dram["row_token"].rearrange("(p b) a -> p (b a)", p=P), zero_i[:]).then_inc(sig("table_zero"), 16)
            pool.wait_ge(sig("table_zero"), 16)
            pool.wait_ge(sig("dest"), 2)
            for t in range(TT):
                for j in range(2):
                    pool.indirect_dma_start(dram["row_token"], bass.IndirectOffsetOnAxis(ap=dest[:, t, j:j + 1], axis=0),
                                            token[:, t:t + 1], None).then_inc(sig("scattered"), 16)

        @block.scalar
        def _(act):
            act.wait_ge(sig("rt_gshift"), 1)
            nc.scalar.activation(gexp[:], gexp[:], ACT.Exp).then_inc(sig("rt_gexp"), 1)
            act.wait_ge(sig("rt_ratio"), 1)
            nc.scalar.activation(best[:, 1, :], best[:, 1, :], ACT.Exp).then_inc(sig("rt_ratio_exp"), 1)

        @block.tensor
        def _(pe):
            pe.wait_ge(sig("rt_const"), 1)
            pe.wait_ge(sig("rt_both"), 1)
            for t in range(TT):
                for s in range(t + 1):
                    nc.tensor.matmul(bank[0][:, t * E:(t + 1) * E], ones[:] if s < t else before[:], both[:, s, :],
                                     start=(s == 0), stop=(s == t))
            for s in range(TT):
                last = nc.tensor.matmul(bank[1][:, 0:E], ones[:], both[:, s, :], start=(s == 0), stop=(s == TT - 1))
            last.then_inc(sig("ranks"), 1)
            pe.wait_ge(sig("back_f"), 1)
            nc.tensor.transpose(bank[2][:, 0:BLOCKS], back_f[:], const["ident"][0:BLOCKS, 0:BLOCKS]).then_inc(sig("back_flipped"), 1)

        @block.vector
        def _(dve):
            link = Link(dve, sig("dve_link_t"))
            tt, stt, ts, red = nc.vector.tensor_tensor, nc.vector.scalar_tensor_tensor, nc.vector.tensor_scalar, nc.vector.tensor_reduce
            gl = logits[:, :, 0:G]
            dve.wait_ge(sig("rt_const"), 1)

            def first_hot(out, vals, top, iota, n):
                link(tt(out, vals, bt(top, n), ALU.is_equal))
                link(stt(out=out, in0=out, scalar=-BIG, in1=be(iota, n), op0=ALU.mult, op1=ALU.add))
                link(red(idx[:], out, AX.X, ALU.min))
                link(ts(idx[:], idx[:], BIG, None, ALU.add))
                link(tt(out, be(iota, n), bt(idx[:], n), ALU.is_equal))

            link(red(gmax[:], gl, AX.X, ALU.max))
            tt(gexp[:], gl, bt(gmax[:], G), ALU.subtract).then_inc(sig("rt_gshift"), 1)
            first_hot(ghot[:], gl, gmax[:], iota_g[:], G)
            link(ts(ghot[:], ghot[:], 1.0, -NEG, ALU.subtract, ALU.mult))
            link(tt(el[:].rearrange("p t (g e) -> p t g e", e=EPG), logits[:, :, G:G + E].rearrange("p t (g e) -> p t g e", e=EPG),
                    ghot[:].unsqueeze(3).to_broadcast([P, TT, G, EPG]), ALU.add))
            link(red(best[:, 0, :], el[:], AX.X, ALU.max))
            first_hot(hot[:, 0], el[:], best[:, 0, :], iota_e[:], E)
            link(stt(out=el[:], in0=hot[:, 0], scalar=2.0 * NEG, in1=el[:], op0=ALU.mult, op1=ALU.add))
            link(red(best[:, 1, :], el[:], AX.X, ALU.max))
            first_hot(hot[:, 1], el[:], best[:, 1, :], iota_e[:], E)
            tt(both[:], hot[:, 0], hot[:, 1], ALU.add).then_inc(sig("rt_both"), 1)
            tt(best[:, 1, :], best[:, 1, :], best[:, 0, :], ALU.subtract).then_inc(sig("rt_ratio"), 1)
            dve.wait_ge(sig("rt_gexp"), 1)
            link(red(gsum[:], gexp[:], AX.X, ALU.add))
            dve.wait_ge(sig("rt_ratio_exp"), 1)
            link(ts(best[:, 0, :], best[:, 1, :], 1.0, None, ALU.add))
            link(tt(gsum[:], gsum[:], best[:, 0, :], ALU.mult))
            link(nc.vector.reciprocal(pair_w[:, :, 0], gsum[:]))
            link(tt(pair_w[:, :, 1], pair_w[:, :, 0], best[:, 1, :], ALU.mult))
            dve.wait_ge(sig("ranks"), 1)
            link(nc.vector.memset(extra[:], 0.0))
            link(nc.vector.memset(ones_e[:], 1.0))
            for j in range(1, S // P):
                link(stt(out=extra[:], in0=bank[1][:, 0:E], scalar=float(j * P), in1=extra[:], op0=ALU.is_gt, op1=ALU.add))
            link(nc.vector.tensor_tensor_scan(extra_end[:], ones_e[:], extra[:], 0.0, ALU.mult, ALU.add))
            link(tt(over_row[:], extra_end[:], extra[:], ALU.subtract))
            link(ts(over_row[:], over_row[:], float(P), float(E * P - P), ALU.mult, ALU.add))
            link(tt(diff[:], first_row[:], over_row[:], ALU.subtract))
            rank = bank[0][:, 0:TT * E].rearrange("p (t e) -> p t e", e=E)
            link(nc.vector.tensor_copy(tmp[:], rank))
            link(stt(out=row[:], in0=tmp[:], scalar=float(P), in1=be(diff[:], E), op0=ALU.is_lt, op1=ALU.mult))
            link(tt(row[:], row[:], tmp[:], ALU.add))
            link(tt(row[:], row[:], be(over_row[:], E), ALU.add))
            for j in range(2):
                link(tt(tmp[:], row[:], hot[:, j], ALU.mult))
                link(red(destf[:], tmp[:], AX.X, ALU.add))
                nc.vector.tensor_copy(dest[:, :, j], destf[:]).then_inc(sig("dest"), 1)
                dve.wait_ge(sig("dest"), j + 1)
            link(nc.vector.tensor_copy(tablef[0:1, 1:1 + E], iota_e[0:1, :]))
            over = table[0:1, 0:OVERFLOW_BLOCKS, :]
            link(tt(over, extra_end[0:1, :].unsqueeze(1).to_broadcast([1, OVERFLOW_BLOCKS, E]),
                    iota_b[0:1, :].unsqueeze(2).to_broadcast([1, OVERFLOW_BLOCKS, E]), ALU.is_le))
            link(red(tablef[0:1, 1 + E:1 + BLOCKS], over, AX.X, ALU.add))
            link(ts(tablef[0:1, 1 + E:1 + BLOCKS], tablef[0:1, 1 + E:1 + BLOCKS], float(E - 1), None, ALU.min))
            link(ts(table[0:1, 0, 0:OVERFLOW_BLOCKS // 2], iota_b[0:1, 0:OVERFLOW_BLOCKS // 2], 2.0, None, ALU.mult))
            link(tt(table[0:1, 0, 0:OVERFLOW_BLOCKS // 2], table[0:1, 0, 0:OVERFLOW_BLOCKS // 2],
                    extra_end[0:1, E - 1:E].to_broadcast([1, OVERFLOW_BLOCKS // 2]), ALU.is_lt))
            link(red(tablef[0:1, 0:1], table[0:1, 0, 0:OVERFLOW_BLOCKS // 2], AX.X, ALU.add))
            link(ts(tablef[0:1, 0:1], tablef[0:1, 0:1], float(E // 2 - 2), None, ALU.add))
            link(nc.vector.tensor_copy(keep["blocks"][:], tablef[:]))
            dve.wait_ge(sig("rows_back"), 16)
            nc.vector.tensor_copy(back_f[:], back_i[:]).then_inc(sig("back_f"), 1)
            dve.wait_ge(sig("back_flipped"), 1)
            link(nc.vector.tensor_copy(keep["row_tok"][:], bank[2][:, 0:BLOCKS]))


def weight_loads(nc, sp, sig, keep, ins, par, e):
    w1, w3, w2 = (ins[n][0] for n in ("exp_w1", "exp_w3", "exp_w2"))

    def of(w, p=P):
        src = w[e] if isinstance(e, int) else w[bass.ds(e, 1)].rearrange("a k n -> (a k) n")
        return src.rearrange("(k p) n -> p k n", p=p)

    sp.dma_start(keep["w13"][:, par, :, 0, :], of(w1)).then_inc(sig(f"w13_in{par}"), 16)
    sp.dma_start(keep["w13"][:, par, :, 1, :], of(w3)).then_inc(sig(f"w13_in{par}"), 16)


def weight_loads_down(nc, sp, sig, keep, ins, par, e):
    w = ins["exp_w2"][0]
    src = w[e] if isinstance(e, int) else w[bass.ds(e, 1)].rearrange("a k n -> (a k) n")
    sp.dma_start(keep["w2"][:, par], src.rearrange("(k p) n -> p k n", p=P)).then_inc(sig(f"w2_in{par}"), 16)


def prefetch_weights(nc, sp, sig, keep, ins):
    for b in range(2):
        weight_loads(nc, sp, sig, keep, ins, b, b)
        weight_loads_down(nc, sp, sig, keep, ins, b, b)


def experts(nc, sig, bank, const, keep, ins, dram):
    psum, ident = const["psum"], const["ident"]
    blocks, row_tok, w13, w2 = keep["blocks"], keep["row_tok"], keep["w13"], keep["w2"]
    FK = FE // P
    with ExitStack() as ctx:
        sb = lambda name, shape, dt=F32: ctx.enter_context(nc.sbuf_tensor(name, shape, dt))
        x_in = sb("ex_x", [P, 2, D])
        x_t = sb("ex_x_t", [P, 2, KT, P])
        sigm = sb("ex_sigm", [P, FE])
        hidden = sb("ex_hidden", [P, FE])
        hid_t = sb("ex_hid_t", [P, 2, FK, P])
        y = sb("ex_y", [P, 2, D])
        idx = sb("ex_idx", [P, 2], I32)
        spare = sb("ex_spare", [P, 1])
        block = ctx.enter_context(nc.Block("experts"))

        def slots(eng, slot):
            inner = eng.value_load(blocks[0:1, 0:1], min_val=E // 2 - 2, max_val=BLOCKS // 2 - 2)
            slot((0, 0), None, (1, 0))
            slot((1, 0), (0, 0), (0, 1))
            slot((0, 1), (1, 0), (1, 1))
            with eng.Fori(1, inner + 1) as j:
                slot((1, j), (0, j), (0, j + 1))
                slot((0, j + 1), (1, j), (1, j + 1))
            slot((1, inner + 1), (0, inner + 1), None)

        @block.sync
        def _(sp):
            inner = sp.value_load(blocks[0:1, 0:1], min_val=E // 2 - 2, max_val=BLOCKS // 2 - 2)
            with sp.Fori(1, inner + 2) as i:
                for par in range(2):
                    e = sp.value_load(blocks[0:1, bass.ds(2 * i + par + 1, 1)], min_val=0, max_val=E - 1)
                    sp.wait_ge(sig(f"up_full{par}"), i)
                    weight_loads(nc, sp, sig, keep, ins, par, e)
                    sp.wait_ge(sig(f"down_full{par}"), i)
                    weight_loads_down(nc, sp, sig, keep, ins, par, e)

        @block.gpsimd
        def _(pool):
            def gather(par, pair):
                b = 2 * pair + par
                if not (isinstance(pair, int) and pair == 0):
                    pool.wait_ge(sig(f"x_flipped{par}"), pair)
                src = row_tok[:, b:b + 1] if isinstance(b, int) else row_tok[:, bass.ds(b, 1)]
                nc.gpsimd.tensor_copy(idx[:, par:par + 1], src).then_inc(sig(f"idx{par}"), 1)
                pool.wait_ge(sig(f"idx{par}"), pair + 1)
                nc.gpsimd.tensor_tensor(spare[:], const["neghalf"][:, 0:1], const["neghalf"][:, 0:1], ALU.mult)
                pool.indirect_dma_start(x_in[:, par, :], None, dram["h_mid"],
                                        bass.IndirectOffsetOnAxis(ap=idx[:, par:par + 1], axis=0)).then_inc(sig(f"x_in_e{par}"), 16)

            def store(par, pair):
                pool.wait_ge(sig(f"y_e{par}"), pair + 1)
                b = 2 * pair + par
                rows = slice(b * P, (b + 1) * P) if isinstance(b, int) else bass.ds(b * P, P)
                pool.dma_start(dram["expert_rows"][rows, :], y[:, par, :]).then_inc(sig(f"y_out{par}"), 16)

            inner = pool.value_load(blocks[0:1, 0:1], min_val=E // 2 - 2, max_val=BLOCKS // 2 - 2)
            gather(0, 0)
            gather(1, 0)
            gather(0, 1)
            store(0, 0)
            gather(1, 1)
            with pool.Fori(0, inner) as j:
                gather(0, j + 2)
                store(1, j)
                gather(1, j + 2)
                store(0, j + 1)
            store(1, inner)
            store(0, inner + 1)
            store(1, inner + 1)
            for q in range(2):
                pool.wait_ge(sig(f"y_out{q}"), 16 * (inner + 2))

        @block.tensor
        def _(pe):
            def flip_x(blk, before):
                pe.wait_ge(sig(f"x_in_e{blk[0]}"), 16 * (blk[1] + 1))
                if before:
                    pe.wait_ge(sig(f"x_t_e{before[0]}"), before[1] + 1)
                for k in range(KT):
                    last = nc.tensor.transpose(psum[:, k * P:(k + 1) * P], x_in[:, blk[0], k * P:(k + 1) * P], ident[:])
                last.then_inc(sig(f"x_flipped{blk[0]}"), 1)

            def down(blk, y_before):
                par, pair = blk
                pe.wait_ge(sig(f"w2_in{par}"), 16 * (pair + 1))
                pe.wait_ge(sig(f"hid_t{par}"), pair + 1)
                if y_before:
                    pe.wait_ge(sig(f"y_e{y_before[0]}"), y_before[1])
                for half in range(2):
                    for k in range(FK):
                        last = nc.tensor.matmul(bank[6 + half], hid_t[:, par, k, :], w2[:, par, k, half * NC5:(half + 1) * NC5],
                                                start=(k == 0), stop=(k == FK - 1))
                last.then_inc(sig(f"down_full{par}"), 1)

            def slot(blk, before, behind):
                par, pair = blk
                if not before:
                    flip_x(blk, None)
                pe.wait_ge(sig(f"x_t_e{par}"), pair + 1)
                pe.wait_ge(sig(f"w13_in{par}"), 32 * (pair + 1))
                if before:
                    pe.wait_ge(sig(f"hidden{before[0]}"), before[1] + 1)
                for j in range(2):
                    for k in range(KT):
                        last = nc.tensor.matmul(bank[2 + j], x_t[:, par, k, :], w13[:, par, k, j, :],
                                                start=(k == 0), stop=(k == KT - 1))
                last.then_inc(sig(f"up_full{par}"), 1)
                if behind:
                    flip_x(behind, blk)
                if before:
                    first = isinstance(pair, int) and pair == 0
                    down(before, None if first else (par, pair))
                pe.wait_ge(sig(f"hidden{par}"), pair + 1)
                if before:
                    pe.wait_ge(sig(f"hid_t{before[0]}"), before[1] + 1)
                for k in range(FK):
                    last = nc.tensor.transpose(bank[4][:, k * P:(k + 1) * P], hidden[:, k * P:(k + 1) * P], ident[:])
                last.then_inc(sig(f"hid_flipped{par}"), 1)
                if not behind:
                    down(blk, (before[0], before[1] + 1))

            slots(pe, slot)

        @block.scalar
        def _(act):
            def move_x(par, pair):
                act.wait_ge(sig(f"x_flipped{par}"), pair + 1)
                nc.scalar.activation(x_t[:, par].rearrange("p k t -> p (k t)"), psum[:, 0:D], ACT.Copy).then_inc(sig(f"x_t_e{par}"), 1)

            def slot(blk, before, behind):
                par, pair = blk
                if not before:
                    move_x(*blk)
                act.wait_ge(sig(f"up_full{par}"), pair + 1)
                nc.scalar.activation(sigm[:], bank[2], ACT.Sigmoid).then_inc(sig(f"sigm{par}"), 1)
                if behind:
                    move_x(*behind)
                act.wait_ge(sig(f"hid_flipped{par}"), pair + 1)
                nc.scalar.activation(hid_t[:, par].rearrange("p k t -> p (k t)"), bank[4], ACT.Copy).then_inc(sig(f"hid_t{par}"), 1)

            slots(act, slot)

        @block.vector
        def _(dve):
            def move_y(par, pair):
                dve.wait_ge(sig(f"down_full{par}"), pair + 1)
                if not (isinstance(pair, int) and pair == 0):
                    dve.wait_ge(sig(f"y_out{par}"), 16 * pair)
                nc.vector.tensor_copy(y[:, par, :], psum[:, 6 * NC5:8 * NC5]).then_inc(sig(f"y_e{par}"), 1)

            def slot(blk, before, behind):
                par, pair = blk
                dve.wait_ge(sig(f"sigm{par}"), pair + 1)
                nc.vector.tensor_tensor(sigm[:], bank[2], sigm[:], ALU.mult).then_inc(sig(f"silu{par}"), 1)
                dve.wait_ge(sig(f"silu{par}"), pair + 1)
                nc.vector.tensor_tensor(hidden[:], bank[3], sigm[:], ALU.mult).then_inc(sig(f"hidden{par}"), 1)
                if before:
                    move_y(*before)
                if not behind:
                    move_y(*blk)

            slots(dve, slot)


def combine(nc, sig, bank, const, keep, ins, dram, out):
    mod_bc, dest, pair_w = keep["mod_bc"], keep["dest"], keep["pair_w"]
    with ExitStack() as ctx:
        sb = lambda name, shape: ctx.enter_context(nc.sbuf_tensor(name, shape, F32))
        rows = sb("cb_rows", [P, 3, 2, D])
        x_in = sb("cb_x", [P, 3, D])
        sq = sb("cb_sq", [P, D])
        ms = sb("cb_ms", [P, TT])
        block = ctx.enter_context(nc.Block("combine"))

        @block.sync
        def _(sp):
            sp.dma_start(mod_bc[:, 4, :], ins["final_g"].rearrange("(a n) -> a n", a=1).partition_broadcast(P).rearrange("p a n -> p (a n)")).then_inc(sig("fg_in"), 16)
            for t in range(TT):
                if t >= 3:
                    sp.wait_ge(sig(f"out_done{t % 3}"), 16 * (t // 3))
                sp.dma_start(x_in[:, t % 3, :], dram["x_mid"][t * P:(t + 1) * P, :]).then_inc(sig(f"cb_x_in{t % 3}"), 16)

        @block.gpsimd
        def _(pool):
            def gather(t):
                if t >= 3:
                    pool.wait_ge(sig("cb_x"), t - 2)
                for j in range(2):
                    pool.indirect_dma_start(rows[:, t % 3, j, :], None, dram["expert_rows"],
                                            bass.IndirectOffsetOnAxis(ap=dest[:, t, j:j + 1], axis=0)).then_inc(sig(f"cb_rows_in{t % 3}"), 16)
            for t in range(3):
                gather(t)
            for t in range(TT):
                pool.wait_ge(sig("cb_ms"), t + 1)
                nc.gpsimd.tensor_tensor(ms[:, t:t + 1], ms[:, t:t + 1], const["neghalf"][:, 0:1], ALU.pow).then_inc(sig("cb_rstd"), 1)
                if t + 3 < TT:
                    gather(t + 3)

        @block.scalar
        def _(act):
            for t in range(TT):
                act.wait_ge(sig("cb_x"), t + 1)
                if t >= 1:
                    act.wait_ge(sig("cb_ss"), t)
                nc.scalar.activation(sq[:], x_in[:, t % 3, :], ACT.Square, accum_out=ms[:, t:t + 1]).then_inc(sig("cb_ss"), 1)
                act.wait_ge(sig("cb_out"), t + 1)
                act.dma_start(out[0, t * P:(t + 1) * P, :], x_in[:, t % 3, :]).then_inc(sig(f"out_done{t % 3}"), 16)
            for b in range(3):
                act.wait_ge(sig(f"out_done{b}"), 16 * ((TT + 2 - b) // 3))

        @block.tensor
        def _(pe):
            pass

        @block.vector
        def _(dve):
            link = Link(dve, sig("dve_link_c"))
            tt, stt, ts = nc.vector.tensor_tensor, nc.vector.scalar_tensor_tensor, nc.vector.tensor_scalar
            dve.wait_ge(sig("fg_in"), 16)
            for t in range(TT):
                a, b, x = rows[:, t % 3, 0, :], rows[:, t % 3, 1, :], x_in[:, t % 3, :]
                dve.wait_ge(sig(f"cb_rows_in{t % 3}"), 32 * (t // 3 + 1))
                dve.wait_ge(sig(f"cb_x_in{t % 3}"), 16 * (t // 3 + 1))
                link(ts(a, a, pair_w[:, t, 0:1], None, ALU.mult))
                link(stt(out=a, in0=b, scalar=pair_w[:, t, 1:2], in1=a, op0=ALU.mult, op1=ALU.add))
                link(tt(a, a, mod_bc[:, 3, :], ALU.mult))
                tt(x, x, a, ALU.add).then_inc(sig("cb_x"), 1)
                dve.wait_ge(sig("cb_ss"), t + 1)
                ts(ms[:, t:t + 1], ms[:, t:t + 1], 1.0 / D, EPS, ALU.mult, ALU.add).then_inc(sig("cb_ms"), 1)
                dve.wait_ge(sig("cb_rstd"), t + 1)
                stt(out=x, in0=x, scalar=ms[:, t:t + 1], in1=mod_bc[:, 4, :], op0=ALU.mult, op1=ALU.mult).then_inc(sig("cb_out"), 1)


def constants(nc, sig, const):
    with nc.Block("constants") as block:
        @block.gpsimd
        def _(pool):
            nc.gpsimd.memset(const["ident"][:], 0.0).then_inc(sig("const_set"), 1)
            nc.gpsimd.memset(const["ones_row"][:], 1.0).then_inc(sig("const_set"), 1)
            nc.gpsimd.memset(const["neghalf"][:], -0.5).then_inc(sig("const_set"), 1)
            pool.wait_ge(sig("const_set"), 1)
            nc.gpsimd.affine_select(out=const["ident"][:], in_=const["ident"][:], compare_op=ALU.not_equal, fill=1.0,
                                    base=0, pattern=[[-1, P]], channel_multiplier=1).then_inc(sig("const_set"), 1)
            pool.wait_ge(sig("const_set"), 4)


def build(nc, ins, out):
    dram = {
        "p_rwkv": nc.dram_tensor("p_rwkv", (S + 1, SHIFT), F32, kind="Internal").ap(),
        "gates": nc.dram_tensor("gates", (S, 2 * D), F32, kind="Internal").ap(),
        "x_mid": nc.dram_tensor("x_mid", (S, D), F32, kind="Internal").ap(),
        "h_mid": nc.dram_tensor("h_mid", (S, D), F32, kind="Internal").ap(),
        "row_token": nc.dram_tensor("row_token", (ROWS, 1), I32, kind="Internal").ap(),
        "expert_rows": nc.dram_tensor("expert_rows", (ROWS, D), F32, kind="Internal").ap(),
    }
    with ExitStack() as ctx:
        sig = Signals(nc, ctx)
        psum = ctx.enter_context(nc.psum_tensor("psum", [P, 8 * NC5], F32))
        bank = [psum[:, i * NC5:(i + 1) * NC5] for i in range(8)]
        sb = lambda name, shape, dt=F32: ctx.enter_context(nc.sbuf_tensor(name, shape, dt))
        const = {"ident": sb("ident", [P, P]), "ones_row": sb("ones_row", [1, P]), "neghalf": sb("neghalf", [P, H]), "psum": psum}
        keep = {"mod_bc": sb("mod_bc", [P, 5, D])}
        keep["logits"] = keep["mod_bc"][:, 4, 0:TT * (G + E)].rearrange("p (t e) -> p t e", e=G + E)
        constants(nc, sig, const)
        sig.next_stage("constants")
        with ExitStack() as mid:
            sbm = lambda name, shape: mid.enter_context(nc.sbuf_tensor(name, shape, F32))
            keep["o_fox"] = sbm("o_fox", [P, TT, W])
            with ExitStack() as early:
                sbe = lambda name, shape: early.enter_context(nc.sbuf_tensor(name, shape, F32))
                keep["q_t"] = sbe("q_t", [P, W // P, S])
                keep["k_t"] = sbe("k_t", [P, W // P, S])
                keep["v_tok"] = sbe("v_tok", [P, TT, W])
                keep["ncum"] = sbe("ncum", [H, S])
                project(nc, sig, bank, const, keep, ins, dram)
                sig.next_stage("project")
                attend(nc, sig, bank, const, keep, dram)
                sig.next_stage("attend")
            keep["o_rwkv"] = sbm("o_rwkv", [P, TT, W])
            recur(nc, sig, bank, const, keep, ins, dram)
            sig.next_stage("recur")
            merge(nc, sig, bank, const, keep, ins, dram)
            sig.next_stage("merge")
        with ExitStack() as late:
            sbl = lambda name, shape, dt=F32: late.enter_context(nc.sbuf_tensor(name, shape, dt))
            keep["dest"] = sbl("dest", [P, TT, 2], I32)
            keep["pair_w"] = sbl("pair_w", [P, TT, 2])
            keep["blocks"] = sbl("blocks", [1, 1 + BLOCKS], I32)
            keep["row_tok"] = sbl("row_tok", [P, BLOCKS], I32)
            keep["w13"] = sbl("w13", [P, 2, KT, 2, FE])
            keep["w2"] = sbl("w2", [P, 2, FE // P, D])
            route(nc, sig, bank, const, keep, ins, dram)
            sig.next_stage("route")
            experts(nc, sig, bank, const, keep, ins, dram)
            sig.next_stage("experts")
            combine(nc, sig, bank, const, keep, ins, dram, out)


INPUTS = ["x", "c", "ada_w", "ada_b", "norm1_g", "w_in", "fox_forget_b", "shift_mu", "rwkv_w0", "rwkv_w2", "rwkv_a0",
          "rwkv_a2", "rwkv_g2", "rwkv_k_k", "rwkv_k_a", "rwkv_r_k", "ln_x_g", "ln_x_b", "w_out_fox", "w_out_rwkv",
          "w_o", "norm2_g", "router_group_w", "router_group_b", "router_expert_w", "router_expert_b", "exp_w1",
          "exp_w3", "exp_w2", "final_g"]


def kernel(**inputs):
    import numpy as _np
    import concourse.bacc as _bacc
    from concourse import mybir as _mybir
    from concourse.bass_utils import run_bass_kernel_spmd as _run

    nc = _bacc.Bacc("TRN2", target_bir_lowering=False, num_devices=1)
    arrays, aps = {}, {}
    for name in INPUTS:
        a = _np.ascontiguousarray(inputs[name])
        arrays[f"in_{name}"] = a
        aps[name] = nc.dram_tensor(f"in_{name}", a.shape, _mybir.dt.from_np(a.dtype), kind="ExternalInput").ap()
    out = nc.dram_tensor("out", (1, S, D), F32, kind="ExternalOutput").ap()
    build(nc, aps, out)
    r = _run(nc, [arrays], core_ids=[0])
    return r.results[0]["out"]
```

```python
from contextlib import ExitStack

import numpy as np

import concourse.bass as bass
from concourse import mybir

F32 = mybir.dt.float32
F32R = mybir.dt.float32r
I32 = mybir.dt.int32
ALU = mybir.AluOpType
ACT = mybir.ActivationFunctionType
AX = mybir.AxisListType

P = 128
D = 1024
S = 1024
TT = S // P
KT = D // P
H = 8
HD = 64
W = H * HD
NC5 = 512
LORA = 64
GLORA = 128
SHIFT = 3 * W + 2 * LORA + GLORA
COL_V = 2 * W
COL_F = 3 * W
COL_R = COL_F + H
COL_G = COL_R + SHIFT
CHUNK = 64
G, EPG = 4, 8
E = G * EPG
FE = 512
NEG = -1.0e30
EPS = 1e-6
LN_EPS = 64e-5
EXPM05 = float(np.exp(-0.5))
OVERFLOW_BLOCKS = 2 * S // P
BLOCKS = E + OVERFLOW_BLOCKS
ROWS = BLOCKS * P
LASTING = ("chunk_in0", "chunk_in1", "ring_used", "w13_in00", "w13_in01", "w13_in10", "w13_in11", "w2_in0", "w2_in1")
SOFTWARE_DMA = ("g1_in", "adab_in", "fb_in", "wf_in", "g2_in", "zrow_out", "mu_in", "x_mid_out0", "x_mid_out1",
                "h_mid_out0", "h_mid_out1", "table_set", "scattered", "x_in_e0", "x_in_e1", "y_out0", "y_out1")


class Signals:

    POOL = 100

    def __init__(self, nc, ctx):
        self.nc = nc
        self.pool = [ctx.enter_context(nc.semaphore(f"stage_{i}")) for i in range(self.POOL)]
        self.lasting = {n: ctx.enter_context(nc.semaphore(n)) for n in LASTING + SOFTWARE_DMA}
        self.names = {}

    def __call__(self, name):
        if name in self.lasting:
            return self.lasting[name]
        return self.pool[self.names.setdefault(name, len(self.names))]

    def next_stage(self, stage):
        used = [self.pool[i].num for i in range(len(self.names))]
        self.names = {}
        assert used == list(range(used[0], used[0] + len(used)))
        with self.nc.Block(f"{stage}_cleared") as block:
            @block.gpsimd
            def _(pool):
                pool.sem_clear(range(used[0], used[0] + len(used)))


class Ring:

    def __init__(self, sig, ring, ins):
        self.sig, self.ring = sig, ring
        ada = ins["ada_w"][0].rearrange("(p k) n -> p k n", k=KT)
        w_in = ins["w_in"][0].rearrange("(k p) n -> p k n", p=P)
        mod = [("mod", j, ada[:, :, j * NC5:(j + 1) * NC5]) for j in range(12)]
        self.proj = [(("q", "k")[j], 0, w_in[:, :, j * NC5:(j + 1) * NC5]) for j in range(2)]
        self.proj += [("v", 0, w_in[:, :, COL_V:COL_V + NC5])]
        self.proj += [("rwkv", j, w_in[:, :, COL_R + j * NC5:COL_R + min((j + 1) * NC5, SHIFT)]) for j in range(-(-SHIFT // NC5))]
        self.proj += [("gate", j, w_in[:, :, COL_G + j * NC5:COL_G + (j + 1) * NC5]) for j in range(2 * D // NC5)]
        self.order = mod[:4]
        for i, c in enumerate(self.proj):
            self.order += [c] + mod[4 + i:5 + i] if i < 8 else [c]
        self.turn = {(kind, j): i for i, (kind, j, _) in enumerate(self.order)}

    def load(self, sp, turns):
        for i in turns:
            src = self.order[i][2]
            if i >= 2:
                sp.wait_ge(self.sig("ring_used"), i - 1)
            sp.dma_start(self.ring[:, i % 2, :, 0:src.shape[2]], src).then_inc(self.sig(f"chunk_in{i % 2}"), 16)

    def arrived(self, eng, i):
        eng.wait_ge(self.sig(f"chunk_in{i % 2}"), 16 * (i // 2 + 1))

    def accumulate(self, nc, dve, link, j, c_silu, dst):
        i = self.turn["mod", j]
        self.arrived(dve, i)
        link(nc.vector.tensor_scalar(dst, self.ring[:, i % 2, 0, :], c_silu[:, 0:1], None, ALU.mult))
        for k in range(1, KT):
            last = nc.vector.scalar_tensor_tensor(out=dst, in0=self.ring[:, i % 2, k, :], scalar=c_silu[:, k:k + 1],
                                                  in1=dst, op0=ALU.mult, op1=ALU.add)
            if k < KT - 1:
                link(last)
        last.then_inc(self.sig("ring_used"), 1)
        dve.wait_ge(self.sig("ring_used"), i + 1)


class Link:

    def __init__(self, eng, sem, start=0):
        self.eng, self.sem, self.n = eng, sem, start

    def __call__(self, ins):
        self.n += 1
        ins.then_inc(self.sem, 1)
        self.eng.wait_ge(self.sem, self.n)


def modulate(nc, sig, bank, const, keep, ins, dram, weights):
    h_hi, h_lo, c_silu = keep["h_hi"], keep["h_lo"], keep["c_silu"]
    HALF = TT // 2
    with ExitStack() as ctx:
        sb = lambda name, shape, dt=F32: ctx.enter_context(nc.sbuf_tensor(name, shape, dt))
        x_in = sb("x_in", [P, TT, D])
        acc = sb("mod_acc", [P, 2, D])
        full = sb("h_full", [P, 2, NC5])
        sq = sb("x_sq", [P, D])
        c_col = sb("c_col", [P, KT])
        g1_col = sb("g1_col", [P, KT])
        b_col = sb("b_col", [P, 2 * KT])
        cols = sb("mod_cols", [P, 2 * KT])
        ss = sb("ss", [P, TT])
        zero = sb("zero_row", [1, SHIFT])
        block = ctx.enter_context(nc.Block("modulate"))

        @block.sync
        def _(sp):
            sp.dma_start(c_col[:], ins["c"][0].rearrange("(p k) -> p k", k=KT)).then_inc(sig("c_in"), 16)
            for t in range(TT):
                sp.dma_start(x_in[:, t, :], ins["x"][0, t * P:(t + 1) * P, :]).then_inc(sig(f"x_in{t}"), 16)
                if t < 2:
                    weights.load(sp, [t])
            weights.load(sp, range(2, 6))

        @block.gpsimd
        def _(pool):
            pool.dma_start(g1_col[:], ins["norm1_g"][0].rearrange("(k p) -> p k", p=P), allow_slow_non_contiguous=True).then_inc(sig("g1_in"), 16)
            pool.dma_start(b_col[:], ins["ada_b"][0, 0:2 * D].rearrange("(k p) -> p k", p=P), allow_slow_non_contiguous=True).then_inc(sig("adab_in"), 16)
            nc.gpsimd.memset(zero[:], 0.0).then_inc(sig("zrow"), 1)
            pool.wait_ge(sig("zrow"), 1)
            pool.dma_start(dram["p_rwkv"][0:1, :], zero[:]).then_inc(sig("zrow_out"), 16)
            for t in range(TT):
                pool.wait_ge(sig("x_ms"), t + 1)
                nc.gpsimd.tensor_tensor(ss[:, t:t + 1], ss[:, t:t + 1], const["neghalf"][:, 0:1], ALU.pow).then_inc(sig("x_rstd"), 1)
            pool.wait_ge(sig("zrow_out"), 16)

        @block.vector
        def _(dve):
            link = Link(dve, sig("dve_link_a"))
            tt, stt, ts = nc.vector.tensor_tensor, nc.vector.scalar_tensor_tensor, nc.vector.tensor_scalar
            dve.wait_ge(sig("c_sig"), 1)
            link(tt(c_silu[:], c_silu[:], c_col[:], ALU.mult))
            for t in range(TT):
                dve.wait_ge(sig("x_ss"), t + 1)
                ts(ss[:, t:t + 1], ss[:, t:t + 1], 1.0 / D, EPS, ALU.mult, ALU.add).then_inc(sig("x_ms"), 1)
                dve.wait_ge(sig("x_rstd"), t + 1)
                ts(x_in[:, t, :], x_in[:, t, :], ss[:, t:t + 1], None, ALU.mult).then_inc(sig("xn_ready"), 1)
                if t % 2 == 1:
                    j = t // 2
                    weights.accumulate(nc, dve, link, j, c_silu, acc[:, j // 2, (j % 2) * NC5:(j % 2 + 1) * NC5])
                    nc.vector.engine_nop().then_inc(sig("mod_acc"), 1)
            dve.wait_ge(sig("mod_cols"), 1)
            dve.wait_ge(sig("g1_in"), 16)
            dve.wait_ge(sig("adab_in"), 16)
            link(tt(cols[:], bank[0][:, 0:2 * KT], b_col[:], ALU.add))
            stt(out=cols[:, KT:2 * KT], in0=cols[:, KT:2 * KT], scalar=1.0, in1=g1_col[:], op0=ALU.add, op1=ALU.mult).then_inc(sig("cols_ready"), 1)
            dve.wait_ge(sig("cols_ready"), 1)
            for n in range(2 * KT):
                k, half = n // 2, n % 2
                dve.wait_ge(sig("h_hi"), n + 1)
                ts(full[:, n % 2, :], bank[1 + n % 4], cols[:, KT + k:KT + k + 1], cols[:, k:k + 1], ALU.mult, ALU.add).then_inc(sig("h_full"), 1)
                dve.wait_ge(sig("h_full"), n + 1)
                part = h_lo[:, k, half * NC5:(half + 1) * NC5]
                tt(part, full[:, n % 2, :], h_hi[:, k, half * NC5:(half + 1) * NC5].bitcast(F32), ALU.subtract).then_inc(sig("h_lo"), 1)
            dve.wait_ge(sig("h_lo"), 2 * KT)

        @block.scalar
        def _(act):
            act.wait_ge(sig("c_in"), 16)
            nc.scalar.activation(c_silu[:], c_col[:], ACT.Sigmoid).then_inc(sig("c_sig"), 1)
            for t in range(TT):
                act.wait_ge(sig(f"x_in{t}"), 16)
                if t >= 1:
                    act.wait_ge(sig("x_ss"), t)
                nc.scalar.activation(sq[:], x_in[:, t, :], ACT.Square, accum_out=ss[:, t:t + 1]).then_inc(sig("x_ss"), 1)
            act.wait_ge(sig("cols_ready"), 1)
            for n in range(2 * KT):
                k, half = n // 2, n % 2
                act.wait_ge(sig("x_flipped"), n + 1)
                nc.scalar.activation(h_hi[:, k, half * NC5:(half + 1) * NC5], bank[1 + n % 4], ACT.Identity,
                                     scale=cols[:, KT + k:KT + k + 1], bias=cols[:, k:k + 1]).then_inc(sig("h_hi"), 1)

        @block.tensor
        def _(pe):
            for i in range(2 * KT):
                if i % 4 == 0:
                    pe.wait_ge(sig("mod_acc"), i // 4 + 1)
                last = nc.tensor.matmul(bank[0][:, i:i + 1], acc[:, i // KT, (i % KT) * P:(i % KT + 1) * P], const["ones"][:, 0:1],
                                        start=True, stop=True)
            last.then_inc(sig("mod_cols"), 1)
            pe.wait_ge(sig("xn_ready"), TT)
            for n in range(2 * KT):
                k, half = n // 2, n % 2
                if n >= 4:
                    pe.wait_ge(sig("h_full"), n - 3)
                for t in range(HALF):
                    last = nc.tensor.transpose(bank[1 + n % 4][:, t * P:(t + 1) * P],
                                               x_in[:, half * HALF + t, k * P:(k + 1) * P], const["ident"][:])
                last.then_inc(sig("x_flipped"), 1)


def matmul3(nc, out, pairs):
    n = len(pairs)
    for i, ((a_hi, a_lo), (b_hi, b_lo)) in enumerate(pairs):
        nc.tensor.matmul(out, a_hi, b_hi, start=(i == 0), stop=False)
        nc.tensor.matmul(out, a_hi, b_lo, start=False, stop=False)
        last = nc.tensor.matmul(out, a_lo, b_hi, start=False, stop=(i == n - 1))
    return last


def project(nc, sig, bank, const, keep, ins, dram, weights):
    h_hi, h_lo, c_silu, mod_bc, ring = (keep[n] for n in ("h_hi", "h_lo", "c_silu", "mod_bc", "ring"))
    proj = weights.proj
    with ExitStack() as ctx:
        sb = lambda name, shape, dt=F32: ctx.enter_context(nc.sbuf_tensor(name, shape, dt))
        w_hi = sb("w_hi", [P, 2, KT, NC5], F32R)
        w_lo = sb("w_lo", [P, 2, KT, NC5], F32R)
        stage = sb("stage", [P, 3, NC5])
        stage_r = sb("stage_r", [P, 3, 2, NC5], F32R)
        w_f = sb("w_f", [P, KT, H])
        wf_r = sb("wf_r", [P, 2, KT, H], F32R)
        f_b = sb("f_b", [H, 1])
        f_abs = sb("f_abs", [H, NC5])
        f_min = sb("f_min", [H, NC5])
        ncum = sb("ncum_sb", [H, 2, NC5])
        block = ctx.enter_context(nc.Block("project"))
        def mod_dst(j):
            return mod_bc[:, (j - 4) // 2, (j % 2) * NC5:(j % 2 + 1) * NC5]

        @block.sync
        def _(sp):
            weights.load(sp, range(6, len(weights.order)))

        @block.gpsimd
        def _(pool):
            pool.dma_start(w_f[:], ins["w_in"][0].rearrange("(k p) n -> p k n", p=P)[:, :, COL_F:COL_R]).then_inc(sig("wf_in"), 16)
            pool.dma_start(f_b[:], ins["fox_forget_b"][0].rearrange("(h a) -> h a", a=1)).then_inc(sig("fb_in"), 16)
            pool.dma_start(mod_bc[:, 4, :], ins["norm2_g"].partition_broadcast(P).rearrange("p a n -> p (a n)")).then_inc(sig("g2_in"), 16)

        @block.vector
        def _(dve):
            link = Link(dve, sig("dve_link_p"))
            tt, stt, ts = nc.vector.tensor_tensor, nc.vector.scalar_tensor_tensor, nc.vector.tensor_scalar

            def split(j):
                kind, num, src = proj[j]
                i, n = weights.turn[kind, num], src.shape[2]
                dve.wait_ge(sig("w_hi"), j + 1)
                tt(w_lo[:, j % 2, :, 0:n], ring[:, i % 2, :, 0:n], w_hi[:, j % 2, :, 0:n].bitcast(F32), ALU.subtract).then_inc(sig("ring_used"), 1)

            split(0)
            dve.wait_ge(sig("wf_hi"), 1)
            tt(wf_r[:, 1], w_f[:], wf_r[:, 0].bitcast(F32), ALU.subtract).then_inc(sig("wf_lo"), 1)
            weights.accumulate(nc, dve, link, 4, c_silu, mod_dst(4))
            split(1)
            dve.wait_ge(sig("fb_in"), 16)
            for half in range(2):
                dve.wait_ge(sig("f_abs"), half + 1)
                ts(f_min[:], bank[half][0:H, :], f_b[:], 0.0, ALU.add, ALU.min).then_inc(sig("f_min"), 1)
                dve.wait_ge(sig("f_ln"), half + 1)
                dve.wait_ge(sig("f_min"), half + 1)
                tt(f_min[:], f_abs[:], f_min[:], ALU.subtract).then_inc(sig("f_neg"), 1)
                dve.wait_ge(sig("f_neg"), half + 1)
                nc.vector.tensor_tensor_scan(ncum[:, half, :], const["ones"][0:H, 0:1].to_broadcast([H, NC5]), f_min[:], ncum[:, 0, NC5 - 1:NC5] if half else 0.0,
                                             ALU.mult, ALU.add).then_inc(sig("ncum"), 1)
                dve.wait_ge(sig("ncum"), half + 1)
            for j in range(len(proj)):
                kind, num, _ = proj[j]
                for i in range(8):
                    fill = 8 * j + i
                    if kind in ("q", "k"):
                        dve.wait_ge(sig("proj_evac"), fill + 1)
                        tt(stage_r[:, fill % 3, 1, :], bank[2 + fill % 4], stage_r[:, fill % 3, 0, :].bitcast(F32), ALU.subtract).then_inc(sig("qk_lo"), 1)
                    if i == 1 and j >= 1 and j + 1 < len(proj):
                        split(j + 1)
                if j < 7:
                    weights.accumulate(nc, dve, link, 5 + j, c_silu, mod_dst(5 + j))
            dve.wait_ge(sig("g2_in"), 16)
            dve.wait_ge(sig("bc_evac"), 8)
            for j in range(8):
                dst = mod_bc[:, j // 2, (j % 2) * NC5:(j % 2 + 1) * NC5]
                dve.wait_ge(sig(f"adab_in{j % 3}"), 16 * (j // 3 + 1))
                tt(dst, dst, stage[:, j % 3, :], ALU.add).then_inc(sig("mod_biased"), 1)
            dve.wait_ge(sig("mod_biased"), 8)
            stt(out=mod_bc[:, 2, :], in0=mod_bc[:, 2, :], scalar=1.0, in1=mod_bc[:, 4, :],
                op0=ALU.add, op1=ALU.mult).then_inc(sig("a2_ready"), 1)
            dve.wait_ge(sig("a2_ready"), 1)

        @block.scalar
        def _(act):
            def high(j):
                kind, num, src = proj[j]
                i, n = weights.turn[kind, num], src.shape[2]
                weights.arrived(act, i)
                if j >= 2:
                    act.wait_ge(sig("proj_full"), 8 * (j - 1))
                nc.scalar.activation(w_hi[:, j % 2, :, 0:n], ring[:, i % 2, :, 0:n], ACT.Copy).then_inc(sig("w_hi"), 1)

            high(0)
            act.wait_ge(sig("wf_in"), 16)
            nc.scalar.activation(wf_r[:, 0], w_f[:], ACT.Copy).then_inc(sig("wf_hi"), 1)
            high(1)
            act.wait_ge(sig("fb_in"), 16)
            for half in range(2):
                act.wait_ge(sig("f_full"), half + 1)
                if half:
                    act.wait_ge(sig("f_neg"), 1)
                nc.scalar.activation(f_abs[:], bank[half][0:H, :], ACT.Abs, bias=f_b[:]).then_inc(sig("f_abs"), 1)
                act.wait_ge(sig("f_abs"), half + 1)
                nc.scalar.activation(f_abs[:], f_abs[:], ACT.Exp, scale=-1.0).then_inc(sig("f_exp"), 1)
                act.wait_ge(sig("f_exp"), half + 1)
                nc.scalar.activation(f_abs[:], f_abs[:], ACT.Ln, bias=1.0).then_inc(sig("f_ln"), 1)
            act.wait_ge(sig("ncum"), 2)
            act.dma_start(dram["ncum"], ncum[:].rearrange("h a s -> h (a s)")).then_inc(sig("ncum_out"), 16)
            staged, out3 = 0, [0, 0, 0]
            for j, (kind, num, src) in enumerate(proj):
                n = src.shape[2]
                for i in range(8):
                    fill = 8 * j + i
                    ps = bank[2 + fill % 4]
                    act.wait_ge(sig("proj_full"), fill + 1)
                    if kind in ("q", "k"):
                        if fill >= 3:
                            act.wait_ge(sig(f"qk_out{fill % 3}"), 16 * (fill // 3))
                        nc.scalar.activation(stage_r[:, fill % 3, 0, :], ps, ACT.Copy).then_inc(sig("proj_evac"), 1)
                        act.wait_ge(sig("qk_lo"), fill + 1)
                        dst = dram["qk"][j, :, (i // 2) * P:(i // 2 + 1) * P, (i % 2) * NC5:(i % 2 + 1) * NC5]
                        act.dma_start(dst.rearrange("a p n -> p a n"), stage_r[:, fill % 3].bitcast(F32)).then_inc(sig(f"qk_out{fill % 3}"), 16)
                    else:
                        b = staged % 3
                        if staged >= 3:
                            act.wait_ge(sig(f"staged_out{b}"), 16 * (staged // 3))
                        nc.scalar.activation(stage[:, b, 0:n], ps[:, 0:n], ACT.Sigmoid if kind == "gate" else ACT.Copy).then_inc(sig("proj_evac"), 1)
                        act.wait_ge(sig("proj_evac"), fill + 1)
                        rows = slice(i * P, (i + 1) * P)
                        dst = {"v": lambda: dram["v"][rows, :],
                               "rwkv": lambda: dram["p_rwkv"][1 + i * P:1 + (i + 1) * P, num * NC5:num * NC5 + n],
                               "gate": lambda: dram["gates"][rows, num * NC5:num * NC5 + n]}[kind]()
                        act.dma_start(dst, stage[:, b, 0:n]).then_inc(sig(f"staged_out{b}"), 16)
                        staged += 1
                    if i == 1 and j >= 1 and j + 1 < len(proj):
                        high(j + 1)
            for i in range(8):
                act.wait_ge(sig("bc_full"), i + 1)
                nc.scalar.activation(mod_bc[:, i // 2, (i % 2) * NC5:(i % 2 + 1) * NC5], bank[i % 2], ACT.Copy).then_inc(sig("bc_evac"), 1)
            for b in range(3):
                act.wait_ge(sig(f"staged_out{b}"), 16 * ((staged + 2 - b) // 3))
                act.wait_ge(sig(f"qk_out{b}"), 16 * ((16 + 2 - b) // 3))
            act.wait_ge(sig("ncum_out"), 16)
            for j in range(8):
                if j >= 3:
                    act.wait_ge(sig("mod_biased"), j - 2)
                act.dma_start(stage[:, j % 3, :], ins["ada_b"][:, (4 + j) * NC5:(5 + j) * NC5].partition_broadcast(P).rearrange("p a n -> p (a n)")).then_inc(sig(f"adab_in{j % 3}"), 16)

        @block.tensor
        def _(pe):
            pe.wait_ge(sig("wf_lo"), 1)
            for half in range(2):
                tok = slice(half * NC5, (half + 1) * NC5)
                matmul3(nc, bank[half][0:H, :], [((wf_r[:, 0, k, :], wf_r[:, 1, k, :]), (h_hi[:, k, tok], h_lo[:, k, tok]))
                                                 for k in range(KT)]).then_inc(sig("f_full"), 1)
            for j, (kind, num, src) in enumerate(proj):
                n = src.shape[2]
                pe.wait_ge(sig("ring_used"), weights.turn[kind, num] + 1)
                for i in range(8):
                    fill = 8 * j + i
                    if fill >= 4:
                        pe.wait_ge(sig("proj_evac"), fill - 3)
                        if fill - 4 < 16:
                            pe.wait_ge(sig("qk_lo"), fill - 3)
                    ps = bank[2 + fill % 4]
                    if kind in ("q", "k"):
                        f, tok = slice((i // 2) * P, (i // 2 + 1) * P), slice((i % 2) * NC5, (i % 2 + 1) * NC5)
                        pairs = [((w_hi[:, j % 2, k, f], w_lo[:, j % 2, k, f]), (h_hi[:, k, tok], h_lo[:, k, tok])) for k in range(KT)]
                    else:
                        tok = slice(i * P, (i + 1) * P)
                        pairs = [((h_hi[:, k, tok], h_lo[:, k, tok]), (w_hi[:, j % 2, k, 0:n], w_lo[:, j % 2, k, 0:n])) for k in range(KT)]
                    matmul3(nc, ps[:, 0:n], pairs).then_inc(sig("proj_full"), 1)
            pe.wait_ge(sig("f_min"), 2)
            pe.wait_ge(sig("ring_used"), len(weights.order))
            for i in range(8):
                if i >= 2:
                    pe.wait_ge(sig("bc_evac"), i - 1)
                nc.tensor.matmul(bank[i % 2], const["ones"][:], mod_bc[:, i // 2, (i % 2) * NC5:(i % 2 + 1) * NC5],
                                 start=True, stop=True).then_inc(sig("bc_full"), 1)


def attend(nc, sig, bank, const, keep, dram):
    psum = const["psum"]
    items = [(h, t) for h in range(H) for t in range(TT)]
    with ExitStack() as ctx:
        sb = lambda name, shape, dt=F32: ctx.enter_context(nc.sbuf_tensor(name, shape, dt))
        causal = sb("causal", [P, P])
        gate_bias = sb("gate_bias", [P, 2, S])
        q2 = sb("q2", [P, 2, S], F32R)
        k2 = sb("k2", [P, 2, 2, S], F32R)
        v_h = sb("v_h", [P, 2, TT, HD])
        logits = sb("att_logits", [P, 2, S])
        probs = sb("att_probs", [P, 3, S])
        probs_t = sb("att_probs_t", [P, 2, S])
        o_t = sb("att_o_t", [HD, 2, S])
        neg_max = sb("neg_max", [P, len(items)])
        row_sum = sb("row_sum", [P, len(items)])
        block = ctx.enter_context(nc.Block("attend"))

        def scores(n):
            return psum[:, (n % 2) * 2 * NC5:(n % 2 + 1) * 2 * NC5]

        @block.sync
        def _(sp):
            def store(h):
                sp.wait_ge(sig("o_t"), 2 * (h + 1))
                sp.dma_start(dram["o_fox_t"][h * HD:(h + 1) * HD, :], o_t[:, h % 2, :]).then_inc(sig(f"o_t_out{h % 2}"), 16)

            for h in range(H):
                b = h % 2
                if h >= 2:
                    sp.wait_ge(sig("mixed"), TT * (h - 1))
                rows = slice(h * HD, (h + 1) * HD)
                for part in range(2):
                    half = slice(part * HD, (part + 1) * HD)
                    sp.dma_start(q2[half, b, :].bitcast(F32), dram["qk"][0, part, rows, :]).then_inc(sig(f"head_in{b}"), 16)
                    for copy in range(2):
                        sp.dma_start(k2[copy * HD:(copy + 1) * HD, b, part, :].bitcast(F32), dram["qk"][1, part, rows, :]).then_inc(sig(f"head_in{b}"), 16)
                sp.dma_start(v_h[:, b], dram["v"][:, rows].rearrange("(t p) d -> p t d", p=P)).then_inc(sig(f"head_in{b}"), 16)
                sp.dma_start(gate_bias[:, b, :], dram["ncum"][h:h + 1, :].partition_broadcast(P).rearrange("p a n -> p (a n)")).then_inc(sig(f"head_in{b}"), 16)
                if h >= 2:
                    store(h - 2)
            store(H - 2)
            store(H - 1)
            for b in range(2):
                sp.wait_ge(sig(f"o_t_out{b}"), 16 * H // 2)

        def head_here(eng, h):
            eng.wait_ge(sig(f"head_in{h % 2}"), 16 * 8 * (h // 2 + 1))

        @block.gpsimd
        def _(pool):
            nc.gpsimd.memset(causal[:], 0.0).then_inc(sig("att_const"), 1)
            pool.wait_ge(sig("att_const"), 1)
            nc.gpsimd.affine_select(out=causal[:], in_=causal[:], compare_op=ALU.is_ge, fill=NEG, base=0,
                                    pattern=[[-1, P]], channel_multiplier=1).then_inc(sig("att_const"), 1)

        @block.tensor
        def _(pe):
            def score(n):
                h, t = items[n]
                if t == 0:
                    head_here(pe, h)
                if n >= 2:
                    pe.wait_ge(sig("scores_read"), n - 1)
                for lo in range(0, (t + 1) * P, NC5):
                    hi = max(min(lo + NC5, (t + 1) * P), lo + 2 * P)
                    for part in range(2):
                        last = nc.tensor.matmul(scores(n)[:, lo:hi], q2[:, h % 2, t * P:(t + 1) * P], k2[:, h % 2, part, lo:hi],
                                                start=(part == 0), stop=(part == 1))
                last.then_inc(sig("scores_full"), 1)

            def flip(n):
                h, t = items[n]
                pe.wait_ge(sig("probs_scaled"), n + 1)
                if n >= 1:
                    pe.wait_ge(sig("probs_t"), n)
                for k in range(t + 1):
                    last = nc.tensor.transpose(psum[:, 4 * NC5 + k * P:4 * NC5 + (k + 1) * P],
                                               probs[:, n % 3, k * P:(k + 1) * P], const["ident"][:])
                last.then_inc(sig("flipped"), 1)

            def mix(n):
                h, t = items[n]
                pe.wait_ge(sig("probs_t"), n + 1)
                if n >= 8 and t % 4 == 0:
                    pe.wait_ge(sig("o_t"), 2 * (h - 1) + t // 4 + 1)
                for k in range(t + 1):
                    last = nc.tensor.matmul(bank[6 + t // 4][0:HD, (t % 4) * P:(t % 4 + 1) * P], v_h[:, h % 2, k, :],
                                            probs_t[:, n % 2, k * P:(k + 1) * P], start=(k == 0), stop=(k == t))
                last.then_inc(sig("mixed"), 1)

            score(0)
            for n in range(len(items) + 2):
                if n + 1 < len(items):
                    score(n + 1)
                if 1 <= n <= len(items):
                    flip(n - 1)
                if n >= 2:
                    mix(n - 2)

        @block.scalar
        def _(act):
            def evacuate(n):
                cols = (items[n][1] + 1) * P
                act.wait_ge(sig("flipped"), n + 1)
                if n >= 2:
                    act.wait_ge(sig("mixed"), n - 1)
                nc.scalar.activation(probs_t[:, n % 2, 0:cols], psum[:, 4 * NC5:4 * NC5 + cols], ACT.Copy).then_inc(sig("probs_t"), 1)

            for n, (h, t) in enumerate(items):
                act.wait_ge(sig("neg_max"), n + 1)
                if n >= 3:
                    act.wait_ge(sig("flipped"), n - 2)
                cols = (t + 1) * P
                nc.scalar.activation(probs[:, n % 3, 0:cols], logits[:, n % 2, 0:cols], ACT.Exp,
                                     bias=neg_max[:, n:n + 1], accum_out=row_sum[:, n:n + 1]).then_inc(sig("probs"), 1)
                if n >= 1:
                    evacuate(n - 1)
            evacuate(len(items) - 1)

        @block.vector
        def _(dve):
            def scale(n):
                cols = (items[n][1] + 1) * P
                dve.wait_ge(sig("probs"), n + 1)
                nc.vector.reciprocal(row_sum[:, n:n + 1], row_sum[:, n:n + 1]).then_inc(sig("row_scale"), 1)
                dve.wait_ge(sig("row_scale"), n + 1)
                p = probs[:, n % 3, 0:cols]
                nc.vector.tensor_scalar(p, p, row_sum[:, n:n + 1], None, ALU.mult).then_inc(sig("probs_scaled"), 1)

            def finish(m):
                h, half = m // 2, m % 2
                dve.wait_ge(sig("mixed"), TT * h + 4 * (half + 1))
                if h >= 2 and half == 0:
                    dve.wait_ge(sig(f"o_t_out{h % 2}"), 16 * (h // 2))
                nc.vector.tensor_copy(o_t[:, h % 2, half * NC5:(half + 1) * NC5], bank[6 + half][0:HD, :]).then_inc(sig("o_t"), 1)

            dve.wait_ge(sig("att_const"), 2)
            for n, (h, t) in enumerate(items):
                cols = (t + 1) * P
                lg = logits[:, n % 2, :]
                dve.wait_ge(sig("scores_full"), n + 1)
                if t == 0:
                    head_here(dve, h)
                if n >= 2:
                    dve.wait_ge(sig("probs"), n - 1)
                nc.vector.scalar_tensor_tensor(out=lg[:, 0:cols], in0=scores(n)[:, 0:cols], scalar=HD ** -0.5,
                                               in1=gate_bias[:, h % 2, 0:cols], op0=ALU.mult, op1=ALU.add).then_inc(sig("scores_read"), 1)
                dve.wait_ge(sig("scores_read"), n + 1)
                nc.vector.tensor_tensor(lg[:, t * P:cols], lg[:, t * P:cols], causal[:], ALU.add).then_inc(sig("masked"), 1)
                dve.wait_ge(sig("masked"), n + 1)
                nc.vector.tensor_reduce(neg_max[:, n:n + 1], lg[:, 0:cols], AX.X, ALU.max, negate=True).then_inc(sig("neg_max"), 1)
                if n >= 1:
                    scale(n - 1)
                if n >= 6 and n % 4 == 2:
                    finish(n // 4 - 1)
            scale(len(items) - 1)
            finish(2 * H - 1)


def recur(nc, sig, bank, const, keep, ins, dram):
    ident = const["ident"]
    LEVELS = 5
    PAIRS = H // 2
    with ExitStack() as ctx:
        sb = lambda name, shape: ctx.enter_context(nc.sbuf_tensor(name, shape, F32))
        cur = sb("rw_cur", [P, 2, SHIFT])
        prev = sb("rw_prev", [P, SHIFT])
        mu_bc = sb("mu_bc", [P, SHIFT])
        names = ["rwkv_w0", "rwkv_a0", "rwkv_k_k", "rwkv_k_a", "rwkv_r_k", "ln_x_g", "ln_x_b"]
        rows = sb("rw_rows", [P, len(names), W])
        w0, a0, k_k, k_a, r_k, ln_g, ln_b = (rows[:, i, :] for i in range(len(names)))
        lora_w = sb("lora_w", [P, 2, W])
        gate_w = sb("gate_w", [P, W])
        in_chunk = sb("in_chunk", [P, 2])
        tri = sb("tri", [P, 2, P])
        off_t = sb("off_t", [P, 6, P])
        lora = sb("lora", [P, 2 * P])
        lora_t = sb("lora_t", [P, 2 * P])
        gate = sb("rw_gate", [P, 2, W])
        sw = sb("sw", [P, W])
        aa = sb("aa", [P, W])
        p_in = sb("p_in", [P, W])
        p_inv = sb("p_inv", [P, W])
        p_ex = sb("p_ex", [P, W])
        p_end = sb("p_end", [P, 2, PAIRS, 2])
        kk = sb("kk", [P, W])
        kp = sb("kp", [P, W])
        tmp = sb("rw_tmp", [P, W])
        norm_k = sb("norm_k", [P, H])
        norm_y = sb("norm_y", [P, H])
        bonus = sb("bonus", [P, H])
        bonus_v = sb("bonus_v", [P, 2, W])
        v_m = sb("v_m", [P, 2, 2, W])
        tm = sb("tm", [P, 2, 4, W])
        fm_ar = sb("fm_ar", [P, 2, PAIRS, 2, P])
        fm_bk = sb("fm_bk", [P, H, 2, P])
        gram_a = sb("gram_a", [P, H, 2, P])
        gram_r = sb("gram_r", [P, 2, H, 2, P])
        inv = sb("inv", [P, H, P])
        inv_t = sb("inv_t", [P, 2, H, P])
        a_off = sb("a_off", [P, 2, H, P])
        grow = sb("grow", [P, H, P])
        xv = keep["mod_bc"][:, 4, :].rearrange("p (b n) -> p b n", b=2)
        w_t = sb("w_t", [P, PAIRS, P])
        sa = sb("sa", [P, 2, W])
        state = sb("state", [P, 2, PAIRS, P])
        y = sb("rw_y", [P, 2, W])
        block = ctx.enter_context(nc.Block("recur"))

        def heads(ap, n=HD):
            return ap.rearrange("p (h d) -> p h d", d=n)

        def head(h):
            return slice(h * HD, (h + 1) * HD)

        def pair(j):
            return slice(j * P, (j + 1) * P)

        def tokens(ch):
            return slice(ch * CHUNK, (ch + 1) * CHUNK)

        def at(t, *pieces):
            if 0 <= t < TT:
                for piece in pieces:
                    piece(t)

        @block.sync
        def _(sp):
            def load(t):
                if t >= 2:
                    sp.wait_ge(sig("bonus_v"), t - 1)
                    sp.wait_ge(sig("v_m"), t - 1)
                sp.dma_start(cur[:, t % 2, :], dram["p_rwkv"][1 + t * P:1 + (t + 1) * P, :]).then_inc(sig(f"cur_in{t % 2}"), 16)
                if t >= 1:
                    sp.wait_ge(sig("shifted"), t)
                sp.dma_start(prev[:], dram["p_rwkv"][t * P:(t + 1) * P, :]).then_inc(sig("prev_in"), 16)

            def store(t):
                sp.wait_ge(sig("tile_done"), t + 1)
                sp.dma_start(dram["o_rwkv"][t * P:(t + 1) * P, :], y[:, t % 2, :]).then_inc(sig(f"o_out{t % 2}"), 16)

            load(0)
            for i, n in enumerate(names):
                src = ins[n] if n != "rwkv_r_k" else ins[n].rearrange("l h d -> l (h d)")
                sp.dma_start(rows[:, i, :], src.partition_broadcast(P).rearrange("p a n -> p (a n)")).then_inc(sig("rows_in"), 16)
            sp.dma_start(lora_w[0:LORA, 0, :], ins["rwkv_w2"][0]).then_inc(sig("rows_in"), 16)
            sp.dma_start(lora_w[LORA:2 * LORA, 1, :], ins["rwkv_a2"][0]).then_inc(sig("rows_in"), 16)
            sp.dma_start(gate_w[:], ins["rwkv_g2"][0]).then_inc(sig("rows_in"), 16)
            load(1)
            for t in range(TT + 1):
                at(t + 2, load)
                at(t - 1, store)
            for b in range(2):
                sp.wait_ge(sig(f"o_out{b}"), 16 * TT // 2)

        @block.gpsimd
        def _(pool):
            link = Link(pool, sig("pool_link_r"))

            def select(ap, pattern, cm, base, op, fill=0.0):
                link(nc.gpsimd.affine_select(out=ap, in_=ap, compare_op=op, fill=fill, base=base,
                                             pattern=pattern, channel_multiplier=cm))

            def shift(t):
                if t == 0:
                    pool.wait_ge(sig("mu_in"), 16)
                pool.wait_ge(sig(f"cur_in{t % 2}"), 16 * (t // 2 + 1))
                pool.wait_ge(sig("prev_in"), 16 * (t + 1))
                c = cur[:, t % 2, :]
                link(nc.gpsimd.tensor_tensor(prev[:], prev[:], c, ALU.subtract))
                link(nc.gpsimd.tensor_tensor(prev[:], prev[:], mu_bc[:], ALU.mult))
                nc.gpsimd.tensor_tensor(c, c, prev[:], ALU.add).then_inc(sig("shifted"), 1)

            def part_v(t):
                pool.wait_ge(sig("shifted"), t + 1)
                if t >= 2:
                    pool.wait_ge(sig("y_sum"), t - 1)
                c = cur[:, t % 2, 2 * W:3 * W]
                link(nc.gpsimd.tensor_copy(v_m[tokens(0), t % 2, 0, :], c[tokens(0), :]))
                nc.gpsimd.tensor_copy(v_m[tokens(1), t % 2, 1, :], c[tokens(1), :]).then_inc(sig("v_m"), 1)
                pool.wait_ge(sig("v_m"), t + 1)

            def key_norm(t):
                pool.wait_ge(sig("kk_ss"), t + 1)
                nc.gpsimd.tensor_tensor(norm_k[:], norm_k[:], const["neghalf"][:], ALU.pow).then_inc(sig("kk_rn"), 1)

            def y_norm(t):
                pool.wait_ge(sig("y_var"), t + 1)
                nc.gpsimd.tensor_tensor(norm_y[:], norm_y[:], const["neghalf"][:], ALU.pow).then_inc(sig("y_rstd"), 1)

            def off(i):
                def piece(t):
                    n = LEVELS * t + i
                    for g in range(2):
                        if i == 0:
                            pool.wait_ge(sig("gram"), 2 * (H * t + 4 * (g + 1)))
                        if n >= 2:
                            pool.wait_ge(sig("grow_full"), 2 * (n - 2) + g + 1)
                        hs = slice(4 * g, 4 * g + 4)
                        nc.gpsimd.tensor_tensor(a_off[:, n % 2, hs], gram_a[:, hs, 0, :],
                                                off_t[:, i + 1, :].unsqueeze(1).to_broadcast([P, 4, P]), ALU.mult).then_inc(sig("a_off"), 1)
                return piece

            pool.dma_start(mu_bc[:], ins["shift_mu"].partition_broadcast(P).rearrange("p a n -> p (a n)")).then_inc(sig("mu_in"), 16)
            nc.gpsimd.memset(lora_w[LORA:2 * LORA, 0, :], 0.0).then_inc(sig("lora_zero"), 1)
            nc.gpsimd.memset(lora_w[0:LORA, 1, :], 0.0).then_inc(sig("lora_zero"), 1)
            pool.wait_ge(sig("lora_zero"), 2)
            shift(0)
            pool.wait_ge(sig("shifted"), 1)
            for m in (tri, off_t, in_chunk):
                link(nc.gpsimd.memset(m[:], 1.0))
            for m in (state, v_m, sa, fm_bk):
                link(nc.gpsimd.memset(m[:], 0.0))
            select(in_chunk[:], [[-CHUNK, 2]], 1, 0, ALU.is_ge)
            select(in_chunk[:], [[CHUNK, 2]], -1, CHUNK - 1, ALU.is_ge)
            for i in range(2):
                m = tri[:, i, :].rearrange("p (c t) -> p c t", c=2)
                select(m, [[-CHUNK, 2], [0, CHUNK]], 1, 0, ALU.is_ge)
                select(m, [[CHUNK, 2], [0, CHUNK]], -1, CHUNK - 1, ALU.is_ge)
                select(m, [[CHUNK, 2], [1, CHUNK]], -1, 0, ALU.is_ge if i else ALU.is_gt)
            for i in range(LEVELS + 1):
                n = 1 << i
                m = off_t[:, i, :].rearrange("p (b u v) -> p b u v", u=2, v=n)
                select(m, [[0, P // (2 * n)], [1, 2], [0, n]], 0, -1, ALU.is_ge)
                select(m, [[-2 * n, P // (2 * n)], [0, 2], [0, n]], 1, 0, ALU.is_ge)
                select(m, [[2 * n, P // (2 * n)], [0, 2], [0, n]], -1, n - 1, ALU.is_ge)
            nc.gpsimd.nop().then_inc(sig("masks"), 1)
            for t in range(-1, TT + 1):
                at(t, off(1))
                at(t + 1, key_norm)
                at(t, off(2), off(3), off(4))
                at(t - 1, y_norm)
                at(t + 1, part_v)
                at(t + 2, shift)
                at(t + 1, off(0))

        @block.scalar
        def _(act):
            def copy(out, ps, name):
                nc.scalar.activation(out, ps, ACT.Copy).then_inc(sig(name), 1)

            def lora_in(t):
                c = cur[:, t % 2, :]
                act.wait_ge(sig("shifted"), t + 1)
                nc.scalar.activation(lora[:, 0:LORA], c[:, 3 * W:3 * W + LORA], ACT.Tanh).then_inc(sig("lora"), 1)
                copy(lora[:, LORA:2 * LORA], c[:, 3 * W + LORA:3 * W + 2 * LORA], "lora")
                nc.scalar.activation(lora[:, P:2 * P], c[:, 3 * W + 2 * LORA:SHIFT], ACT.Tanh, scale=0.5).then_inc(sig("lora"), 1)

            def lora_flipped(t):
                act.wait_ge(sig("lora_flipped"), t + 1)
                copy(lora_t[:], bank[4][:, 0:2 * P], "lora_t")

            def decay_tanh(t):
                act.wait_ge(sig("z_biased"), t + 1)
                nc.scalar.activation(sw[:], sw[:], ACT.Tanh, scale=0.5).then_inc(sig("z_tanh"), 1)

            def rate_tanh(t):
                act.wait_ge(sig("a_biased"), t + 1)
                nc.scalar.activation(aa[:], aa[:], ACT.Tanh, scale=0.5).then_inc(sig("a_tanh"), 1)

            def decays(t):
                act.wait_ge(sig("sum_in_full"), t + 1)
                nc.scalar.activation(p_in[:], bank[4], ACT.Exp, scale=-EXPM05).then_inc(sig("p_in"), 1)
                nc.scalar.activation(p_inv[:], bank[4], ACT.Exp, scale=EXPM05).then_inc(sig("p_inv"), 1)
                act.wait_ge(sig("sum_ex_full"), t + 1)
                nc.scalar.activation(p_ex[:], bank[5], ACT.Exp, scale=-EXPM05).then_inc(sig("p_ex"), 1)

            def chunk_decay(t):
                act.wait_ge(sig("sum_end_full"), t + 1)
                if t >= 2:
                    act.wait_ge(sig("state"), 2 * (t - 1))
                nc.scalar.activation(p_end[:, t % 2].rearrange("p j c -> p (j c)"), bank[4][:, 0:2 * PAIRS], ACT.Exp,
                                     scale=-EXPM05).then_inc(sig("p_end"), 1)

            def flipped(j):
                def piece(t):
                    ps = bank[4 + j % 2]
                    act.wait_ge(sig("fm_full"), PAIRS * t + j + 1)
                    copy(fm_ar[:, t % 2, j].rearrange("p a t -> p (a t)"), ps[:, 0:2 * P], "fm")
                    for h in range(2):
                        rows_h = slice(h * HD, (h + 1) * HD)
                        copy(fm_bk[rows_h, 2 * j + h].rearrange("p a t -> p (a t)"), ps[rows_h, 2 * P:4 * P], "fm")
                return piece

            def first(g):
                def piece(t):
                    act.wait_ge(sig("first_full"), 2 * t + g + 1)
                    copy(inv[:, 4 * g:4 * g + 4].rearrange("p h s -> p (h s)"), bank[4 + g], "first")
                return piece

            def grown(i, g):
                def piece(t):
                    hs = slice(4 * g, 4 * g + 4)
                    act.wait_ge(sig("inv_full"), 2 * (LEVELS * t + i) + g + 1)
                    if i < LEVELS - 1:
                        copy(inv[:, hs].rearrange("p h s -> p (h s)"), bank[2], "inv")
                    copy(inv_t[:, t % 2, hs].rearrange("p h s -> p (h s)"), bank[3], "inv_t")
                return piece

            def keys_v(t):
                act.wait_ge(sig("xv_full"), t + 1)
                copy(xv[:, t % 2, :], bank[5], "xv")

            def gates(t):
                act.wait_ge(sig("g_full"), t + 1)
                if t >= 2:
                    act.wait_ge(sig("tile_done"), t - 1)
                copy(gate[:, t % 2, :], bank[4], "gate")

            def read_w(t):
                act.wait_ge(sig("w_full"), t + 1)
                copy(w_t[:].rearrange("p j t -> p (j t)"), bank[7], "w_t")

            def read_sa(ch):
                def piece(t):
                    act.wait_ge(sig("sa_full"), 2 * t + ch + 1)
                    copy(sa[tokens(ch), ch, :], bank[7][tokens(ch), :], "sa")
                return piece

            act.wait_ge(sig("masks"), 1)
            for t in range(-1, TT + 1):
                at(t + 1, lora_in)
                at(t - 1, read_w)
                at(t, first(1))
                at(t + 1, lora_flipped)
                at(t, grown(0, 0))
                at(t - 1, read_sa(0))
                at(t + 1, decay_tanh)
                at(t, grown(0, 1))
                at(t + 1, rate_tanh)
                at(t, grown(1, 0))
                at(t + 1, decays)
                at(t, grown(1, 1))
                at(t - 1, read_sa(1))
                at(t, grown(2, 0))
                at(t + 1, chunk_decay)
                at(t, grown(2, 1))
                at(t + 1, flipped(0), flipped(1))
                at(t, grown(3, 0))
                at(t + 1, flipped(2), flipped(3))
                at(t, grown(3, 1), grown(4, 0), grown(4, 1))
                at(t + 1, first(0), keys_v, gates)

        @block.tensor
        def _(pe):
            mm = nc.tensor.matmul

            def flip_lora(t):
                pe.wait_ge(sig("lora"), 3 * (t + 1))
                pe.wait_ge(sig("lora_sig"), t + 1)
                if t >= 1:
                    pe.wait_ge(sig("gate"), t)
                for i in range(2):
                    last = nc.tensor.transpose(bank[4][:, i * P:(i + 1) * P], lora[:, i * P:(i + 1) * P], ident[:])
                last.then_inc(sig("lora_flipped"), 1)

            def decay_logit(t):
                if t >= 1:
                    pe.wait_ge(sig("first"), 2 * t)
                pe.wait_ge(sig("lora_t"), t + 1)
                mm(bank[5], lora_t[:, 0:P], lora_w[:, 0, :], start=True, stop=True).then_inc(sig("z_full"), 1)

            def rate_logit(t):
                mm(bank[4], lora_t[:, 0:P], lora_w[:, 1, :], start=True, stop=True).then_inc(sig("a_full"), 1)

            def decay_sums(t):
                pe.wait_ge(sig("sw"), t + 1)
                pe.wait_ge(sig("a_biased"), t + 1)
                mm(bank[4], tri[:, 1, :], sw[:], start=True, stop=True).then_inc(sig("sum_in_full"), 1)
                mm(bank[5], tri[:, 0, :], sw[:], start=True, stop=True).then_inc(sig("sum_ex_full"), 1)

            def chunk_sums(t):
                pe.wait_ge(sig("p_in"), t + 1)
                pe.wait_ge(sig("p_inv"), t + 1)
                for j in range(PAIRS):
                    last = mm(bank[4][:, 2 * j:2 * j + 2], sw[:, pair(j)], in_chunk[:], start=True, stop=True)
                last.then_inc(sig("sum_end_full"), 1)

            def flip(j):
                def piece(t):
                    if j == 0:
                        pe.wait_ge(sig("tm"), 4 * (t + 1))
                        pe.wait_ge(sig("p_end"), t + 1)
                        pe.wait_ge(sig("p_ex"), t + 1)
                    if j >= 2:
                        pe.wait_ge(sig("fm"), 3 * (PAIRS * t + j - 1))
                    for i in range(4):
                        last = nc.tensor.transpose(bank[4 + j % 2][:, i * P:(i + 1) * P], tm[:, t % 2, i, pair(j)], ident[:])
                    last.then_inc(sig("fm_full"), 1)
                return piece

            def products(h):
                def piece(t):
                    if h == 0:
                        pe.wait_ge(sig("fm"), 3 * (PAIRS * t + 3))
                    elif h == 1:
                        pe.wait_ge(sig("fm"), 3 * PAIRS * (t + 1))
                    else:
                        pe.wait_ge(sig("gram"), 2 * (H * t + h - 1))
                    ar = fm_ar[:, t % 2, h // 2].rearrange("p a t -> p (a t)")
                    ps = bank[4 + h % 2]
                    mm(ps[:, 0:2 * P], fm_bk[:, h, 0, :], ar, start=True, stop=True)
                    mm(ps[:, 2 * P:4 * P], fm_bk[:, h, 1, :], ar, start=True, stop=True).then_inc(sig("gram_full"), 1)
                return piece

            def first(g):
                def piece(t):
                    pe.wait_ge(sig("inv_first"), 2 * t + g + 1)
                    if g == 0:
                        pe.wait_ge(sig("gram"), 2 * (H * (t + 1) - 1))
                    else:
                        pe.wait_ge(sig("xv"), t + 1)
                    for h in range(4):
                        last = nc.tensor.transpose(bank[4 + g][:, h * P:(h + 1) * P], inv_t[:, t % 2, 4 * g + h, :], ident[:])
                    last.then_inc(sig("first_full"), 1)
                return piece

            def keys_v(t):
                pe.wait_ge(sig("gram"), 2 * H * (t + 1))
                pe.wait_ge(sig("v_m"), t + 1)
                for ch in range(2):
                    for h in range(H):
                        last = mm(bank[5][tokens(ch), head(h)], gram_a[:, h, 1, tokens(ch)], v_m[:, t % 2, ch, head(h)],
                                  start=True, stop=True)
                last.then_inc(sig("xv_full"), 1)

            def gates(t):
                pe.wait_ge(sig("first"), 2 * t + 1)
                mm(bank[4], lora_t[:, P:2 * P], gate_w[:], start=True, stop=True).then_inc(sig("g_full"), 1)

            def offset(i, g):
                def piece(t):
                    n = LEVELS * t + i
                    if i == 0:
                        pe.wait_ge(sig("first"), 2 * t + g + 1)
                    else:
                        pe.wait_ge(sig("inv"), 2 * ((LEVELS - 1) * t + i - 1) + g + 1)
                    pe.wait_ge(sig("a_off"), 2 * n + g + 1)
                    if n >= 1:
                        pe.wait_ge(sig("grow"), 2 * (n - 1) + g + 1)
                    for h in range(4):
                        last = mm(bank[g][:, h * P:(h + 1) * P], a_off[:, n % 2, 4 * g + h, :], inv[:, 4 * g + h, :],
                                  start=True, stop=True)
                    last.then_inc(sig("grow_full"), 1)
                return piece

            def doubled(i, g):
                def piece(t):
                    n = 2 * (LEVELS * t + i) + g
                    pe.wait_ge(sig("grow"), n + 1)
                    if n >= 1:
                        pe.wait_ge(sig("inv_t"), n)
                        before = (LEVELS - 1) * (n // (2 * LEVELS)) * 2 + min(n % (2 * LEVELS), 2 * (LEVELS - 1))
                        pe.wait_ge(sig("inv"), before)
                    for h in range(4):
                        cols, it = slice(h * P, (h + 1) * P), inv_t[:, t % 2, 4 * g + h, :]
                        if i < LEVELS - 1:
                            mm(bank[2][:, cols], it, grow[:, 4 * g + h, :], start=True, stop=True)
                        last = mm(bank[3][:, cols], grow[:, 4 * g + h, :], it, start=True, stop=True)
                    last.then_inc(sig("inv_full"), 1)
                return piece

            def w_rows(t):
                pe.wait_ge(sig("inv_t"), 2 * LEVELS * (t + 1))
                if t >= 1:
                    pe.wait_ge(sig("state_read"), 2 * t)
                for h in range(H):
                    rows_h = slice(h % 2 * HD, (h % 2 + 1) * HD)
                    last = mm(bank[7][rows_h, pair(h // 2)], tm[:, t % 2, 0, head(h)], inv_t[:, t % 2, h, :], start=True, stop=True)
                last.then_inc(sig("w_full"), 1)

            def scan(ch):
                def piece(t):
                    n, tok = 2 * t + ch, tokens(ch)
                    pe.wait_ge(sig("w_t"), t + 1)
                    if n >= 1:
                        pe.wait_ge(sig("state_read"), n)
                    for h in range(H):
                        mm(bank[7][tok, head(h)], inv_t[:, t % 2, h, tok], xv[:, t % 2, head(h)], start=(h == 0), stop=False)
                    if n >= 1:
                        pe.wait_ge(sig("state"), n)
                    for j in range(PAIRS):
                        last = mm(bank[7][tok, pair(j)], w_t[:, j, tok], state[:, ch, j, :], start=False, stop=(j == PAIRS - 1))
                    last.then_inc(sig("sa_full"), 1)
                    if t >= 1:
                        pe.wait_ge(sig("y_sum"), t)
                    for j in range(PAIRS):
                        mm(bank[6][tok, pair(j)], fm_ar[:, t % 2, j, 1, tok], state[:, ch, j, :], start=(j == 0), stop=False)
                return piece

            def advance(ch):
                def piece(t):
                    pe.wait_ge(sig("sa"), 2 * t + ch + 1)
                    for j in range(PAIRS):
                        mm(bank[7][:, pair(j)], tm[:, t % 2, 3, pair(j)], v_m[:, t % 2, ch, pair(j)], start=True, stop=False)
                        last = mm(bank[7][:, pair(j)], tm[:, t % 2, 2, pair(j)], sa[:, ch, pair(j)], start=False, stop=True)
                    last.then_inc(sig("state_full"), 1)
                return piece

            def out(ch):
                def piece(t):
                    tok = tokens(ch)
                    for h in range(H):
                        ps = bank[6][tok, head(h)]
                        mm(ps, gram_r[:, t % 2, h, 1, tok], v_m[:, t % 2, ch, head(h)], start=False, stop=False)
                        last = mm(ps, gram_r[:, t % 2, h, 0, tok], sa[:, ch, head(h)], start=False, stop=(h == H - 1))
                    last.then_inc(sig("y_full"), 1)
                return piece

            pe.wait_ge(sig("masks"), 1)
            pe.wait_ge(sig("lora_zero"), 2)
            pe.wait_ge(sig("rows_in"), 16 * 10)
            for t in range(-1, TT + 1):
                at(t, offset(0, 0))
                at(t - 1, w_rows)
                at(t, first(1), offset(0, 1))
                at(t + 1, flip_lora)
                at(t, doubled(0, 0))
                at(t - 1, scan(0))
                at(t + 1, decay_logit)
                at(t, doubled(0, 1))
                at(t + 1, rate_logit)
                at(t, offset(1, 0), offset(1, 1))
                at(t - 1, advance(0))
                at(t, doubled(1, 0))
                at(t + 1, decay_sums)
                at(t, doubled(1, 1))
                at(t - 1, scan(1))
                at(t, offset(2, 0), offset(2, 1))
                at(t - 1, advance(1))
                at(t, doubled(2, 0))
                at(t - 1, out(0))
                at(t + 1, chunk_sums)
                at(t, doubled(2, 1))
                at(t - 1, out(1))
                at(t, offset(3, 0), offset(3, 1))
                at(t + 1, flip(0), flip(1))
                at(t, doubled(3, 0))
                at(t + 1, flip(2), flip(3))
                at(t, doubled(3, 1))
                at(t + 1, products(0), products(1))
                at(t, offset(4, 0), offset(4, 1))
                at(t + 1, products(2), products(3))
                at(t, doubled(4, 0))
                at(t + 1, products(4), products(5))
                at(t, doubled(4, 1))
                at(t + 1, products(6), products(7), first(0), keys_v, gates)

        @block.vector
        def _(dve):
            link = Link(dve, sig("dve_link_r"))
            tt, stt, ts = nc.vector.tensor_tensor, nc.vector.scalar_tensor_tensor, nc.vector.tensor_scalar

            def mark(ins, name, count):
                ins.then_inc(sig(name), 1)
                dve.wait_ge(sig(name), count)

            def rkv(t):
                return (cur[:, t % 2, i * W:(i + 1) * W] for i in range(3))

            def gate_half(t):
                dve.wait_ge(sig("lora"), 3 * (t + 1))
                ts(lora[:, P:2 * P], lora[:, P:2 * P], 0.5, 0.5, ALU.mult, ALU.add).then_inc(sig("lora_sig"), 1)

            def unit_keys(t):
                r, k, v = rkv(t)
                link(tt(kk[:], k, k_k, ALU.mult))
                link(tt(tmp[:], kk[:], kk[:], ALU.mult))
                link(nc.vector.tensor_reduce(norm_k[:], heads(tmp[:]), AX.X, ALU.add))
                ts(norm_k[:], norm_k[:], 1e-24, None, ALU.max).then_inc(sig("kk_ss"), 1)

            def bias(t):
                dve.wait_ge(sig("z_full"), t + 1)
                tt(sw[:], bank[5], w0, ALU.add).then_inc(sig("z_biased"), 1)
                dve.wait_ge(sig("a_full"), t + 1)
                tt(aa[:], bank[4], a0, ALU.add).then_inc(sig("a_biased"), 1)
                dve.wait_ge(sig("kk_rn"), t + 1)
                link(tt(heads(kk[:]), heads(kk[:]), norm_k[:].unsqueeze(2).to_broadcast([P, H, HD]), ALU.mult))
                dve.wait_ge(sig("z_tanh"), t + 1)
                mark(ts(sw[:], sw[:], 0.5, 0.5, ALU.mult, ALU.add), "sw", t + 1)

            def rates(t):
                r, k, v = rkv(t)
                dve.wait_ge(sig("a_tanh"), t + 1)
                link(ts(aa[:], aa[:], 0.5, 0.5, ALU.mult, ALU.add))
                link(stt(out=kp[:], in0=aa[:], scalar=1.0, in1=k_a, op0=ALU.subtract, op1=ALU.mult))
                link(stt(out=kp[:], in0=kp[:], scalar=1.0, in1=k, op0=ALU.add, op1=ALU.mult))
                link(tt(aa[:], aa[:], kk[:], ALU.mult))

            def key_vectors(t):
                r, k, v = rkv(t)
                b = t % 2
                dve.wait_ge(sig("p_ex"), t + 1)
                stt(out=tm[:, b, 0, :], in0=kk[:], scalar=-1.0, in1=p_ex[:], op0=ALU.mult, op1=ALU.mult).then_inc(sig("tm"), 1)
                tt(tm[:, b, 1, :], r, p_in[:], ALU.mult).then_inc(sig("tm"), 1)
                tt(tm[:, b, 2, :], aa[:], p_inv[:], ALU.mult).then_inc(sig("tm"), 1)
                tt(tm[:, b, 3, :], kp[:], p_inv[:], ALU.mult).then_inc(sig("tm"), 1)

            def bonuses(t):
                r, k, v = rkv(t)
                link(tt(tmp[:], r, kp[:], ALU.mult))
                link(tt(tmp[:], tmp[:], r_k, ALU.mult))
                link(nc.vector.tensor_reduce(bonus[:], heads(tmp[:]), AX.X, ALU.add))

            def bonus_values(t):
                r, k, v = rkv(t)
                mark(tt(heads(bonus_v[:, t % 2, :]), heads(v), bonus[:].unsqueeze(2).to_broadcast([P, H, HD]), ALU.mult), "bonus_v", t + 1)

            def masked(*hs):
                def piece(t):
                    for h in hs:
                        ps = bank[4 + h % 2].rearrange("p (k a t) -> p k a t", k=2, a=2)
                        dve.wait_ge(sig("gram_full"), H * t + h + 1)
                        if h == 0 and t >= 1:
                            dve.wait_ge(sig("a_off"), 2 * LEVELS * t)
                        for a, dst in enumerate((gram_a[:, h], gram_r[:, t % 2, h])):
                            tt(dst, ps[:, :, a, :], tri[:, a, :].unsqueeze(1).to_broadcast([P, 2, P]), ALU.mult).then_inc(sig("gram"), 1)
                return piece

            ident_h = ident[:].unsqueeze(1).to_broadcast([P, 4, P])

            def first(g):
                def piece(t):
                    hs = slice(4 * g, 4 * g + 4)
                    dve.wait_ge(sig("gram"), 2 * (H * t + 4 * (g + 1)))
                    link(tt(inv_t[:, t % 2, hs], gram_a[:, hs, 0, :], off_t[:, 0, :].unsqueeze(1).to_broadcast([P, 4, P]), ALU.mult))
                    mark(tt(inv_t[:, t % 2, hs], inv_t[:, t % 2, hs], ident_h, ALU.add), "inv_first", 2 * t + g + 1)
                return piece

            def grown(i):
                def piece(t):
                    for g in range(2):
                        dve.wait_ge(sig("grow_full"), 2 * (LEVELS * t + i) + g + 1)
                        tt(grow[:, 4 * g:4 * g + 4], heads(bank[g], P), ident_h, ALU.add).then_inc(sig("grow"), 1)
                return piece

            def advance(ch):
                def piece(t):
                    n = 2 * t + ch
                    dve.wait_ge(sig("state_full"), n + 1)
                    nxt = state[:, 1 - ch]
                    halves = [(slice(h * HD, (h + 1) * HD), slice(h * HD, (h + 1) * HD)) for h in range(2)]
                    for ks, vs in halves:
                        last = tt(nxt[ks, :, vs], heads(bank[7], P)[ks, :, vs], state[ks, ch, :, vs], ALU.add)
                        if ks.start == 0:
                            link(last)
                    mark(last, "state_read", n + 1)
                    for ks, vs in halves:
                        last = tt(nxt[ks, :, vs], nxt[ks, :, vs], p_end[ks, t % 2, :, ch:ch + 1].to_broadcast([HD, PAIRS, HD]), ALU.mult)
                        if ks.start == 0:
                            link(last)
                    mark(last, "state", n + 1)
                return piece

            def y_moments(t):
                yt = y[:, t % 2, :]
                dve.wait_ge(sig("y_full"), 2 * (t + 1))
                if t >= 2:
                    dve.wait_ge(sig(f"o_out{t % 2}"), 16 * (t // 2))
                mark(nc.vector.tensor_copy(yt, bank[6]), "y_sum", t + 1)
                link(nc.vector.tensor_reduce(norm_y[:], heads(yt), AX.X, ALU.add))
                link(ts(norm_y[:], norm_y[:], 1.0 / HD, None, ALU.mult))
                link(tt(heads(yt), heads(yt), norm_y[:].unsqueeze(2).to_broadcast([P, H, HD]), ALU.subtract))
                link(tt(tmp[:], yt, yt, ALU.mult))
                link(nc.vector.tensor_reduce(norm_y[:], heads(tmp[:]), AX.X, ALU.add))
                ts(norm_y[:], norm_y[:], 1.0 / HD, LN_EPS, ALU.mult, ALU.add).then_inc(sig("y_var"), 1)

            def y_finish(t):
                yt = y[:, t % 2, :]
                dve.wait_ge(sig("y_rstd"), t + 1)
                link(tt(heads(yt), heads(yt), norm_y[:].unsqueeze(2).to_broadcast([P, H, HD]), ALU.mult))
                link(tt(yt, yt, ln_g, ALU.mult))
                link(tt(yt, yt, ln_b, ALU.add))
                link(tt(yt, yt, bonus_v[:, t % 2, :], ALU.add))
                dve.wait_ge(sig("gate"), t + 1)
                mark(tt(yt, yt, gate[:, t % 2, :], ALU.mult), "tile_done", t + 1)

            dve.wait_ge(sig("masks"), 1)
            dve.wait_ge(sig("rows_in"), 16 * 10)
            for t in range(-1, TT + 1):
                at(t + 1, gate_half)
                at(t, grown(0))
                at(t + 1, unit_keys, bias)
                at(t, grown(1))
                at(t - 1, advance(0))
                at(t + 1, rates)
                at(t, grown(2))
                at(t - 1, advance(1))
                at(t + 1, key_vectors)
                at(t, grown(3))
                at(t - 1, y_moments)
                at(t + 1, bonuses)
                at(t - 1, y_finish)
                at(t + 1, bonus_values, masked(0, 1))
                at(t, grown(4))
                at(t + 1, masked(2, 3), first(0), masked(4, 5, 6, 7), first(1))


def merge(nc, sig, bank, const, keep, ins, dram):
    ident, psum = const["ident"], const["psum"]
    mod_bc, logits = keep["mod_bc"], keep["logits"]
    GE = G + E
    with ExitStack() as ctx:
        sb = lambda name, shape: ctx.enter_context(nc.sbuf_tensor(name, shape, F32))
        w_fox = sb("w_fox", [P, W // P, D])
        w_rwkv = sb("w_rwkv", [P, W // P, D])
        w_o = sb("w_o", [P, KT, D])
        w_route = sb("w_route", [P, KT, GE])
        b_route = sb("b_route", [P, GE])
        gates = sb("mg_gates", [P, 2, 2 * D])
        x_in = sb("mg_x", [P, 2, D])
        o_fox_t = sb("mg_o_fox_t", [P, W // P, S])
        o_rwkv = sb("mg_o_rwkv", [P, TT, W])
        o_t = sb("mg_o_t", [P, W // P, P])
        mixed = sb("mg_mixed", [P, 2, D])
        mixed_t = sb("mg_mixed_t", [P, KT, P])
        part = sb("mg_part", [P, D])
        x_mid = sb("mg_x_mid", [P, 2, D])
        h_mid = sb("mg_h_mid", [P, 2, D])
        h_t = sb("mg_h_t", [P, KT, P])
        ms = sb("mg_ms", [P, TT])
        block = ctx.enter_context(nc.Block("merge"))

        @block.sync
        def _(sp):
            sp.dma_start(o_rwkv[:], dram["o_rwkv"].rearrange("(t p) n -> p t n", p=P)).then_inc(sig("o_rwkv_in"), 16)
            sp.dma_start(w_fox[:], ins["w_out_fox"][0].rearrange("(k p) n -> p k n", p=P)).then_inc(sig("mg_w_in"), 16)
            sp.dma_start(w_rwkv[:], ins["w_out_rwkv"][0].rearrange("(k p) n -> p k n", p=P)).then_inc(sig("mg_w_in"), 16)
            sp.dma_start(o_fox_t[:], dram["o_fox_t"].rearrange("(k p) n -> p k n", p=P)).then_inc(sig("mg_w_in"), 16)
            for t in range(TT):
                if t >= 2:
                    sp.wait_ge(sig("x_mid"), t - 1)
                sp.dma_start(gates[:, t % 2, :], dram["gates"][t * P:(t + 1) * P, :]).then_inc(sig(f"gates_in{t % 2}"), 16)
                sp.dma_start(x_in[:, t % 2, :], ins["x"][0, t * P:(t + 1) * P, :]).then_inc(sig(f"mg_x_in{t % 2}"), 16)
                if t == 0:
                    sp.dma_start(w_o[:], ins["w_o"][0].rearrange("(k p) n -> p k n", p=P)).then_inc(sig("w_o_in"), 16)
                    sp.dma_start(w_route[:, :, 0:G], ins["router_group_w"][0].rearrange("(k p) n -> p k n", p=P)).then_inc(sig("w_route_in"), 16)
                    sp.dma_start(w_route[:, :, G:GE], ins["router_expert_w"][0].rearrange("(k p) n -> p k n", p=P)).then_inc(sig("w_route_in"), 16)
                    sp.dma_start(b_route[:, 0:G], ins["router_group_b"].partition_broadcast(P).rearrange("p a n -> p (a n)")).then_inc(sig("w_route_in"), 16)
                    sp.dma_start(b_route[:, G:GE], ins["router_expert_b"].partition_broadcast(P).rearrange("p a n -> p (a n)")).then_inc(sig("w_route_in"), 16)

        @block.gpsimd
        def _(pool):
            for t in range(TT):
                pool.wait_ge(sig("mg_ms"), t + 1)
                nc.gpsimd.tensor_tensor(ms[:, t:t + 1], ms[:, t:t + 1], const["neghalf"][:, 0:1], ALU.pow).then_inc(sig("mg_rstd"), 1)
                pool.dma_start(dram["x_mid"][t * P:(t + 1) * P, :], x_mid[:, t % 2, :]).then_inc(sig(f"x_mid_out{t % 2}"), 16)
                pool.wait_ge(sig("h_mid"), t + 1)
                pool.dma_start(dram["h_mid"][t * P:(t + 1) * P, :], h_mid[:, t % 2, :]).then_inc(sig(f"h_mid_out{t % 2}"), 16)
            for b in range(2):
                pool.wait_ge(sig(f"x_mid_out{b}"), 16 * TT // 2)
                pool.wait_ge(sig(f"h_mid_out{b}"), 16 * TT // 2)

        @block.tensor
        def _(pe):
            def flip(src, name, need, count):
                pe.wait_ge(sig(need), count)
                for k in range(KT):
                    last = nc.tensor.transpose(psum[:, k * P:(k + 1) * P], src(k), ident[:])
                last.then_inc(sig(name), 1)

            def branches(t):
                if t >= 3:
                    pe.wait_ge(sig("logits"), t - 2)
                elif t >= 2:
                    pe.wait_ge(sig("mixed_t"), t - 1)
                elif t >= 1:
                    pe.wait_ge(sig("o_t"), t)
                else:
                    pe.wait_ge(sig("o_rwkv_in"), 16)
                for k in range(W // P):
                    last = nc.tensor.transpose(psum[:, k * P:(k + 1) * P], o_rwkv[:, t, k * P:(k + 1) * P], ident[:])
                last.then_inc(sig("o_flipped"), 1)
                pe.wait_ge(sig("o_t"), t + 1)
                if t == 0:
                    pe.wait_ge(sig("mg_w_in"), 48)
                for half in range(2):
                    cols = slice(half * NC5, (half + 1) * NC5)
                    if t >= 1:
                        pe.wait_ge(sig("branches_read"), 2 * (t - 1) + half + 1)
                    for j, w in enumerate((w_fox, w_rwkv)):
                        for k in range(W // P):
                            o = o_t[:, k, :] if j else o_fox_t[:, k, t * P:(t + 1) * P]
                            last = nc.tensor.matmul(bank[2 + 2 * half + j], o, w[:, k, cols],
                                                    start=(k == 0), stop=(k == W // P - 1))
                    last.then_inc(sig("branches_full"), 1)

            def outward(t):
                flip(lambda k: mixed[:, t % 2, k * P:(k + 1) * P], "mixed_flipped", "mg_mixed", 2 * (t + 1))
                pe.wait_ge(sig("mixed_t"), t + 1)
                if t == 0:
                    pe.wait_ge(sig("w_o_in"), 16)
                if t >= 1:
                    pe.wait_ge(sig("w_o_read"), t)
                for half in range(2):
                    for k in range(KT):
                        last = nc.tensor.matmul(bank[6 + half], mixed_t[:, k, :], w_o[:, k, half * NC5:(half + 1) * NC5],
                                                start=(k == 0), stop=(k == KT - 1))
                last.then_inc(sig("w_o_full"), 1)

            def router(t):
                flip(lambda k: h_mid[:, t % 2, k * P:(k + 1) * P], "h_flipped", "h_mid", t + 1)
                pe.wait_ge(sig("mg_h_t"), t + 1)
                if t == 0:
                    pe.wait_ge(sig("w_route_in"), 64)
                for k in range(KT):
                    last = nc.tensor.matmul(bank[0][:, 0:GE], h_t[:, k, :], w_route[:, k, :], start=(k == 0), stop=(k == KT - 1))
                last.then_inc(sig("logits_full"), 1)

            for s in range(TT + 2):
                if s < TT:
                    branches(s)
                if 1 <= s <= TT:
                    outward(s - 1)
                if s >= 2:
                    if s == TT + 1:
                        pass
                    router(s - 2)

        @block.scalar
        def _(act):
            for s in range(TT + 2):
                if s < TT:
                    act.wait_ge(sig("o_flipped"), s + 1)
                    nc.scalar.activation(o_t[:].rearrange("p k t -> p (k t)"), bank[0], ACT.Copy).then_inc(sig("o_t"), 1)
                if 1 <= s <= TT:
                    act.wait_ge(sig("mixed_flipped"), s)
                    nc.scalar.activation(mixed_t[:].rearrange("p k t -> p (k t)"), psum[:, 0:D], ACT.Copy).then_inc(sig("mixed_t"), 1)
                if s >= 2:
                    t = s - 2
                    act.wait_ge(sig("h_flipped"), t + 1)
                    nc.scalar.activation(h_t[:].rearrange("p k t -> p (k t)"), psum[:, 0:D], ACT.Copy).then_inc(sig("mg_h_t"), 1)
                if 1 <= s <= TT:
                    t = s - 1
                    act.wait_ge(sig("x_mid"), t + 1)
                    if t >= 1:
                        act.wait_ge(sig("h_scaled"), t)
                    nc.scalar.activation(part[:], x_mid[:, t % 2, :], ACT.Square, accum_out=ms[:, t:t + 1]).then_inc(sig("mg_ss"), 1)

        @block.vector
        def _(dve):
            link = Link(dve, sig("dve_link_m"))
            tt, stt, ts = nc.vector.tensor_tensor, nc.vector.scalar_tensor_tensor, nc.vector.tensor_scalar

            def gate(t):
                dve.wait_ge(sig(f"gates_in{t % 2}"), 16 * (t // 2 + 1))
                for half in range(2):
                    cols = slice(half * NC5, (half + 1) * NC5)
                    m = mixed[:, t % 2, cols]
                    g = gates[:, t % 2, :]
                    dve.wait_ge(sig("branches_full"), 2 * t + half + 1)
                    if t >= 2:
                        dve.wait_ge(sig("mixed_flipped"), t - 1)
                    tt(m, bank[2 + 2 * half], g[:, cols], ALU.mult).then_inc(sig("fox_gated"), 1)
                    g2 = g[:, D + half * NC5:D + (half + 1) * NC5]
                    tt(g2, bank[3 + 2 * half], g2, ALU.mult).then_inc(sig("branches_read"), 1)
                    dve.wait_ge(sig("branches_read"), 2 * t + half + 1)
                    dve.wait_ge(sig("fox_gated"), 2 * t + half + 1)
                    tt(m, m, g2, ALU.add).then_inc(sig("mg_mixed"), 1)

            def residual(t):
                xm, hm = x_mid[:, t % 2, :], h_mid[:, t % 2, :]
                dve.wait_ge(sig("w_o_full"), t + 1)
                dve.wait_ge(sig(f"mg_x_in{t % 2}"), 16 * (t // 2 + 1))
                if t >= 2:
                    dve.wait_ge(sig(f"x_mid_out{t % 2}"), 16 * (t // 2))
                    dve.wait_ge(sig(f"h_mid_out{t % 2}"), 16 * (t // 2))
                    dve.wait_ge(sig("h_flipped"), t - 1)
                tt(xm, psum[:, 6 * NC5:8 * NC5], mod_bc[:, 0, :], ALU.mult).then_inc(sig("w_o_read"), 1)
                dve.wait_ge(sig("w_o_read"), t + 1)
                tt(xm, xm, x_in[:, t % 2, :], ALU.add).then_inc(sig("x_mid"), 1)
                dve.wait_ge(sig("mg_ss"), t + 1)
                ts(ms[:, t:t + 1], ms[:, t:t + 1], 1.0 / D, EPS, ALU.mult, ALU.add).then_inc(sig("mg_ms"), 1)
                dve.wait_ge(sig("mg_rstd"), t + 1)
                stt(out=hm, in0=xm, scalar=ms[:, t:t + 1], in1=mod_bc[:, 2, :], op0=ALU.mult, op1=ALU.mult).then_inc(sig("h_scaled"), 1)
                dve.wait_ge(sig("h_scaled"), t + 1)
                tt(hm, hm, mod_bc[:, 1, :], ALU.add).then_inc(sig("h_mid"), 1)

            for s in range(TT + 2):
                if s >= 2:
                    t = s - 2
                    dve.wait_ge(sig("logits_full"), t + 1)
                    tt(logits[:, t, :], bank[0][:, 0:GE], b_route[:], ALU.add).then_inc(sig("logits"), 1)
                if s < TT:
                    gate(s)
                if 1 <= s <= TT:
                    residual(s - 1)


def route(nc, sig, bank, const, keep, ins, dram):
    logits, dest, pair_w = keep["logits"], keep["dest"], keep["pair_w"]
    psum = const["psum"]
    BIG = 1024.0
    with ExitStack() as ctx:
        sb = lambda name, shape, dt=F32: ctx.enter_context(nc.sbuf_tensor(name, shape, dt))
        ones = sb("rt_ones", [P, P])
        before = sb("rt_before", [P, P])
        iota_e = sb("iota_e", [P, E])
        iota_g = sb("iota_g", [P, G])
        iota_b = sb("iota_b", [P, OVERFLOW_BLOCKS])
        first_row = sb("first_row", [P, E])
        token = sb("rt_token", [P, 2, TT], I32)
        gmax = sb("rt_gmax", [P, TT])
        gexp = sb("rt_gexp", [P, TT, G])
        gsum = sb("rt_gsum", [P, TT])
        ghot = sb("rt_ghot", [P, TT, G])
        el = sb("rt_el", [P, TT, E])
        best = sb("rt_best", [P, 2, TT])
        hot = sb("rt_hot", [P, 2, TT, E])
        both = sb("rt_both", [P, TT, E])
        tmp = sb("rt_tmp", [P, TT, E])
        idx = sb("rt_idx", [P, TT])
        extra = sb("rt_extra", [P, E])
        extra_end = sb("rt_extra_end", [P, E])
        over_row = sb("rt_over_row", [P, E])
        diff = sb("rt_diff", [P, E])
        ones_e = sb("rt_ones_e", [P, E])
        row = sb("rt_row", [P, TT, E])
        destf = sb("rt_destf", [P, TT])
        table = sb("rt_table", [1, BLOCKS, E])
        tablef = sb("rt_tablef", [1, 1 + BLOCKS])
        free_row = sb("rt_free_row", [P, BLOCKS], I32)
        back_i = sb("rt_back_i", [BLOCKS, P], I32)
        back_f = sb("rt_back_f", [BLOCKS, P])
        pair_f = sb("rt_pair_f", [P, BLOCKS])
        token_f = sb("rt_token_f", [P, BLOCKS])
        block = ctx.enter_context(nc.Block("route"))

        def bt(ap, n):
            return ap.unsqueeze(2).to_broadcast([P, TT, n])

        def be(ap, n):
            return ap.unsqueeze(1).to_broadcast([P, TT, n])

        @block.sync
        def _(sp):
            prefetch_weights(nc, sp, sig, keep, ins)
            sp.wait_ge(sig("scattered"), 16 * 2 * TT)
            sp.dma_start(back_i[:], dram["row_pairs"].rearrange("(b p) a -> b (p a)", p=P)).then_inc(sig("rows_back"), 16)

        @block.gpsimd
        def _(pool):
            link = Link(pool, sig("pool_link_t"))
            nc.gpsimd.iota(free_row[:], [[1, BLOCKS]], base=2 * S, channel_multiplier=BLOCKS).then_inc(sig("rt_free"), 1)
            pool.wait_ge(sig("rt_free"), 1)
            link(nc.gpsimd.memset(ones[:], 1.0))
            link(nc.gpsimd.memset(before[:], 1.0))
            link(nc.gpsimd.affine_select(out=before[:], in_=before[:], compare_op=ALU.is_gt, fill=0.0, base=0,
                                         pattern=[[1, P]], channel_multiplier=-1))
            for ap, pattern, cm in ((iota_e, [[1, E]], 0), (iota_g, [[1, G]], 0), (iota_b, [[1, OVERFLOW_BLOCKS]], 0),
                                    (first_row, [[P, E]], 0)):
                link(nc.gpsimd.iota(ap[:], pattern, base=0, channel_multiplier=cm, allow_small_or_imprecise_dtypes=True))
            link(nc.gpsimd.iota(token[:], [[S, 2], [P, TT]], base=0, channel_multiplier=1))
            nc.gpsimd.nop().then_inc(sig("rt_const"), 1)
            pool.dma_start(dram["row_pairs"].rearrange("(p b) a -> p (b a)", p=P), free_row[:]).then_inc(sig("table_set"), 16)
            pool.wait_ge(sig("table_set"), 16)
            pool.wait_ge(sig("dest"), 2)
            for t in range(TT):
                for j in range(2):
                    pool.indirect_dma_start(dram["row_pairs"], bass.IndirectOffsetOnAxis(ap=dest[:, t, j:j + 1], axis=0),
                                            token[:, j, t:t + 1], None).then_inc(sig("scattered"), 16)

        @block.scalar
        def _(act):
            act.wait_ge(sig("rt_gshift"), 1)
            nc.scalar.activation(gexp[:], gexp[:], ACT.Exp).then_inc(sig("rt_gexp"), 1)
            act.wait_ge(sig("rt_ratio"), 1)
            nc.scalar.activation(best[:, 1, :], best[:, 1, :], ACT.Exp).then_inc(sig("rt_ratio_exp"), 1)

        @block.tensor
        def _(pe):
            pe.wait_ge(sig("rt_const"), 1)
            pe.wait_ge(sig("rt_both"), 1)
            for t in range(TT):
                for s in range(t + 1):
                    nc.tensor.matmul(bank[0][:, t * E:(t + 1) * E], ones[:] if s < t else before[:], both[:, s, :],
                                     start=(s == 0), stop=(s == t))
            for s in range(TT):
                last = nc.tensor.matmul(bank[1][:, 0:E], ones[:], both[:, s, :], start=(s == 0), stop=(s == TT - 1))
            last.then_inc(sig("ranks"), 1)
            pe.wait_ge(sig("back_f"), 1)
            nc.tensor.transpose(bank[2][:, 0:BLOCKS], back_f[:], const["ident"][0:BLOCKS, 0:BLOCKS]).then_inc(sig("back_flipped"), 1)

        @block.vector
        def _(dve):
            link = Link(dve, sig("dve_link_t"))
            tt, stt, ts, red = nc.vector.tensor_tensor, nc.vector.scalar_tensor_tensor, nc.vector.tensor_scalar, nc.vector.tensor_reduce
            gl = logits[:, :, 0:G]
            dve.wait_ge(sig("rt_const"), 1)

            def first_hot(out, vals, top, iota, n):
                link(tt(out, vals, bt(top, n), ALU.is_equal))
                link(stt(out=out, in0=out, scalar=-BIG, in1=be(iota, n), op0=ALU.mult, op1=ALU.add))
                link(red(idx[:], out, AX.X, ALU.min))
                link(ts(idx[:], idx[:], BIG, None, ALU.add))
                link(tt(out, be(iota, n), bt(idx[:], n), ALU.is_equal))

            link(red(gmax[:], gl, AX.X, ALU.max))
            tt(gexp[:], gl, bt(gmax[:], G), ALU.subtract).then_inc(sig("rt_gshift"), 1)
            first_hot(ghot[:], gl, gmax[:], iota_g[:], G)
            link(ts(ghot[:], ghot[:], 1.0, -NEG, ALU.subtract, ALU.mult))
            link(tt(el[:].rearrange("p t (g e) -> p t g e", e=EPG), logits[:, :, G:G + E].rearrange("p t (g e) -> p t g e", e=EPG),
                    ghot[:].unsqueeze(3).to_broadcast([P, TT, G, EPG]), ALU.add))
            link(red(best[:, 0, :], el[:], AX.X, ALU.max))
            first_hot(hot[:, 0], el[:], best[:, 0, :], iota_e[:], E)
            link(stt(out=el[:], in0=hot[:, 0], scalar=2.0 * NEG, in1=el[:], op0=ALU.mult, op1=ALU.add))
            link(red(best[:, 1, :], el[:], AX.X, ALU.max))
            first_hot(hot[:, 1], el[:], best[:, 1, :], iota_e[:], E)
            tt(both[:], hot[:, 0], hot[:, 1], ALU.add).then_inc(sig("rt_both"), 1)
            tt(best[:, 1, :], best[:, 1, :], best[:, 0, :], ALU.subtract).then_inc(sig("rt_ratio"), 1)
            dve.wait_ge(sig("rt_gexp"), 1)
            link(red(gsum[:], gexp[:], AX.X, ALU.add))
            dve.wait_ge(sig("rt_ratio_exp"), 1)
            link(ts(best[:, 0, :], best[:, 1, :], 1.0, None, ALU.add))
            link(tt(gsum[:], gsum[:], best[:, 0, :], ALU.mult))
            link(nc.vector.reciprocal(pair_w[:, :, 0], gsum[:]))
            link(tt(pair_w[:, :, 1], pair_w[:, :, 0], best[:, 1, :], ALU.mult))
            dve.wait_ge(sig("ranks"), 1)
            link(nc.vector.memset(extra[:], 0.0))
            link(nc.vector.memset(ones_e[:], 1.0))
            for j in range(1, S // P):
                link(stt(out=extra[:], in0=bank[1][:, 0:E], scalar=float(j * P), in1=extra[:], op0=ALU.is_gt, op1=ALU.add))
            link(nc.vector.tensor_tensor_scan(extra_end[:], ones_e[:], extra[:], 0.0, ALU.mult, ALU.add))
            link(tt(over_row[:], extra_end[:], extra[:], ALU.subtract))
            link(ts(over_row[:], over_row[:], float(P), float(E * P - P), ALU.mult, ALU.add))
            link(tt(diff[:], first_row[:], over_row[:], ALU.subtract))
            rank = bank[0][:, 0:TT * E].rearrange("p (t e) -> p t e", e=E)
            link(nc.vector.tensor_copy(tmp[:], rank))
            link(stt(out=row[:], in0=tmp[:], scalar=float(P), in1=be(diff[:], E), op0=ALU.is_lt, op1=ALU.mult))
            link(tt(row[:], row[:], tmp[:], ALU.add))
            link(tt(row[:], row[:], be(over_row[:], E), ALU.add))
            for j in range(2):
                link(tt(tmp[:], row[:], hot[:, j], ALU.mult))
                link(red(destf[:], tmp[:], AX.X, ALU.add))
                nc.vector.tensor_copy(dest[:, :, j], destf[:]).then_inc(sig("dest"), 1)
                dve.wait_ge(sig("dest"), j + 1)
            link(nc.vector.tensor_copy(tablef[0:1, 1:1 + E], iota_e[0:1, :]))
            over = table[0:1, 0:OVERFLOW_BLOCKS, :]
            link(tt(over, extra_end[0:1, :].unsqueeze(1).to_broadcast([1, OVERFLOW_BLOCKS, E]),
                    iota_b[0:1, :].unsqueeze(2).to_broadcast([1, OVERFLOW_BLOCKS, E]), ALU.is_le))
            link(red(tablef[0:1, 1 + E:1 + BLOCKS], over, AX.X, ALU.add))
            link(ts(tablef[0:1, 1 + E:1 + BLOCKS], tablef[0:1, 1 + E:1 + BLOCKS], float(E - 1), None, ALU.min))
            link(ts(table[0:1, 0, 0:OVERFLOW_BLOCKS // 2], iota_b[0:1, 0:OVERFLOW_BLOCKS // 2], 2.0, None, ALU.mult))
            link(tt(table[0:1, 0, 0:OVERFLOW_BLOCKS // 2], table[0:1, 0, 0:OVERFLOW_BLOCKS // 2],
                    extra_end[0:1, E - 1:E].to_broadcast([1, OVERFLOW_BLOCKS // 2]), ALU.is_lt))
            link(red(tablef[0:1, 0:1], table[0:1, 0, 0:OVERFLOW_BLOCKS // 2], AX.X, ALU.add))
            link(ts(tablef[0:1, 0:1], tablef[0:1, 0:1], float(E // 2 - 2), None, ALU.add))
            link(nc.vector.tensor_copy(keep["blocks"][:], tablef[:]))
            dve.wait_ge(sig("rows_back"), 16)
            nc.vector.tensor_copy(back_f[:], back_i[:]).then_inc(sig("back_f"), 1)
            dve.wait_ge(sig("back_flipped"), 1)
            link(nc.vector.tensor_copy(pair_f[:], bank[2][:, 0:BLOCKS]))
            link(nc.vector.tensor_copy(keep["row_pair"][:], pair_f[:]))
            link(ts(token_f[:], pair_f[:], float(S), float(-S), ALU.is_ge, ALU.mult))
            link(tt(token_f[:], token_f[:], pair_f[:], ALU.add))
            link(nc.vector.tensor_copy(keep["row_token"][:], token_f[:]))


HALF_K = KT // 2


def load_up(nc, sp, sig, keep, ins, par, q, e):
    for j, name in enumerate(("exp_w1", "exp_w3")):
        w = ins[name][0]
        src = w[e] if isinstance(e, int) else w[bass.ds(e, 1)].rearrange("a k n -> (a k) n")
        src = src.rearrange("(k p) n -> p k n", p=P)[:, q * HALF_K:(q + 1) * HALF_K, :]
        sp.dma_start(keep["w13"][:, par, q * HALF_K:(q + 1) * HALF_K, j, :], src).then_inc(sig(f"w13_in{par}{q}"), 16)


def load_down(nc, sp, sig, keep, ins, par, e):
    w = ins["exp_w2"][0]
    src = w[e] if isinstance(e, int) else w[bass.ds(e, 1)].rearrange("a k n -> (a k) n")
    sp.dma_start(keep["w2"][:, par], src.rearrange("(k p) n -> p k n", p=P)).then_inc(sig(f"w2_in{par}"), 16)


def prefetch_weights(nc, sp, sig, keep, ins):
    for b in range(2):
        for q in range(2):
            load_up(nc, sp, sig, keep, ins, b, q, b)
        load_down(nc, sp, sig, keep, ins, b, b)


def experts(nc, sig, bank, const, keep, ins, dram):
    psum, ident = const["psum"], const["ident"]
    blocks, w13, w2 = keep["blocks"], keep["w13"], keep["w2"]
    FK = FE // P
    RING = 4
    with ExitStack() as ctx:
        sb = lambda name, shape, dt=F32: ctx.enter_context(nc.sbuf_tensor(name, shape, dt))
        x_in = sb("ex_x", [P, 2, D])
        x_t = sb("ex_x_t", [P, 2, 2, KT, P], F32R)
        w_r = sb("ex_w_r", [P, RING, 2, D], F32R)
        sigm = sb("ex_sigm", [P, FE])
        hidden = sb("ex_hidden", [P, FE])
        hid_t = sb("ex_hid_t", [P, 2, 2, FK, P], F32R)
        y = sb("ex_y", [P, 2, D])
        idx = sb("ex_idx", [P, 2, 2], I32)
        spare = sb("ex_spare", [P, 1])
        block = ctx.enter_context(nc.Block("experts"))

        def up_count(blk, n):
            return 16 * blk[1] + (8 * blk[0] + n)

        def down_count(blk, n):
            return 8 * blk[1] + (4 * blk[0] + n)

        def slots(eng, slot):
            inner = eng.value_load(blocks[0:1, 0:1], min_val=E // 2 - 2, max_val=BLOCKS // 2 - 2)
            slot((0, 0), None, (1, 0))
            slot((1, 0), (0, 0), (0, 1))
            slot((0, 1), (1, 0), (1, 1))
            with eng.Fori(1, inner + 1) as j:
                slot((1, j), (0, j), (0, j + 1))
                slot((0, j + 1), (1, j), (1, j + 1))
            slot((1, inner + 1), (0, inner + 1), None)

        @block.sync
        def _(sp):
            inner = sp.value_load(blocks[0:1, 0:1], min_val=E // 2 - 2, max_val=BLOCKS // 2 - 2)
            with sp.Fori(0, inner + 1) as i:
                for par in range(2):
                    e = sp.value_load(blocks[0:1, bass.ds(2 * i + par + 3, 1)], min_val=0, max_val=E - 1)
                    for q in range(2):
                        sp.wait_ge(sig("up_lo"), up_count((par, i), HALF_K * (q + 1)))
                        load_up(nc, sp, sig, keep, ins, par, q, e)
                    sp.wait_ge(sig("down_lo"), down_count((par, i), FK))
                    load_down(nc, sp, sig, keep, ins, par, e)

        @block.gpsimd
        def _(pool):
            def index(kind, table, par, pair):
                b = 2 * pair + par
                src = table[:, b:b + 1] if isinstance(b, int) else table[:, bass.ds(b, 1)]
                nc.gpsimd.tensor_copy(idx[:, kind, par:par + 1], src).then_inc(sig(f"idx{kind}{par}"), 1)
                pool.wait_ge(sig(f"idx{kind}{par}"), pair + 1)
                nc.gpsimd.tensor_tensor(spare[:], const["neghalf"][:, 0:1], const["neghalf"][:, 0:1], ALU.mult)
                return bass.IndirectOffsetOnAxis(ap=idx[:, kind, par:par + 1], axis=0)

            def gather(par, pair):
                if not (isinstance(pair, int) and pair == 0):
                    pool.wait_ge(sig(f"x_flipped{par}"), pair)
                at = index(0, keep["row_token"], par, pair)
                pool.indirect_dma_start(x_in[:, par, :], None, dram["h_mid"], at, bounds_check=S - 1,
                                        oob_is_err=False).then_inc(sig(f"x_in_e{par}"), 16)

            def store(par, pair):
                pool.wait_ge(sig(f"y_e{par}"), pair + 1)
                at = index(1, keep["row_pair"], par, pair)
                pool.indirect_dma_start(dram["pair_rows"], at, y[:, par, :], None, bounds_check=2 * S - 1,
                                        oob_is_err=False).then_inc(sig(f"y_out{par}"), 16)

            inner = pool.value_load(blocks[0:1, 0:1], min_val=E // 2 - 2, max_val=BLOCKS // 2 - 2)
            nc.gpsimd.memset(x_in[:], 0.0).then_inc(sig("x_zero"), 1)
            pool.wait_ge(sig("x_zero"), 1)
            gather(0, 0)
            gather(1, 0)
            gather(0, 1)
            store(0, 0)
            gather(1, 1)
            with pool.Fori(0, inner) as j:
                gather(0, j + 2)
                store(1, j)
                gather(1, j + 2)
                store(0, j + 1)
            store(1, inner)
            store(0, inner + 1)
            store(1, inner + 1)
            for q in range(2):
                pool.wait_ge(sig(f"y_out{q}"), 16 * (inner + 2))

        @block.tensor
        def _(pe):
            def product(out, lhs, unit, cols, first, last):
                hi, lo = w_r[:, unit % RING, 0, cols], w_r[:, unit % RING, 1, cols]
                nc.tensor.matmul(out, lhs[0], hi, start=first, stop=False)
                nc.tensor.matmul(out, lhs[0], lo, start=False, stop=False)
                return nc.tensor.matmul(out, lhs[1], hi, start=False, stop=last)

            def flip_x(blk, before):
                pe.wait_ge(sig(f"x_in_e{blk[0]}"), 16 * (blk[1] + 1))
                if before:
                    pe.wait_ge(sig(f"x_lo{before[0]}"), before[1] + 1)
                for k in range(KT):
                    last = nc.tensor.transpose(psum[:, k * P:(k + 1) * P], x_in[:, blk[0], k * P:(k + 1) * P], ident[:])
                last.then_inc(sig(f"x_flipped{blk[0]}"), 1)

            def down(blk, y_before):
                par, pair = blk
                pe.wait_ge(sig(f"hid_lo{par}"), pair + 1)
                if y_before:
                    pe.wait_ge(sig(f"y_e{y_before[0]}"), y_before[1])
                for k in range(FK):
                    pe.wait_ge(sig("down_lo"), down_count(blk, k + 1))
                    for half in range(2):
                        last = product(bank[6 + half], [hid_t[:, par, i, k, :] for i in range(2)], k,
                                       slice(half * NC5, (half + 1) * NC5), k == 0, k == FK - 1)
                    last.then_inc(sig("down_used"), 1)

            def slot(blk, before, behind):
                par, pair = blk
                if not before:
                    flip_x(blk, None)
                pe.wait_ge(sig(f"x_lo{par}"), pair + 1)
                if before:
                    pe.wait_ge(sig(f"hidden{before[0]}"), before[1] + 1)
                for k in range(KT):
                    pe.wait_ge(sig("up_lo"), up_count(blk, k + 1))
                    for j in range(2):
                        last = product(bank[2 + j], [x_t[:, par, i, k, :] for i in range(2)], k,
                                       slice(j * FE, (j + 1) * FE), k == 0, k == KT - 1)
                    last.then_inc(sig("up_used"), 1)
                if behind:
                    flip_x(behind, blk)
                if before:
                    first = isinstance(pair, int) and pair == 0
                    down(before, None if first else (par, pair))
                pe.wait_ge(sig(f"hidden{par}"), pair + 1)
                if before:
                    pe.wait_ge(sig(f"hid_lo{before[0]}"), before[1] + 1)
                for k in range(FK):
                    last = nc.tensor.transpose(bank[4][:, k * P:(k + 1) * P], hidden[:, k * P:(k + 1) * P], ident[:])
                last.then_inc(sig(f"hid_flipped{par}"), 1)
                if not behind:
                    down(blk, (before[0], before[1] + 1))

            slots(pe, slot)

        @block.scalar
        def _(act):
            def copy(out, src):
                return nc.scalar.activation(out, src, ACT.Copy)

            def x_hi(par, pair):
                act.wait_ge(sig(f"x_flipped{par}"), pair + 1)
                copy(x_t[:, par, 0].rearrange("p k t -> p (k t)"), psum[:, 0:D]).then_inc(sig(f"x_hi{par}"), 1)

            def up_hi(blk, units, used):
                for u in units:
                    if u % HALF_K == 0:
                        act.wait_ge(sig(f"w13_in{blk[0]}{u // HALF_K}"), 32 * (blk[1] + 1))
                    if used:
                        act.wait_ge(*used(u))
                    copy(w_r[:, u % RING, 0, :], w13[:, blk[0], u].rearrange("p j n -> p (j n)")).then_inc(sig("up_hi"), 1)

            def down_hi(blk, used):
                act.wait_ge(sig(f"w2_in{blk[0]}"), 16 * (blk[1] + 1))
                for u in range(FK):
                    act.wait_ge(*used(u))
                    copy(w_r[:, u, 0, :], w2[:, blk[0], u, :]).then_inc(sig("down_hi"), 1)

            def move_y(blk):
                par, pair = blk
                act.wait_ge(sig("down_used"), down_count(blk, FK))
                if not (isinstance(pair, int) and pair == 0):
                    act.wait_ge(sig(f"y_out{par}"), 16 * pair)
                copy(y[:, par, :], psum[:, 6 * NC5:8 * NC5]).then_inc(sig(f"y_e{par}"), 1)

            def slot(blk, before, behind):
                par, pair = blk
                if not before:
                    x_hi(*blk)
                    up_hi(blk, range(RING), None)
                up_hi(blk, range(RING, KT), lambda u: (sig("up_used"), up_count(blk, u - RING + 1)))
                if before:
                    down_hi(before, lambda u: (sig("up_used"), up_count(blk, u + RING + 1)))
                act.wait_ge(sig("up_used"), up_count(blk, KT))
                nc.scalar.activation(sigm[:], bank[2], ACT.Sigmoid).then_inc(sig(f"sigm{par}"), 1)
                if behind:
                    x_hi(*behind)
                    if before:
                        up_hi(behind, range(RING), lambda u: (sig("down_used"), down_count(before, u + 1)))
                    else:
                        up_hi(behind, range(RING), lambda u: (sig("up_used"), up_count(blk, u + RING + 1)))
                if before:
                    move_y(before)
                act.wait_ge(sig(f"hid_flipped{par}"), pair + 1)
                copy(hid_t[:, par, 0].rearrange("p k t -> p (k t)"), bank[4]).then_inc(sig(f"hid_hi{par}"), 1)
                if not behind:
                    down_hi(blk, lambda u: (sig("down_used"), down_count(before, u + 1)))
                    move_y(blk)

            slots(act, slot)

        @block.vector
        def _(dve):
            def low(out, whole, high):
                return nc.vector.tensor_tensor(out, whole, high.bitcast(F32), ALU.subtract)

            def x_lo(par, pair):
                dve.wait_ge(sig(f"x_hi{par}"), pair + 1)
                parts = [x_t[:, par, i].rearrange("p k t -> p (k t)") for i in range(2)]
                low(parts[1], psum[:, 0:D], parts[0]).then_inc(sig(f"x_lo{par}"), 1)

            def up_lo(blk, units):
                for u in units:
                    dve.wait_ge(sig("up_hi"), up_count(blk, u + 1))
                    low(w_r[:, u % RING, 1, :], w13[:, blk[0], u].rearrange("p j n -> p (j n)"), w_r[:, u % RING, 0, :]).then_inc(sig("up_lo"), 1)

            def down_lo(blk):
                for u in range(FK):
                    dve.wait_ge(sig("down_hi"), down_count(blk, u + 1))
                    low(w_r[:, u, 1, :], w2[:, blk[0], u, :], w_r[:, u, 0, :]).then_inc(sig("down_lo"), 1)

            def slot(blk, before, behind):
                par, pair = blk
                if not before:
                    x_lo(*blk)
                    up_lo(blk, range(RING))
                up_lo(blk, range(RING, KT))
                if before:
                    down_lo(before)
                dve.wait_ge(sig(f"sigm{par}"), pair + 1)
                nc.vector.tensor_tensor(sigm[:], bank[2], sigm[:], ALU.mult).then_inc(sig(f"silu{par}"), 1)
                dve.wait_ge(sig(f"silu{par}"), pair + 1)
                nc.vector.tensor_tensor(hidden[:], bank[3], sigm[:], ALU.mult).then_inc(sig(f"hidden{par}"), 1)
                if behind:
                    x_lo(*behind)
                    up_lo(behind, range(RING))
                dve.wait_ge(sig(f"hid_hi{par}"), pair + 1)
                parts = [hid_t[:, par, i].rearrange("p k t -> p (k t)") for i in range(2)]
                low(parts[1], bank[4], parts[0]).then_inc(sig(f"hid_lo{par}"), 1)
                if not behind:
                    down_lo(blk)

            slots(dve, slot)


def combine(nc, sig, bank, const, keep, ins, dram, out):
    mod_bc, pair_w = keep["mod_bc"], keep["pair_w"]
    with ExitStack() as ctx:
        sb = lambda name, shape: ctx.enter_context(nc.sbuf_tensor(name, shape, F32))
        rows = sb("cb_rows", [P, 3, 2, D])
        x_in = sb("cb_x", [P, 3, D])
        sq = sb("cb_sq", [P, D])
        ms = sb("cb_ms", [P, TT])
        block = ctx.enter_context(nc.Block("combine"))

        @block.sync
        def _(sp):
            sp.dma_start(mod_bc[:, 4, :], ins["final_g"].rearrange("(a n) -> a n", a=1).partition_broadcast(P).rearrange("p a n -> p (a n)")).then_inc(sig("fg_in"), 16)
            for t in range(TT):
                if t >= 3:
                    sp.wait_ge(sig(f"out_done{t % 3}"), 16 * (t // 3))
                sp.dma_start(x_in[:, t % 3, :], dram["x_mid"][t * P:(t + 1) * P, :]).then_inc(sig(f"cb_x_in{t % 3}"), 16)
                if t >= 3:
                    sp.wait_ge(sig("cb_x"), t - 2)
                for j in range(2):
                    sp.dma_start(rows[:, t % 3, j, :], dram["pair_rows"][j * S + t * P:j * S + (t + 1) * P, :]).then_inc(sig(f"cb_rows_in{t % 3}"), 16)

        @block.gpsimd
        def _(pool):
            for t in range(TT):
                pool.wait_ge(sig("cb_ms"), t + 1)
                nc.gpsimd.tensor_tensor(ms[:, t:t + 1], ms[:, t:t + 1], const["neghalf"][:, 0:1], ALU.pow).then_inc(sig("cb_rstd"), 1)

        @block.scalar
        def _(act):
            for t in range(TT):
                act.wait_ge(sig("cb_x"), t + 1)
                if t >= 1:
                    act.wait_ge(sig("cb_ss"), t)
                nc.scalar.activation(sq[:], x_in[:, t % 3, :], ACT.Square, accum_out=ms[:, t:t + 1]).then_inc(sig("cb_ss"), 1)
                act.wait_ge(sig("cb_out"), t + 1)
                act.dma_start(out[0, t * P:(t + 1) * P, :], x_in[:, t % 3, :]).then_inc(sig(f"out_done{t % 3}"), 16)
            for b in range(3):
                act.wait_ge(sig(f"out_done{b}"), 16 * ((TT + 2 - b) // 3))

        @block.tensor
        def _(pe):
            pass

        @block.vector
        def _(dve):
            link = Link(dve, sig("dve_link_c"))
            tt, stt, ts = nc.vector.tensor_tensor, nc.vector.scalar_tensor_tensor, nc.vector.tensor_scalar
            dve.wait_ge(sig("fg_in"), 16)
            for t in range(TT):
                a, b, x = rows[:, t % 3, 0, :], rows[:, t % 3, 1, :], x_in[:, t % 3, :]
                dve.wait_ge(sig(f"cb_rows_in{t % 3}"), 32 * (t // 3 + 1))
                dve.wait_ge(sig(f"cb_x_in{t % 3}"), 16 * (t // 3 + 1))
                link(ts(a, a, pair_w[:, t, 0:1], None, ALU.mult))
                link(stt(out=a, in0=b, scalar=pair_w[:, t, 1:2], in1=a, op0=ALU.mult, op1=ALU.add))
                link(tt(a, a, mod_bc[:, 3, :], ALU.mult))
                tt(x, x, a, ALU.add).then_inc(sig("cb_x"), 1)
                dve.wait_ge(sig("cb_ss"), t + 1)
                ts(ms[:, t:t + 1], ms[:, t:t + 1], 1.0 / D, EPS, ALU.mult, ALU.add).then_inc(sig("cb_ms"), 1)
                dve.wait_ge(sig("cb_rstd"), t + 1)
                stt(out=x, in0=x, scalar=ms[:, t:t + 1], in1=mod_bc[:, 4, :], op0=ALU.mult, op1=ALU.mult).then_inc(sig("cb_out"), 1)


def constants(nc, sig, const):
    with nc.Block("constants") as block:
        @block.gpsimd
        def _(pool):
            nc.gpsimd.memset(const["ident"][:], 0.0).then_inc(sig("const_set"), 1)
            nc.gpsimd.memset(const["ones"][:], 1.0).then_inc(sig("const_set"), 1)
            nc.gpsimd.memset(const["neghalf"][:], -0.5).then_inc(sig("const_set"), 1)
            pool.wait_ge(sig("const_set"), 1)
            nc.gpsimd.affine_select(out=const["ident"][:], in_=const["ident"][:], compare_op=ALU.not_equal, fill=1.0,
                                    base=0, pattern=[[-1, P]], channel_multiplier=1).then_inc(sig("const_set"), 1)
            pool.wait_ge(sig("const_set"), 4)


def build(nc, ins, out):
    dram = {
        "p_rwkv": nc.dram_tensor("p_rwkv", (S + 1, SHIFT), F32, kind="Internal").ap(),
        "qk": nc.dram_tensor("qk", (2, 2, W, S), F32, kind="Internal").ap(),
        "v": nc.dram_tensor("v", (S, W), F32, kind="Internal").ap(),
        "ncum": nc.dram_tensor("ncum", (H, S), F32, kind="Internal").ap(),
        "o_fox_t": nc.dram_tensor("o_fox_t", (W, S), F32, kind="Internal").ap(),
        "o_rwkv": nc.dram_tensor("o_rwkv", (S, W), F32, kind="Internal").ap(),
        "gates": nc.dram_tensor("gates", (S, 2 * D), F32, kind="Internal").ap(),
        "x_mid": nc.dram_tensor("x_mid", (S, D), F32, kind="Internal").ap(),
        "h_mid": nc.dram_tensor("h_mid", (S, D), F32, kind="Internal").ap(),
        "row_pairs": nc.dram_tensor("row_pairs", (ROWS, 1), I32, kind="Internal").ap(),
        "pair_rows": nc.dram_tensor("pair_rows", (2 * S, D), F32, kind="Internal").ap(),
    }
    with ExitStack() as ctx:
        sig = Signals(nc, ctx)
        psum = ctx.enter_context(nc.psum_tensor("psum", [P, 8 * NC5], F32))
        bank = [psum[:, i * NC5:(i + 1) * NC5] for i in range(8)]
        sb = lambda name, shape, dt=F32: ctx.enter_context(nc.sbuf_tensor(name, shape, dt))
        const = {"ident": sb("ident", [P, P]), "ones": sb("ones", [P, P]), "neghalf": sb("neghalf", [P, H]), "psum": psum}
        keep = {"mod_bc": sb("mod_bc", [P, 5, D])}
        keep["logits"] = keep["mod_bc"][:, 4, 0:TT * (G + E)].rearrange("p (t e) -> p t e", e=G + E)
        constants(nc, sig, const)
        sig.next_stage("constants")
        with ExitStack() as early:
            sbe = lambda name, shape, dt=F32: early.enter_context(nc.sbuf_tensor(name, shape, dt))
            keep["ring"] = sbe("w_ring", [P, 2, KT, NC5])
            keep["h_hi"] = sbe("h_hi", [P, KT, S], F32R)
            keep["h_lo"] = sbe("h_lo", [P, KT, S], F32R)
            keep["c_silu"] = sbe("c_silu", [P, KT])
            weights = Ring(sig, keep["ring"], ins)
            modulate(nc, sig, bank, const, keep, ins, dram, weights)
            sig.next_stage("modulate")
            project(nc, sig, bank, const, keep, ins, dram, weights)
            sig.next_stage("project")
        attend(nc, sig, bank, const, keep, dram)
        sig.next_stage("attend")
        recur(nc, sig, bank, const, keep, ins, dram)
        sig.next_stage("recur")
        merge(nc, sig, bank, const, keep, ins, dram)
        sig.next_stage("merge")
        with ExitStack() as late:
            sbl = lambda name, shape, dt=F32: late.enter_context(nc.sbuf_tensor(name, shape, dt))
            keep["dest"] = sbl("dest", [P, TT, 2], I32)
            keep["pair_w"] = sbl("pair_w", [P, TT, 2])
            keep["blocks"] = sbl("blocks", [1, 1 + BLOCKS], I32)
            keep["row_token"] = sbl("row_token", [P, BLOCKS], I32)
            keep["row_pair"] = sbl("row_pair", [P, BLOCKS], I32)
            keep["w13"] = sbl("w13", [P, 2, KT, 2, FE])
            keep["w2"] = sbl("w2", [P, 2, FE // P, D])
            route(nc, sig, bank, const, keep, ins, dram)
            sig.next_stage("route")
            experts(nc, sig, bank, const, keep, ins, dram)
            sig.next_stage("experts")
            combine(nc, sig, bank, const, keep, ins, dram, out)


INPUTS = ["x", "c", "ada_w", "ada_b", "norm1_g", "w_in", "fox_forget_b", "shift_mu", "rwkv_w0", "rwkv_w2", "rwkv_a0",
          "rwkv_a2", "rwkv_g2", "rwkv_k_k", "rwkv_k_a", "rwkv_r_k", "ln_x_g", "ln_x_b", "w_out_fox", "w_out_rwkv",
          "w_o", "norm2_g", "router_group_w", "router_group_b", "router_expert_w", "router_expert_b", "exp_w1",
          "exp_w3", "exp_w2", "final_g"]


def kernel(**inputs):
    import numpy as _np
    import concourse.bacc as _bacc
    from concourse import mybir as _mybir
    from concourse.bass_utils import run_bass_kernel_spmd as _run

    nc = _bacc.Bacc("TRN2", target_bir_lowering=False, num_devices=1)
    arrays, aps = {}, {}
    for name in INPUTS:
        a = _np.ascontiguousarray(inputs[name])
        arrays[f"in_{name}"] = a
        aps[name] = nc.dram_tensor(f"in_{name}", a.shape, _mybir.dt.from_np(a.dtype), kind="ExternalInput").ap()
    out = nc.dram_tensor("out", (1, S, D), F32, kind="ExternalOutput").ap()
    build(nc, aps, out)
    r = _run(nc, [arrays], core_ids=[0])
    return r.results[0]["out"]
```

```python
from contextlib import ExitStack

import numpy as np

import concourse.bass as bass
from concourse import mybir

F32 = mybir.dt.float32
F32R = mybir.dt.float32r
I32 = mybir.dt.int32
ALU = mybir.AluOpType
ACT = mybir.ActivationFunctionType
AX = mybir.AxisListType

P = 128
D = 1024
S = 1024
TT = S // P
KT = D // P
H = 8
HD = 64
W = H * HD
NC5 = 512
LORA = 64
GLORA = 128
SHIFT = 3 * W + 2 * LORA + GLORA
COL_V = 2 * W
COL_F = 3 * W
COL_R = COL_F + H
COL_G = COL_R + SHIFT
CHUNK = 64
G, EPG = 4, 8
E = G * EPG
FE = 512
NEG = -1.0e30
EPS = 1e-6
LN_EPS = 64e-5
EXPM05 = float(np.exp(-0.5))
OVERFLOW_BLOCKS = 2 * S // P
BLOCKS = E + OVERFLOW_BLOCKS
ROWS = BLOCKS * P
LASTING = ("chunk_in0", "chunk_in1", "ring_used", "raw_in0", "raw_in1", "raw_in2", "raw_in3",
           "w13_in00", "w13_in01", "w13_in10", "w13_in11", "w2_in0", "w2_in1")
SOFTWARE_DMA = ("g1_in", "adab_in", "fb_in", "wf_in", "g2_in", "zrow_out", "mu_in", "x_mid_out0", "x_mid_out1",
                "h_mid_out0", "h_mid_out1", "bias_in", "x_in_e0", "x_in_e1", "y_out0", "y_out1")


class Signals:

    POOL = 100

    def __init__(self, nc, ctx):
        self.nc = nc
        self.pool = [ctx.enter_context(nc.semaphore(f"stage_{i}")) for i in range(self.POOL)]
        self.lasting = {n: ctx.enter_context(nc.semaphore(n)) for n in LASTING + SOFTWARE_DMA}
        self.names = {}

    def __call__(self, name):
        if name in self.lasting:
            return self.lasting[name]
        return self.pool[self.names.setdefault(name, len(self.names))]

    def next_stage(self, stage):
        used = [self.pool[i].num for i in range(len(self.names))]
        self.names = {}
        assert used == list(range(used[0], used[0] + len(used)))
        with self.nc.Block(f"{stage}_cleared") as block:
            @block.gpsimd
            def _(pool):
                pool.sem_clear(range(used[0], used[0] + len(used)))


class Ring:

    def __init__(self, sig, ring, ins):
        self.sig, self.ring = sig, ring
        ada = ins["ada_w"][0].rearrange("(p k) n -> p k n", k=KT)
        w_in = ins["w_in"][0].rearrange("(k p) n -> p k n", p=P)
        mod = [("mod", j, ada[:, :, j * NC5:(j + 1) * NC5]) for j in range(12)]
        self.proj = [(("q", "k")[j], 0, w_in[:, :, j * NC5:(j + 1) * NC5]) for j in range(2)]
        self.proj += [("v", 0, w_in[:, :, COL_V:COL_V + NC5])]
        self.proj += [("rwkv", j, w_in[:, :, COL_R + j * NC5:COL_R + min((j + 1) * NC5, SHIFT)]) for j in range(-(-SHIFT // NC5))]
        self.proj += [("gate", j, w_in[:, :, COL_G + j * NC5:COL_G + (j + 1) * NC5]) for j in range(2 * D // NC5)]
        self.order = mod[:4]
        for i, c in enumerate(self.proj):
            self.order += [c] + mod[4 + i:5 + i] if i < 8 else [c]
        self.turn = {(kind, j): i for i, (kind, j, _) in enumerate(self.order)}

    def load(self, sp, turns):
        for i in turns:
            src = self.order[i][2]
            if i >= 2:
                sp.wait_ge(self.sig("ring_used"), i - 1)
            sp.dma_start(self.ring[:, i % 2, :, 0:src.shape[2]], src).then_inc(self.sig(f"chunk_in{i % 2}"), 16)

    def arrived(self, eng, i):
        eng.wait_ge(self.sig(f"chunk_in{i % 2}"), 16 * (i // 2 + 1))

    def accumulate(self, nc, dve, link, j, c_silu, dst):
        i = self.turn["mod", j]
        self.arrived(dve, i)
        link(nc.vector.tensor_scalar(dst, self.ring[:, i % 2, 0, :], c_silu[:, 0:1], None, ALU.mult))
        for k in range(1, KT):
            last = nc.vector.scalar_tensor_tensor(out=dst, in0=self.ring[:, i % 2, k, :], scalar=c_silu[:, k:k + 1],
                                                  in1=dst, op0=ALU.mult, op1=ALU.add)
            if k < KT - 1:
                link(last)
        last.then_inc(self.sig("ring_used"), 1)
        dve.wait_ge(self.sig("ring_used"), i + 1)


class Link:

    def __init__(self, eng, sem, start=0):
        self.eng, self.sem, self.n = eng, sem, start

    def __call__(self, ins):
        self.n += 1
        ins.then_inc(self.sem, 1)
        self.eng.wait_ge(self.sem, self.n)


def modulate(nc, sig, bank, const, keep, ins, dram, weights):
    h_hi, h_lo, c_silu = keep["h_hi"], keep["h_lo"], keep["c_silu"]
    HALF = TT // 2
    with ExitStack() as ctx:
        sb = lambda name, shape, dt=F32: ctx.enter_context(nc.sbuf_tensor(name, shape, dt))
        x_in = sb("x_in", [P, TT, D])
        acc = sb("mod_acc", [P, 2, D])
        full = sb("h_full", [P, 3, NC5])
        sq = sb("x_sq", [P, D])
        c_col = sb("c_col", [P, KT])
        g1_col = sb("g1_col", [P, KT])
        b_col = sb("b_col", [P, 2 * KT])
        cols = sb("mod_cols", [P, 2 * KT])
        ss = sb("ss", [P, TT])
        zero = sb("zero_row", [1, SHIFT])
        block = ctx.enter_context(nc.Block("modulate"))

        @block.sync
        def _(sp):
            sp.dma_start(c_col[:], ins["c"][0].rearrange("(p k) -> p k", k=KT)).then_inc(sig("c_in"), 16)
            for t in range(TT):
                sp.dma_start(x_in[:, t, :], ins["x"][0, t * P:(t + 1) * P, :]).then_inc(sig(f"x_in{t}"), 16)
                if t < 2:
                    weights.load(sp, [t])
            weights.load(sp, range(2, 6))

        @block.gpsimd
        def _(pool):
            pool.dma_start(g1_col[:], ins["norm1_g"][0].rearrange("(k p) -> p k", p=P), allow_slow_non_contiguous=True).then_inc(sig("g1_in"), 16)
            pool.dma_start(b_col[:], ins["ada_b"][0, 0:2 * D].rearrange("(k p) -> p k", p=P), allow_slow_non_contiguous=True).then_inc(sig("adab_in"), 16)
            pool.dma_start(keep["w_f"][:], ins["w_in"][0].rearrange("(k p) n -> p k n", p=P)[:, :, COL_F:COL_R]).then_inc(sig("wf_in"), 16)
            nc.gpsimd.memset(zero[:], 0.0).then_inc(sig("zrow"), 1)
            pool.wait_ge(sig("zrow"), 1)
            pool.dma_start(dram["p_rwkv"][0:1, :], zero[:]).then_inc(sig("zrow_out"), 16)
            for t in range(TT):
                pool.wait_ge(sig("x_ms"), t + 1)
                nc.gpsimd.tensor_tensor(ss[:, t:t + 1], ss[:, t:t + 1], const["neghalf"][:, 0:1], ALU.pow).then_inc(sig("x_rstd"), 1)
            pool.wait_ge(sig("zrow_out"), 16)
            pool.wait_ge(sig("wf_in"), 16)

        @block.vector
        def _(dve):
            link = Link(dve, sig("dve_link_a"))
            tt, stt, ts = nc.vector.tensor_tensor, nc.vector.scalar_tensor_tensor, nc.vector.tensor_scalar
            dve.wait_ge(sig("c_sig"), 1)
            link(tt(c_silu[:], c_silu[:], c_col[:], ALU.mult))
            for t in range(TT):
                dve.wait_ge(sig("x_ss"), t + 1)
                ts(ss[:, t:t + 1], ss[:, t:t + 1], 1.0 / D, EPS, ALU.mult, ALU.add).then_inc(sig("x_ms"), 1)
                dve.wait_ge(sig("x_rstd"), t + 1)
                ts(x_in[:, t, :], x_in[:, t, :], ss[:, t:t + 1], None, ALU.mult).then_inc(sig("xn_ready"), 1)
                if t % 2 == 1:
                    j = t // 2
                    weights.accumulate(nc, dve, link, j, c_silu, acc[:, j // 2, (j % 2) * NC5:(j % 2 + 1) * NC5])
                    nc.vector.engine_nop().then_inc(sig("mod_acc"), 1)
            dve.wait_ge(sig("mod_cols"), 1)
            dve.wait_ge(sig("g1_in"), 16)
            dve.wait_ge(sig("adab_in"), 16)
            link(tt(cols[:], bank[0][:, 0:2 * KT], b_col[:], ALU.add))
            stt(out=cols[:, KT:2 * KT], in0=cols[:, KT:2 * KT], scalar=1.0, in1=g1_col[:], op0=ALU.add, op1=ALU.mult).then_inc(sig("cols_ready"), 1)
            dve.wait_ge(sig("cols_ready"), 1)
            for n in range(2 * KT):
                k, half = n // 2, n % 2
                dve.wait_ge(sig("h_hi"), n + 1)
                if half == 0:
                    if k >= 1:
                        dve.wait_ge(sig("h_lo"), n - 1)
                    ts(full[:, 0, :], bank[1 + n % 4], cols[:, KT + k:KT + k + 1], cols[:, k:k + 1], ALU.mult, ALU.add).then_inc(sig("h_full0"), 1)
                dve.wait_ge(sig(f"h_full{half}"), k + 1)
                part = h_lo[:, k, half * NC5:(half + 1) * NC5]
                tt(part, full[:, (1 + k % 2) if half else 0, :], h_hi[:, k, half * NC5:(half + 1) * NC5].bitcast(F32), ALU.subtract).then_inc(sig("h_lo"), 1)
            dve.wait_ge(sig("h_lo"), 2 * KT)

        @block.scalar
        def _(act):
            act.wait_ge(sig("c_in"), 16)
            nc.scalar.activation(c_silu[:], c_col[:], ACT.Sigmoid).then_inc(sig("c_sig"), 1)
            for t in range(TT):
                act.wait_ge(sig(f"x_in{t}"), 16)
                if t >= 1:
                    act.wait_ge(sig("x_ss"), t)
                nc.scalar.activation(sq[:], x_in[:, t, :], ACT.Square, accum_out=ss[:, t:t + 1]).then_inc(sig("x_ss"), 1)
            act.wait_ge(sig("cols_ready"), 1)
            for n in range(2 * KT):
                k, half = n // 2, n % 2
                act.wait_ge(sig("x_flipped"), n + 1)
                nc.scalar.activation(h_hi[:, k, half * NC5:(half + 1) * NC5], bank[1 + n % 4], ACT.Identity,
                                     scale=cols[:, KT + k:KT + k + 1], bias=cols[:, k:k + 1]).then_inc(sig("h_hi"), 1)
                if half == 1:
                    if k >= 2:
                        act.wait_ge(sig("h_lo"), n - 3)
                    nc.scalar.activation(full[:, 1 + k % 2, :], bank[1 + n % 4], ACT.Identity,
                                         scale=cols[:, KT + k:KT + k + 1], bias=cols[:, k:k + 1]).then_inc(sig("h_full1"), 1)

        @block.tensor
        def _(pe):
            for i in range(2 * KT):
                if i % 4 == 0:
                    pe.wait_ge(sig("mod_acc"), i // 4 + 1)
                last = nc.tensor.matmul(bank[0][:, i:i + 1], acc[:, i // KT, (i % KT) * P:(i % KT + 1) * P], const["ones"][:, 0:1],
                                        start=True, stop=True)
            last.then_inc(sig("mod_cols"), 1)
            pe.wait_ge(sig("xn_ready"), TT)
            for n in range(2 * KT):
                k, half = n // 2, n % 2
                if n >= 4:
                    pe.wait_ge(sig(f"h_full{half}"), (n - 4) // 2 + 1)
                for t in range(HALF):
                    last = nc.tensor.transpose(bank[1 + n % 4][:, t * P:(t + 1) * P],
                                               x_in[:, half * HALF + t, k * P:(k + 1) * P], const["ident"][:])
                last.then_inc(sig("x_flipped"), 1)


def matmul3(nc, out, pairs):
    n = len(pairs)
    for i, ((a_hi, a_lo), (b_hi, b_lo)) in enumerate(pairs):
        nc.tensor.matmul(out, a_hi, b_hi, start=(i == 0), stop=False)
        nc.tensor.matmul(out, a_hi, b_lo, start=False, stop=False)
        last = nc.tensor.matmul(out, a_lo, b_hi, start=False, stop=(i == n - 1))
    return last


def project(nc, sig, bank, const, keep, ins, dram, weights):
    h_hi, h_lo, c_silu, mod_bc, ring, w_f = (keep[n] for n in ("h_hi", "h_lo", "c_silu", "mod_bc", "ring", "w_f"))
    proj = weights.proj
    with ExitStack() as ctx:
        sb = lambda name, shape, dt=F32: ctx.enter_context(nc.sbuf_tensor(name, shape, dt))
        w_hi = sb("w_hi", [P, 2, KT, NC5], F32R)
        w_lo = sb("w_lo", [P, 2, KT, NC5], F32R)
        stage = sb("stage", [P, 3, NC5])
        stage_r = sb("stage_r", [P, 3, 2, NC5], F32R)
        wf_r = sb("wf_r", [P, 2, KT, H], F32R)
        f_b = sb("f_b", [H, 1])
        f_work = sb("f_work", [P, 2, NC5])
        f_abs, f_min = f_work[0:H, 0, :], f_work[0:H, 1, :]
        ncum = sb("ncum_sb", [H, 2, NC5])
        block = ctx.enter_context(nc.Block("project"))
        def mod_dst(j):
            return mod_bc[:, (j - 4) // 2, (j % 2) * NC5:(j % 2 + 1) * NC5]

        def bias_place(j):
            return slice(32 * (j % 4), 32 * (j % 4) + 1), (j - 4) // 4

        SUM_BEFORE = 9

        def bc_bank(i):
            return bank[(0, 1, 6, 7)[i % 4]]

        @block.sync
        def _(sp):
            weights.load(sp, range(6, len(weights.order)))

        @block.gpsimd
        def _(pool):
            pool.dma_start(f_b[:], ins["fox_forget_b"][0].rearrange("(h a) -> h a", a=1)).then_inc(sig("fb_in"), 16)
            pool.dma_start(mod_bc[:, 4, :], ins["norm2_g"].partition_broadcast(P).rearrange("p a n -> p (a n)")).then_inc(sig("g2_in"), 16)
            pool.wait_ge(sig("ncum"), 2)
            for j in range(4, 12):
                row, place = bias_place(j)
                pool.dma_start(f_work[row, place, :], ins["ada_b"][:, j * NC5:(j + 1) * NC5]).then_inc(sig("bias_in"), 16)

        @block.vector
        def _(dve):
            link = Link(dve, sig("dve_link_p"))
            tt, stt, ts = nc.vector.tensor_tensor, nc.vector.scalar_tensor_tensor, nc.vector.tensor_scalar

            def split(j):
                kind, num, src = proj[j]
                i, n = weights.turn[kind, num], src.shape[2]
                dve.wait_ge(sig("w_hi"), j + 1)
                tt(w_lo[:, j % 2, :, 0:n], ring[:, i % 2, :, 0:n], w_hi[:, j % 2, :, 0:n].bitcast(F32), ALU.subtract).then_inc(sig("ring_used"), 1)

            dve.wait_ge(sig("wf_hi"), 1)
            tt(wf_r[:, 1], w_f[:], wf_r[:, 0].bitcast(F32), ALU.subtract).then_inc(sig("wf_lo"), 1)
            split(0)
            weights.accumulate(nc, dve, link, 4, c_silu, mod_dst(4))
            split(1)
            dve.wait_ge(sig("fb_in"), 16)
            for half in range(2):
                dve.wait_ge(sig("f_abs"), half + 1)
                ts(f_min, bank[half][0:H, :], f_b[:], 0.0, ALU.add, ALU.min).then_inc(sig("f_min"), 1)
                dve.wait_ge(sig("f_ln"), half + 1)
                dve.wait_ge(sig("f_min"), half + 1)
                tt(f_min, f_abs, f_min, ALU.subtract).then_inc(sig("f_neg"), 1)
                dve.wait_ge(sig("f_neg"), half + 1)
                nc.vector.tensor_tensor_scan(ncum[:, half, :], const["ones"][0:H, 0:1].to_broadcast([H, NC5]), f_min, ncum[:, 0, NC5 - 1:NC5] if half else 0.0,
                                             ALU.mult, ALU.add).then_inc(sig("ncum"), 1)
                dve.wait_ge(sig("ncum"), half + 1)
            for j in range(len(proj)):
                kind, num, _ = proj[j]
                for i in range(8):
                    fill = 8 * j + i
                    if kind in ("q", "k"):
                        dve.wait_ge(sig("proj_evac"), fill + 1)
                        tt(stage_r[:, fill % 3, 1, :], bank[2 + fill % 4], stage_r[:, fill % 3, 0, :].bitcast(F32), ALU.subtract).then_inc(sig("qk_lo"), 1)
                    if i == 1 and j >= 1 and j + 1 < len(proj):
                        split(j + 1)
                if j < 7:
                    weights.accumulate(nc, dve, link, 5 + j, c_silu, mod_dst(5 + j))
                if j == 7:
                    dve.wait_ge(sig("bias_in"), 16 * 8)
                    for m in range(4, 12):
                        row, place = bias_place(m)
                        tt(mod_dst(m)[row, :], mod_dst(m)[row, :], f_work[row, place, :], ALU.add).then_inc(sig("mod_biased"), 1)
            dve.wait_ge(sig("g2_in"), 16)
            dve.wait_ge(sig("bc_evac"), 8)
            stt(out=mod_bc[:, 2, :], in0=mod_bc[:, 2, :], scalar=1.0, in1=mod_bc[:, 4, :],
                op0=ALU.add, op1=ALU.mult).then_inc(sig("a2_ready"), 1)
            dve.wait_ge(sig("a2_ready"), 1)

        @block.scalar
        def _(act):
            def high(j):
                kind, num, src = proj[j]
                i, n = weights.turn[kind, num], src.shape[2]
                weights.arrived(act, i)
                if j >= 2:
                    act.wait_ge(sig("proj_full"), 8 * (j - 1))
                nc.scalar.activation(w_hi[:, j % 2, :, 0:n], ring[:, i % 2, :, 0:n], ACT.Copy).then_inc(sig("w_hi"), 1)

            nc.scalar.activation(wf_r[:, 0], w_f[:], ACT.Copy).then_inc(sig("wf_hi"), 1)
            high(0)
            high(1)
            act.wait_ge(sig("fb_in"), 16)
            for half in range(2):
                act.wait_ge(sig("f_full"), half + 1)
                if half:
                    act.wait_ge(sig("f_neg"), 1)
                nc.scalar.activation(f_abs, bank[half][0:H, :], ACT.Abs, bias=f_b[:]).then_inc(sig("f_abs"), 1)
                act.wait_ge(sig("f_abs"), half + 1)
                nc.scalar.activation(f_abs, f_abs, ACT.Exp, scale=-1.0).then_inc(sig("f_exp"), 1)
                act.wait_ge(sig("f_exp"), half + 1)
                nc.scalar.activation(f_abs, f_abs, ACT.Ln, bias=1.0).then_inc(sig("f_ln"), 1)
            act.wait_ge(sig("ncum"), 2)
            act.dma_start(dram["ncum"], ncum[:].rearrange("h a s -> h (a s)")).then_inc(sig("ncum_out"), 16)
            staged, out3 = 0, [0, 0, 0]
            for j, (kind, num, src) in enumerate(proj):
                n = src.shape[2]
                if j == SUM_BEFORE:
                    for i in range(8):
                        act.wait_ge(sig("bc_full"), i + 1)
                        nc.scalar.activation(mod_dst(4 + i), bc_bank(i), ACT.Copy).then_inc(sig("bc_evac"), 1)
                for i in range(8):
                    fill = 8 * j + i
                    ps = bank[2 + fill % 4]
                    act.wait_ge(sig("proj_full"), fill + 1)
                    if kind in ("q", "k"):
                        if fill >= 3:
                            act.wait_ge(sig(f"qk_out{fill % 3}"), 16 * (fill // 3))
                        nc.scalar.activation(stage_r[:, fill % 3, 0, :], ps, ACT.Copy).then_inc(sig("proj_evac"), 1)
                        act.wait_ge(sig("qk_lo"), fill + 1)
                        dst = dram["qk"][j, :, (i // 2) * P:(i // 2 + 1) * P, (i % 2) * NC5:(i % 2 + 1) * NC5]
                        act.dma_start(dst.rearrange("a p n -> p a n"), stage_r[:, fill % 3].bitcast(F32)).then_inc(sig(f"qk_out{fill % 3}"), 16)
                    else:
                        b = staged % 3
                        if staged >= 3:
                            act.wait_ge(sig(f"staged_out{b}"), 16 * (staged // 3))
                        nc.scalar.activation(stage[:, b, 0:n], ps[:, 0:n], ACT.Sigmoid if kind == "gate" else ACT.Copy).then_inc(sig("proj_evac"), 1)
                        act.wait_ge(sig("proj_evac"), fill + 1)
                        rows = slice(i * P, (i + 1) * P)
                        dst = {"v": lambda: dram["v"][rows, :],
                               "rwkv": lambda: dram["p_rwkv"][1 + i * P:1 + (i + 1) * P, num * NC5:num * NC5 + n],
                               "gate": lambda: dram["gates"][rows, num * NC5:num * NC5 + n]}[kind]()
                        act.dma_start(dst, stage[:, b, 0:n]).then_inc(sig(f"staged_out{b}"), 16)
                        staged += 1
                    if i == 1 and j >= 1 and j + 1 < len(proj):
                        high(j + 1)
            for b in range(3):
                act.wait_ge(sig(f"staged_out{b}"), 16 * ((staged + 2 - b) // 3))
                act.wait_ge(sig(f"qk_out{b}"), 16 * ((16 + 2 - b) // 3))
            act.wait_ge(sig("ncum_out"), 16)

        @block.tensor
        def _(pe):
            pe.wait_ge(sig("wf_lo"), 1)
            for half in range(2):
                tok = slice(half * NC5, (half + 1) * NC5)
                matmul3(nc, bank[half][0:H, :], [((wf_r[:, 0, k, :], wf_r[:, 1, k, :]), (h_hi[:, k, tok], h_lo[:, k, tok]))
                                                 for k in range(KT)]).then_inc(sig("f_full"), 1)
            for j, (kind, num, src) in enumerate(proj):
                n = src.shape[2]
                if j == SUM_BEFORE:
                    pe.wait_ge(sig("mod_biased"), 8)
                    for i in range(8):
                        if i >= 4:
                            pe.wait_ge(sig("bc_evac"), i - 3)
                        nc.tensor.matmul(bc_bank(i), const["ones"][:], mod_dst(4 + i), start=True, stop=True).then_inc(sig("bc_full"), 1)
                pe.wait_ge(sig("ring_used"), weights.turn[kind, num] + 1)
                for i in range(8):
                    fill = 8 * j + i
                    if fill >= 4:
                        pe.wait_ge(sig("proj_evac"), fill - 3)
                        if fill - 4 < 16:
                            pe.wait_ge(sig("qk_lo"), fill - 3)
                    ps = bank[2 + fill % 4]
                    if kind in ("q", "k"):
                        f, tok = slice((i // 2) * P, (i // 2 + 1) * P), slice((i % 2) * NC5, (i % 2 + 1) * NC5)
                        pairs = [((w_hi[:, j % 2, k, f], w_lo[:, j % 2, k, f]), (h_hi[:, k, tok], h_lo[:, k, tok])) for k in range(KT)]
                    else:
                        tok = slice(i * P, (i + 1) * P)
                        pairs = [((h_hi[:, k, tok], h_lo[:, k, tok]), (w_hi[:, j % 2, k, 0:n], w_lo[:, j % 2, k, 0:n])) for k in range(KT)]
                    matmul3(nc, ps[:, 0:n], pairs).then_inc(sig("proj_full"), 1)


def attend(nc, sig, bank, const, keep, ins, dram, ready):
    psum = const["psum"]
    PLACES = 4
    items = [(h, half * TT // 2 + t) for h in range(H) for t in range(TT // 2) for half in range(2)]
    with ExitStack() as ctx:
        sb = lambda name, shape, dt=F32: ctx.enter_context(nc.sbuf_tensor(name, shape, dt))
        causal = sb("causal", [P, P])
        gate_bias = sb("gate_bias", [P, 2, S])
        q2 = sb("q2", [P, 2, S], F32R)
        k2 = sb("k2", [P, 2, 2, S], F32R)
        v_h = sb("v_h", [P, 2, TT, HD])
        logits = sb("att_logits", [P, 2, S])
        probs = sb("att_probs", [P, PLACES, S])
        probs_t = sb("att_probs_t", [P, 2, S])
        o_t = sb("att_o_t", [HD, 2, S])
        neg_max = sb("neg_max", [P, len(items)])
        row_sum = sb("row_sum", [P, len(items)])
        block = ctx.enter_context(nc.Block("attend"))

        def scores(n):
            return psum[:, (n % 2) * 2 * NC5:(n % 2 + 1) * 2 * NC5]

        @block.sync
        def _(sp):
            def store(h):
                sp.wait_ge(sig("o_t"), 2 * (h + 1))
                sp.dma_start(dram["o_fox_t"][h * HD:(h + 1) * HD, :], o_t[:, h % 2, :]).then_inc(sig(f"o_t_out{h % 2}"), 16)

            for h in range(H):
                b = h % 2
                if h >= 2:
                    sp.wait_ge(sig("mixed"), TT * (h - 1))
                rows = slice(h * HD, (h + 1) * HD)
                for part in range(2):
                    half = slice(part * HD, (part + 1) * HD)
                    sp.dma_start(q2[half, b, :].bitcast(F32), dram["qk"][0, part, rows, :]).then_inc(sig(f"head_in{b}"), 16)
                    for copy in range(2):
                        sp.dma_start(k2[copy * HD:(copy + 1) * HD, b, part, :].bitcast(F32), dram["qk"][1, part, rows, :]).then_inc(sig(f"head_in{b}"), 16)
                sp.dma_start(v_h[:, b], dram["v"][:, rows].rearrange("(t p) d -> p t d", p=P)).then_inc(sig(f"head_in{b}"), 16)
                sp.dma_start(gate_bias[:, b, :], dram["ncum"][h:h + 1, :].partition_broadcast(P).rearrange("p a n -> p (a n)")).then_inc(sig(f"head_in{b}"), 16)
                if h >= 2:
                    store(h - 2)
                if h == 1:
                    load_recur(sp, sig, ready, ins, dram)
            store(H - 2)
            store(H - 1)
            for b in range(2):
                sp.wait_ge(sig(f"o_t_out{b}"), 16 * H // 2)

        def head_here(eng, h):
            eng.wait_ge(sig(f"head_in{h % 2}"), 16 * 8 * (h // 2 + 1))

        @block.gpsimd
        def _(pool):
            nc.gpsimd.memset(causal[:], 0.0).then_inc(sig("att_const"), 1)
            pool.wait_ge(sig("att_const"), 1)
            nc.gpsimd.affine_select(out=causal[:], in_=causal[:], compare_op=ALU.is_ge, fill=NEG, base=0,
                                    pattern=[[-1, P]], channel_multiplier=1).then_inc(sig("att_const"), 1)
            pool.wait_ge(sig("att_const"), 2)
            prepare_recur(nc, pool, sig, ready, ins)

        @block.tensor
        def _(pe):
            def score(n):
                h, t = items[n]
                if n % TT == 0:
                    head_here(pe, h)
                if n >= 2:
                    pe.wait_ge(sig("scores_read"), n - 1)
                for lo in range(0, (t + 1) * P, NC5):
                    hi = max(min(lo + NC5, (t + 1) * P), lo + 2 * P)
                    for part in range(2):
                        last = nc.tensor.matmul(scores(n)[:, lo:hi], q2[:, h % 2, t * P:(t + 1) * P], k2[:, h % 2, part, lo:hi],
                                                start=(part == 0), stop=(part == 1))
                last.then_inc(sig("scores_full"), 1)

            def flip(n):
                h, t = items[n]
                pe.wait_ge(sig("probs_scaled"), n + 1)
                if n >= 1:
                    pe.wait_ge(sig("probs_t"), n)
                for k in range(t + 1):
                    last = nc.tensor.transpose(psum[:, 4 * NC5 + k * P:4 * NC5 + (k + 1) * P],
                                               probs[:, n % PLACES, k * P:(k + 1) * P], const["ident"][:])
                last.then_inc(sig("flipped"), 1)

            def mix(n):
                h, t = items[n]
                pe.wait_ge(sig("probs_t"), n + 1)
                if n >= 8 and t % 4 == 0:
                    pe.wait_ge(sig("o_t"), 2 * (h - 1) + t // 4 + 1)
                for k in range(t + 1):
                    last = nc.tensor.matmul(bank[6 + t // 4][0:HD, (t % 4) * P:(t % 4 + 1) * P], v_h[:, h % 2, k, :],
                                            probs_t[:, n % 2, k * P:(k + 1) * P], start=(k == 0), stop=(k == t))
                last.then_inc(sig("mixed"), 1)

            score(0)
            for n in range(len(items) + 3):
                if n + 1 < len(items):
                    score(n + 1)
                if 2 <= n <= len(items) + 1:
                    flip(n - 2)
                if n >= 3:
                    mix(n - 3)

        @block.scalar
        def _(act):
            def evacuate(n):
                cols = (items[n][1] + 1) * P
                act.wait_ge(sig("flipped"), n + 1)
                if n >= 2:
                    act.wait_ge(sig("mixed"), n - 1)
                nc.scalar.activation(probs_t[:, n % 2, 0:cols], psum[:, 4 * NC5:4 * NC5 + cols], ACT.Copy).then_inc(sig("probs_t"), 1)

            def scale(n):
                cols = (items[n][1] + 1) * P
                act.wait_ge(sig("row_scale"), n + 1)
                p = probs[:, n % PLACES, 0:cols]
                nc.scalar.activation(p, p, ACT.Copy, scale=row_sum[:, n:n + 1]).then_inc(sig("probs_scaled"), 1)

            for n in range(len(items) + 2):
                if n < len(items):
                    act.wait_ge(sig("neg_max"), n + 1)
                    if n >= PLACES:
                        act.wait_ge(sig("flipped"), n - PLACES + 1)
                    cols = (items[n][1] + 1) * P
                    nc.scalar.activation(probs[:, n % PLACES, 0:cols], logits[:, n % 2, 0:cols], ACT.Exp,
                                         bias=neg_max[:, n:n + 1], accum_out=row_sum[:, n:n + 1]).then_inc(sig("probs"), 1)
                if 1 <= n <= len(items):
                    scale(n - 1)
                if n >= 2:
                    evacuate(n - 2)

        @block.vector
        def _(dve):
            def scale(n):
                dve.wait_ge(sig("probs"), n + 1)
                nc.vector.reciprocal(row_sum[:, n:n + 1], row_sum[:, n:n + 1]).then_inc(sig("row_scale"), 1)

            def finish(m):
                h, half = m // 2, m % 2
                dve.wait_ge(sig("mixed"), TT * (h + 1) - 1 + half)
                if h >= 2 and half == 0:
                    dve.wait_ge(sig(f"o_t_out{h % 2}"), 16 * (h // 2))
                nc.vector.tensor_copy(o_t[:, h % 2, half * NC5:(half + 1) * NC5], bank[6 + half][0:HD, :]).then_inc(sig("o_t"), 1)

            dve.wait_ge(sig("att_const"), 2)
            for n, (h, t) in enumerate(items):
                cols = (t + 1) * P
                lg = logits[:, n % 2, :]
                dve.wait_ge(sig("scores_full"), n + 1)
                if n % TT == 0:
                    head_here(dve, h)
                if n >= 2:
                    dve.wait_ge(sig("probs"), n - 1)
                nc.vector.scalar_tensor_tensor(out=lg[:, 0:cols], in0=scores(n)[:, 0:cols], scalar=HD ** -0.5,
                                               in1=gate_bias[:, h % 2, 0:cols], op0=ALU.mult, op1=ALU.add).then_inc(sig("scores_read"), 1)
                dve.wait_ge(sig("scores_read"), n + 1)
                nc.vector.tensor_tensor(lg[:, t * P:cols], lg[:, t * P:cols], causal[:], ALU.add).then_inc(sig("masked"), 1)
                dve.wait_ge(sig("masked"), n + 1)
                nc.vector.tensor_reduce(neg_max[:, n:n + 1], lg[:, 0:cols], AX.X, ALU.max, negate=True).then_inc(sig("neg_max"), 1)
                if n >= 1:
                    scale(n - 1)
                if n > TT and n % TT in (2, 3):
                    finish(2 * (h - 1) + n % TT - 2)
            scale(len(items) - 1)
            finish(2 * H - 2)
            finish(2 * H - 1)


RECUR_ROWS = ["rwkv_w0", "rwkv_a0", "rwkv_k_k", "rwkv_k_a", "rwkv_r_k", "ln_x_g", "ln_x_b"]


def recur_buffers(nc, ctx, raw):
    flat = raw[:].rearrange("p k n -> p (k n)")
    ends = np.cumsum([0, 2 * SHIFT, SHIFT, SHIFT, 2 * W])
    cur, prev, mu_bc, lora_w = (flat[:, int(a):int(b)] for a, b in zip(ends, ends[1:]))
    sb = lambda name, shape: ctx.enter_context(nc.sbuf_tensor(name, shape, F32))
    return {
        "cur": cur.rearrange("p (b n) -> p b n", b=2),
        "prev": prev,
        "mu_bc": mu_bc,
        "lora_w": lora_w.rearrange("p (a n) -> p a n", a=2),
        "rows": sb("rw_rows", [P, len(RECUR_ROWS), W]),
        "gate_w": sb("gate_w", [P, W]),
        "in_chunk": sb("in_chunk", [P, 2]),
        "tri": sb("tri", [P, 2, P]),
        "off_t": sb("off_t", [P, 6, P]),
        "v_m": sb("v_m", [P, 2, 2, W]),
        "fm_bk": sb("fm_bk", [P, H, 2, P]),
        "sa": sb("sa", [P, 2, W]),
        "state": sb("state", [P, 2, H // 2, P]),
    }


def load_recur(sp, sig, ready, ins, dram):
    sp.dma_start(ready["cur"][:, 0, :], dram["p_rwkv"][1:1 + P, :]).then_inc(sig("cur_in"), 16)
    sp.dma_start(ready["prev"][:], dram["p_rwkv"][0:P, :]).then_inc(sig("prev_in"), 16)
    for i, n in enumerate(RECUR_ROWS):
        src = ins[n] if n != "rwkv_r_k" else ins[n].rearrange("l h d -> l (h d)")
        sp.dma_start(ready["rows"][:, i, :], src.partition_broadcast(P).rearrange("p a n -> p (a n)")).then_inc(sig("rows_in"), 16)
    sp.dma_start(ready["lora_w"][0:LORA, 0, :], ins["rwkv_w2"][0]).then_inc(sig("rows_in"), 16)
    sp.dma_start(ready["lora_w"][LORA:2 * LORA, 1, :], ins["rwkv_a2"][0]).then_inc(sig("rows_in"), 16)
    sp.dma_start(ready["gate_w"][:], ins["rwkv_g2"][0]).then_inc(sig("rows_in"), 16)


def prepare_recur(nc, pool, sig, ready, ins):
    link = Link(pool, sig("pool_link_a"))
    tri, off_t, in_chunk, lora_w = (ready[n] for n in ("tri", "off_t", "in_chunk", "lora_w"))

    def select(ap, pattern, cm, base, op):
        link(nc.gpsimd.affine_select(out=ap, in_=ap, compare_op=op, fill=0.0, base=base,
                                     pattern=pattern, channel_multiplier=cm))

    pool.dma_start(ready["mu_bc"][:], ins["shift_mu"].partition_broadcast(P).rearrange("p a n -> p (a n)")).then_inc(sig("mu_in"), 16)
    link(nc.gpsimd.memset(lora_w[LORA:2 * LORA, 0, :], 0.0))
    link(nc.gpsimd.memset(lora_w[0:LORA, 1, :], 0.0))
    for m in (tri, off_t, in_chunk):
        link(nc.gpsimd.memset(m[:], 1.0))
    for n in ("v_m", "fm_bk", "sa", "state"):
        link(nc.gpsimd.memset(ready[n][:], 0.0))
    select(in_chunk[:], [[-CHUNK, 2]], 1, 0, ALU.is_ge)
    select(in_chunk[:], [[CHUNK, 2]], -1, CHUNK - 1, ALU.is_ge)
    for i in range(2):
        m = tri[:, i, :].rearrange("p (c t) -> p c t", c=2)
        select(m, [[-CHUNK, 2], [0, CHUNK]], 1, 0, ALU.is_ge)
        select(m, [[CHUNK, 2], [0, CHUNK]], -1, CHUNK - 1, ALU.is_ge)
        select(m, [[CHUNK, 2], [1, CHUNK]], -1, 0, ALU.is_ge if i else ALU.is_gt)
    for i in range(6):
        n = 1 << i
        m = off_t[:, i, :].rearrange("p (b u v) -> p b u v", u=2, v=n)
        select(m, [[0, P // (2 * n)], [1, 2], [0, n]], 0, -1, ALU.is_ge)
        select(m, [[-2 * n, P // (2 * n)], [0, 2], [0, n]], 1, 0, ALU.is_ge)
        select(m, [[2 * n, P // (2 * n)], [0, 2], [0, n]], -1, n - 1, ALU.is_ge)
    pool.wait_ge(sig("mu_in"), 16)
    pool.wait_ge(sig("cur_in"), 16)
    pool.wait_ge(sig("prev_in"), 16)
    token_shift(nc, link, ready["cur"][:, 0, :], ready["prev"], ready["mu_bc"])
    pool.wait_ge(sig("rows_in"), 16 * (len(RECUR_ROWS) + 3))


def token_shift(nc, link, cur, prev, mu_bc):
    link(nc.gpsimd.tensor_tensor(prev[:], prev[:], cur, ALU.subtract))
    link(nc.gpsimd.tensor_tensor(prev[:], prev[:], mu_bc[:], ALU.mult))
    link(nc.gpsimd.tensor_tensor(cur, cur, prev[:], ALU.add))


def recur(nc, sig, bank, const, keep, ins, ready, raw, dram):
    ident = const["ident"]
    LEVELS = 5
    PAIRS = H // 2
    with ExitStack() as ctx:
        sb = lambda name, shape: ctx.enter_context(nc.sbuf_tensor(name, shape, F32))
        cur, prev, mu_bc, rows, lora_w, gate_w, in_chunk, tri, off_t = (
            ready[n] for n in ("cur", "prev", "mu_bc", "rows", "lora_w", "gate_w", "in_chunk", "tri", "off_t"))
        v_m, fm_bk, sa, state = (ready[n] for n in ("v_m", "fm_bk", "sa", "state"))
        w0, a0, k_k, k_a, r_k, ln_g, ln_b = (rows[:, i, :] for i in range(len(RECUR_ROWS)))
        lora = sb("lora", [P, 2 * P])
        lora_t = sb("lora_t", [P, 2 * P])
        gate = sb("rw_gate", [P, 2, W])
        sw = sb("sw", [P, W])
        aa = sb("aa", [P, W])
        p_in = sb("p_in", [P, W])
        p_inv = sb("p_inv", [P, W])
        p_ex = sb("p_ex", [P, W])
        p_end = sb("p_end", [P, 3, PAIRS, 2])
        kk = sb("kk", [P, W])
        kp = sb("kp", [P, W])
        tmp = sb("rw_tmp", [P, W])
        norm_k = sb("norm_k", [P, H])
        norm_y = sb("norm_y", [P, H])
        bonus = sb("bonus", [P, H])
        bonus_v = sb("bonus_v", [P, 3, W])
        tm = sb("tm", [P, 2, 4, W])
        fm_ar = sb("fm_ar", [P, 2, PAIRS, 2, P])
        gram_a = sb("gram_a", [P, H, 2, P])
        gram_r = sb("gram_r", [P, 2, H, 2, P])
        inv = sb("inv", [P, H, P])
        inv_t = sb("inv_t", [P, 2, H, P])
        a_off = sb("a_off", [P, 2, H, P])
        grow = sb("grow", [P, H, P])
        xv = keep["mod_bc"][:, 4, :].rearrange("p (b n) -> p b n", b=2)
        w_t = sb("w_t", [P, PAIRS, P])
        y = sb("rw_y", [P, 2, W])
        block = ctx.enter_context(nc.Block("recur"))

        def heads(ap, n=HD):
            return ap.rearrange("p (h d) -> p h d", d=n)

        def head(h):
            return slice(h * HD, (h + 1) * HD)

        def pair(j):
            return slice(j * P, (j + 1) * P)

        def tokens(ch):
            return slice(ch * CHUNK, (ch + 1) * CHUNK)

        def at(t, *pieces):
            if 0 <= t < TT:
                for piece in pieces:
                    piece(t)

        @block.sync
        def _(sp):
            def load(t):
                if t >= 2:
                    sp.wait_ge(sig("tm"), 4 * (t - 1))
                    sp.wait_ge(sig("v_m"), t - 1)
                sp.dma_start(cur[:, t % 2, :], dram["p_rwkv"][1 + t * P:1 + (t + 1) * P, :]).then_inc(sig(f"cur_in{t % 2}"), 16)
                if t >= 2:
                    sp.wait_ge(sig("shifted"), t - 1)
                sp.dma_start(prev[:], dram["p_rwkv"][t * P:(t + 1) * P, :]).then_inc(sig("prev_in"), 16)

            def store(t):
                sp.wait_ge(sig("tile_done"), t + 1)
                sp.dma_start(dram["o_rwkv"][t * P:(t + 1) * P, :], y[:, t % 2, :]).then_inc(sig(f"o_out{t % 2}"), 16)

            load(1)
            for t in range(TT + 1):
                at(t + 2, load)
                if t == TT:
                    sp.wait_ge(sig("shifted"), TT - 1)
                    sp.wait_ge(sig("tm"), 4 * TT)
                    sp.wait_ge(sig("v_m"), TT)
                    sp.wait_ge(sig("a_full"), TT)
                    load_rows(sp, sig, raw, 0, ins["w_out_fox"][0])
                    load_rows(sp, sig, raw, W // P, ins["w_out_rwkv"][0])
                at(t - 1, store)
            for b in range(2):
                sp.wait_ge(sig(f"o_out{b}"), 16 * TT // 2)

        @block.gpsimd
        def _(pool):
            link = Link(pool, sig("pool_link_r"))

            def shift(t):
                pool.wait_ge(sig(f"cur_in{t % 2}"), 16 * ((t + 1) // 2))
                pool.wait_ge(sig("prev_in"), 16 * t)
                token_shift(nc, link, cur[:, t % 2, :], prev, mu_bc)
                nc.gpsimd.nop().then_inc(sig("shifted"), 1)

            def part_v(t):
                if t >= 1:
                    pool.wait_ge(sig("shifted"), t)
                if t >= 2:
                    pool.wait_ge(sig("y_sum"), t - 1)
                c = cur[:, t % 2, 2 * W:3 * W]
                link(nc.gpsimd.tensor_copy(v_m[tokens(0), t % 2, 0, :], c[tokens(0), :]))
                nc.gpsimd.tensor_copy(v_m[tokens(1), t % 2, 1, :], c[tokens(1), :]).then_inc(sig("v_m"), 1)
                pool.wait_ge(sig("v_m"), t + 1)

            def key_norm(t):
                pool.wait_ge(sig("kk_ss"), t + 1)
                nc.gpsimd.tensor_tensor(norm_k[:], norm_k[:], const["neghalf"][:], ALU.pow).then_inc(sig("kk_rn"), 1)

            def y_norm(t):
                pool.wait_ge(sig("y_var"), t + 1)
                nc.gpsimd.tensor_tensor(norm_y[:], norm_y[:], const["neghalf"][:], ALU.pow).then_inc(sig("y_rstd"), 1)

            def y_gate(t):
                yt = y[:, t % 2, :]
                pool.wait_ge(sig("y_scaled"), t + 1)
                link(nc.gpsimd.tensor_tensor(yt, yt, bonus_v[:, t % 3, :], ALU.add))
                pool.wait_ge(sig("gate"), t + 1)
                nc.gpsimd.tensor_tensor(yt, yt, gate[:, t % 2, :], ALU.mult).then_inc(sig("tile_done"), 1)

            def off(i):
                def piece(t):
                    n = LEVELS * t + i
                    for g in range(2):
                        if i == 0:
                            pool.wait_ge(sig("gram"), 2 * (H * t + 4 * (g + 1)))
                        if n >= 2:
                            pool.wait_ge(sig("grow_full"), 2 * (n - 2) + g + 1)
                        hs = slice(4 * g, 4 * g + 4)
                        nc.gpsimd.tensor_tensor(a_off[:, n % 2, hs], gram_a[:, hs, 0, :],
                                                off_t[:, i + 1, :].unsqueeze(1).to_broadcast([P, 4, P]), ALU.mult).then_inc(sig("a_off"), 1)
                return piece

            for t in range(-1, TT + 1):
                at(t, off(1))
                at(t + 1, key_norm)
                at(t, off(2), off(3), off(4))
                at(t + 2, shift)
                at(t - 1, y_norm)
                at(t + 1, part_v)
                at(t - 1, y_gate)
                at(t + 1, off(0))

        @block.scalar
        def _(act):
            def copy(out, ps, name):
                nc.scalar.activation(out, ps, ACT.Copy).then_inc(sig(name), 1)

            def lora_in(t):
                c = cur[:, t % 2, :]
                if t >= 1:
                    act.wait_ge(sig("shifted"), t)
                nc.scalar.activation(lora[:, 0:LORA], c[:, 3 * W:3 * W + LORA], ACT.Tanh).then_inc(sig("lora"), 1)
                copy(lora[:, LORA:2 * LORA], c[:, 3 * W + LORA:3 * W + 2 * LORA], "lora")
                nc.scalar.activation(lora[:, P:2 * P], c[:, 3 * W + 2 * LORA:SHIFT], ACT.Tanh, scale=0.5).then_inc(sig("lora"), 1)

            def lora_flipped(t):
                act.wait_ge(sig("lora_flipped"), t + 1)
                copy(lora_t[:], bank[4][:, 0:2 * P], "lora_t")

            def decay_tanh(t):
                act.wait_ge(sig("z_biased"), t + 1)
                nc.scalar.activation(sw[:], sw[:], ACT.Tanh, scale=0.5).then_inc(sig("z_tanh"), 1)

            def rate_tanh(t):
                act.wait_ge(sig("a_biased"), t + 1)
                nc.scalar.activation(aa[:], aa[:], ACT.Tanh, scale=0.5).then_inc(sig("a_tanh"), 1)

            def decays(t):
                act.wait_ge(sig("sum_in_full"), t + 1)
                nc.scalar.activation(p_in[:], bank[4], ACT.Exp, scale=-EXPM05).then_inc(sig("p_in"), 1)
                nc.scalar.activation(p_inv[:], bank[4], ACT.Exp, scale=EXPM05).then_inc(sig("p_inv"), 1)
                act.wait_ge(sig("sum_ex_full"), t + 1)
                nc.scalar.activation(p_ex[:], bank[5], ACT.Exp, scale=-EXPM05).then_inc(sig("p_ex"), 1)

            def chunk_decay(t):
                act.wait_ge(sig("sum_end_full"), t + 1)
                if t >= 3:
                    act.wait_ge(sig("state"), 2 * (t - 2))
                nc.scalar.activation(p_end[:, t % 3].rearrange("p j c -> p (j c)"), bank[4][:, 0:2 * PAIRS], ACT.Exp,
                                     scale=-EXPM05).then_inc(sig("p_end"), 1)

            def flipped(j):
                def piece(t):
                    ps = bank[4 + j % 2]
                    act.wait_ge(sig("fm_full"), PAIRS * t + j + 1)
                    copy(fm_ar[:, t % 2, j].rearrange("p a t -> p (a t)"), ps[:, 0:2 * P], "fm")
                    for h in range(2):
                        rows_h = slice(h * HD, (h + 1) * HD)
                        copy(fm_bk[rows_h, 2 * j + h].rearrange("p a t -> p (a t)"), ps[rows_h, 2 * P:4 * P], "fm")
                return piece

            def first(g):
                def piece(t):
                    act.wait_ge(sig("first_full"), 2 * t + g + 1)
                    copy(inv[:, 4 * g:4 * g + 4].rearrange("p h s -> p (h s)"), bank[4 + g], "first")
                return piece

            def grown(i, g):
                def piece(t):
                    hs = slice(4 * g, 4 * g + 4)
                    act.wait_ge(sig("inv_full"), 2 * (LEVELS * t + i) + g + 1)
                    if i < LEVELS - 1:
                        copy(inv[:, hs].rearrange("p h s -> p (h s)"), bank[2 + g], "inv")
                    else:
                        copy(inv_t[:, t % 2, hs].rearrange("p h s -> p (h s)"), bank[2 + g], "inv_t")
                return piece

            def turned(i):
                def piece(t):
                    for g in range(2):
                        act.wait_ge(sig("turned_full"), 2 * ((LEVELS - 1) * t + i) + g + 1)
                        copy(inv_t[:, t % 2, 4 * g:4 * g + 4].rearrange("p h s -> p (h s)"), bank[2 + g], "inv_t")
                return piece

            def keys_v(t):
                act.wait_ge(sig("xv_full"), t + 1)
                copy(xv[:, t % 2, :], bank[5], "xv")

            def gates(t):
                act.wait_ge(sig("g_full"), t + 1)
                if t >= 2:
                    act.wait_ge(sig("tile_done"), t - 1)
                copy(gate[:, t % 2, :], bank[4], "gate")

            def read_w(t):
                act.wait_ge(sig("w_full"), t + 1)
                copy(w_t[:].rearrange("p j t -> p (j t)"), bank[7], "w_t")

            def read_y(t):
                act.wait_ge(sig("y_full"), 2 * (t + 1))
                if t >= 2:
                    act.wait_ge(sig(f"o_out{t % 2}"), 16 * (t // 2))
                copy(y[:, t % 2, :], bank[6], "y_sum")

            def read_sa(ch):
                def piece(t):
                    act.wait_ge(sig("sa_full"), 2 * t + ch + 1)
                    copy(sa[tokens(ch), ch, :], bank[7][tokens(ch), :], "sa")
                return piece

            for t in range(-1, TT + 1):
                at(t + 1, lora_in)
                at(t - 1, read_w)
                at(t, first(1))
                at(t + 1, lora_flipped)
                at(t, grown(0, 0))
                at(t - 1, read_sa(0))
                at(t + 1, decay_tanh)
                at(t, grown(0, 1))
                at(t + 1, rate_tanh)
                at(t, turned(0), grown(1, 0))
                at(t + 1, decays)
                at(t, grown(1, 1))
                at(t - 1, read_sa(1))
                at(t, turned(1), grown(2, 0))
                at(t + 1, chunk_decay)
                at(t, grown(2, 1))
                at(t - 1, read_y)
                at(t, turned(2))
                at(t + 1, flipped(0), flipped(1))
                at(t, grown(3, 0))
                at(t + 1, flipped(2), flipped(3))
                at(t, grown(3, 1), turned(3), grown(4, 0), grown(4, 1))
                at(t + 1, first(0), keys_v, gates)

        @block.tensor
        def _(pe):
            mm = nc.tensor.matmul

            def flip_lora(t):
                pe.wait_ge(sig("lora"), 3 * (t + 1))
                pe.wait_ge(sig("lora_sig"), t + 1)
                if t >= 1:
                    pe.wait_ge(sig("gate"), t)
                for i in range(2):
                    last = nc.tensor.transpose(bank[4][:, i * P:(i + 1) * P], lora[:, i * P:(i + 1) * P], ident[:])
                last.then_inc(sig("lora_flipped"), 1)

            def decay_logit(t):
                if t >= 1:
                    pe.wait_ge(sig("first"), 2 * t)
                pe.wait_ge(sig("lora_t"), t + 1)
                mm(bank[5], lora_t[:, 0:P], lora_w[:, 0, :], start=True, stop=True).then_inc(sig("z_full"), 1)

            def rate_logit(t):
                mm(bank[4], lora_t[:, 0:P], lora_w[:, 1, :], start=True, stop=True).then_inc(sig("a_full"), 1)

            def decay_sums(t):
                pe.wait_ge(sig("sw"), t + 1)
                pe.wait_ge(sig("a_biased"), t + 1)
                mm(bank[4], tri[:, 1, :], sw[:], start=True, stop=True).then_inc(sig("sum_in_full"), 1)
                mm(bank[5], tri[:, 0, :], sw[:], start=True, stop=True).then_inc(sig("sum_ex_full"), 1)

            def chunk_sums(t):
                pe.wait_ge(sig("p_in"), t + 1)
                pe.wait_ge(sig("p_inv"), t + 1)
                for j in range(PAIRS):
                    last = mm(bank[4][:, 2 * j:2 * j + 2], sw[:, pair(j)], in_chunk[:], start=True, stop=True)
                last.then_inc(sig("sum_end_full"), 1)

            def flip(j):
                def piece(t):
                    if j == 0:
                        pe.wait_ge(sig("tm"), 4 * (t + 1))
                        pe.wait_ge(sig("p_end"), t + 1)
                        pe.wait_ge(sig("p_ex"), t + 1)
                    if j >= 2:
                        pe.wait_ge(sig("fm"), 3 * (PAIRS * t + j - 1))
                    for i in range(4):
                        last = nc.tensor.transpose(bank[4 + j % 2][:, i * P:(i + 1) * P], tm[:, t % 2, i, pair(j)], ident[:])
                    last.then_inc(sig("fm_full"), 1)
                return piece

            def products(h):
                def piece(t):
                    if h == 0:
                        pe.wait_ge(sig("fm"), 3 * (PAIRS * t + 3))
                    elif h == 1:
                        pe.wait_ge(sig("fm"), 3 * PAIRS * (t + 1))
                    else:
                        pe.wait_ge(sig("gram"), 2 * (H * t + h - 1))
                    ar = fm_ar[:, t % 2, h // 2].rearrange("p a t -> p (a t)")
                    ps = bank[4 + h % 2]
                    mm(ps[:, 0:2 * P], fm_bk[:, h, 0, :], ar, start=True, stop=True)
                    mm(ps[:, 2 * P:4 * P], fm_bk[:, h, 1, :], ar, start=True, stop=True).then_inc(sig("gram_full"), 1)
                return piece

            def first(g):
                def piece(t):
                    pe.wait_ge(sig("inv_first"), 2 * t + g + 1)
                    if g == 0:
                        pe.wait_ge(sig("gram"), 2 * (H * (t + 1) - 1))
                    else:
                        pe.wait_ge(sig("xv"), t + 1)
                    for h in range(4):
                        last = nc.tensor.transpose(bank[4 + g][:, h * P:(h + 1) * P], inv_t[:, t % 2, 4 * g + h, :], ident[:])
                    last.then_inc(sig("first_full"), 1)
                return piece

            def keys_v(t):
                pe.wait_ge(sig("gram"), 2 * H * (t + 1))
                pe.wait_ge(sig("v_m"), t + 1)
                for ch in range(2):
                    for h in range(H):
                        last = mm(bank[5][tokens(ch), head(h)], gram_a[:, h, 1, tokens(ch)], v_m[:, t % 2, ch, head(h)],
                                  start=True, stop=True)
                last.then_inc(sig("xv_full"), 1)

            def gates(t):
                pe.wait_ge(sig("first"), 2 * t + 1)
                mm(bank[4], lora_t[:, P:2 * P], gate_w[:], start=True, stop=True).then_inc(sig("g_full"), 1)

            def offset(i, g):
                def piece(t):
                    n = LEVELS * t + i
                    if i == 0:
                        pe.wait_ge(sig("first"), 2 * t + g + 1)
                    else:
                        pe.wait_ge(sig("inv"), 2 * ((LEVELS - 1) * t + i - 1) + g + 1)
                    pe.wait_ge(sig("a_off"), 2 * n + g + 1)
                    if n >= 1:
                        pe.wait_ge(sig("grow"), 2 * (n - 1) + g + 1)
                    for h in range(4):
                        last = mm(bank[g][:, h * P:(h + 1) * P], a_off[:, n % 2, 4 * g + h, :], inv[:, 4 * g + h, :],
                                  start=True, stop=True)
                    last.then_inc(sig("grow_full"), 1)
                return piece

            def doubled(i, g):
                def piece(t):
                    n = LEVELS * t + i
                    pe.wait_ge(sig("grow"), 2 * n + g + 1)
                    if n >= 1:
                        pe.wait_ge(sig("inv_t"), 2 * (n - 1) + g + 1)
                    for h in range(4):
                        it, gr = inv_t[:, t % 2, 4 * g + h, :], grow[:, 4 * g + h, :]
                        lhs, rhs = (it, gr) if i < LEVELS - 1 else (gr, it)
                        last = mm(bank[2 + g][:, h * P:(h + 1) * P], lhs, rhs, start=True, stop=True)
                    last.then_inc(sig("inv_full"), 1)
                return piece

            def turned(i):
                def piece(t):
                    for g in range(2):
                        pe.wait_ge(sig("inv"), 2 * ((LEVELS - 1) * t + i) + g + 1)
                        for h in range(4):
                            last = nc.tensor.transpose(bank[2 + g][:, h * P:(h + 1) * P], inv[:, 4 * g + h, :], ident[:])
                        last.then_inc(sig("turned_full"), 1)
                return piece

            def w_rows(t):
                pe.wait_ge(sig("inv_t"), 2 * LEVELS * (t + 1))
                if t >= 1:
                    pe.wait_ge(sig("state_read"), 2 * t)
                for h in range(H):
                    rows_h = slice(h % 2 * HD, (h % 2 + 1) * HD)
                    last = mm(bank[7][rows_h, pair(h // 2)], tm[:, t % 2, 0, head(h)], inv_t[:, t % 2, h, :], start=True, stop=True)
                last.then_inc(sig("w_full"), 1)

            def scan(ch):
                def piece(t):
                    n, tok = 2 * t + ch, tokens(ch)
                    pe.wait_ge(sig("w_t"), t + 1)
                    if n >= 1:
                        pe.wait_ge(sig("state_read"), n)
                    for h in range(H):
                        mm(bank[7][tok, head(h)], inv_t[:, t % 2, h, tok], xv[:, t % 2, head(h)], start=(h == 0), stop=False)
                    if n >= 1:
                        pe.wait_ge(sig("state"), n)
                    for j in range(PAIRS):
                        last = mm(bank[7][tok, pair(j)], w_t[:, j, tok], state[:, ch, j, :], start=False, stop=(j == PAIRS - 1))
                    last.then_inc(sig("sa_full"), 1)
                    if t >= 1:
                        pe.wait_ge(sig("y_sum"), t)
                    for j in range(PAIRS):
                        mm(bank[6][tok, pair(j)], fm_ar[:, t % 2, j, 1, tok], state[:, ch, j, :], start=(j == 0), stop=False)
                return piece

            def advance(ch):
                def piece(t):
                    pe.wait_ge(sig("sa"), 2 * t + ch + 1)
                    for j in range(PAIRS):
                        mm(bank[7][:, pair(j)], tm[:, t % 2, 3, pair(j)], v_m[:, t % 2, ch, pair(j)], start=True, stop=False)
                        last = mm(bank[7][:, pair(j)], tm[:, t % 2, 2, pair(j)], sa[:, ch, pair(j)], start=False, stop=True)
                    last.then_inc(sig("state_full"), 1)
                return piece

            def out(ch):
                def piece(t):
                    tok = tokens(ch)
                    for h in range(H):
                        ps = bank[6][tok, head(h)]
                        mm(ps, gram_r[:, t % 2, h, 1, tok], v_m[:, t % 2, ch, head(h)], start=False, stop=False)
                        last = mm(ps, gram_r[:, t % 2, h, 0, tok], sa[:, ch, head(h)], start=False, stop=(h == H - 1))
                    last.then_inc(sig("y_full"), 1)
                return piece

            for t in range(-1, TT + 1):
                at(t, offset(0, 0))
                at(t - 1, w_rows)
                at(t, first(1), offset(0, 1))
                at(t + 1, flip_lora)
                at(t, doubled(0, 0))
                at(t - 1, scan(0))
                at(t + 1, decay_logit)
                at(t, doubled(0, 1))
                at(t + 1, rate_logit)
                at(t, offset(1, 0), offset(1, 1), turned(0))
                at(t - 1, advance(0))
                at(t, doubled(1, 0))
                at(t + 1, decay_sums)
                at(t, doubled(1, 1))
                at(t - 1, scan(1))
                at(t, offset(2, 0), offset(2, 1), turned(1))
                at(t - 1, advance(1))
                at(t, doubled(2, 0))
                at(t - 1, out(0))
                at(t + 1, chunk_sums)
                at(t, doubled(2, 1))
                at(t - 1, out(1))
                at(t, offset(3, 0), offset(3, 1), turned(2))
                at(t + 1, flip(0), flip(1))
                at(t, doubled(3, 0))
                at(t + 1, flip(2), flip(3))
                at(t, doubled(3, 1))
                at(t + 1, products(0), products(1))
                at(t, offset(4, 0), offset(4, 1), turned(3))
                at(t + 1, products(2), products(3))
                at(t, doubled(4, 0))
                at(t + 1, products(4), products(5))
                at(t, doubled(4, 1))
                at(t + 1, products(6), products(7), first(0), keys_v, gates)

        @block.vector
        def _(dve):
            link = Link(dve, sig("dve_link_r"))
            tt, stt, ts = nc.vector.tensor_tensor, nc.vector.scalar_tensor_tensor, nc.vector.tensor_scalar

            def mark(ins, name, count):
                ins.then_inc(sig(name), 1)
                dve.wait_ge(sig(name), count)

            def rkv(t):
                return (cur[:, t % 2, i * W:(i + 1) * W] for i in range(3))

            def gate_half(t):
                dve.wait_ge(sig("lora"), 3 * (t + 1))
                ts(lora[:, P:2 * P], lora[:, P:2 * P], 0.5, 0.5, ALU.mult, ALU.add).then_inc(sig("lora_sig"), 1)

            def unit_keys(t):
                r, k, v = rkv(t)
                link(tt(kk[:], k, k_k, ALU.mult))
                link(tt(tmp[:], kk[:], kk[:], ALU.mult))
                link(nc.vector.tensor_reduce(norm_k[:], heads(tmp[:]), AX.X, ALU.add))
                ts(norm_k[:], norm_k[:], 1e-24, None, ALU.max).then_inc(sig("kk_ss"), 1)

            def bias(t):
                dve.wait_ge(sig("z_full"), t + 1)
                tt(sw[:], bank[5], w0, ALU.add).then_inc(sig("z_biased"), 1)
                dve.wait_ge(sig("a_full"), t + 1)
                tt(aa[:], bank[4], a0, ALU.add).then_inc(sig("a_biased"), 1)
                dve.wait_ge(sig("kk_rn"), t + 1)
                link(tt(heads(kk[:]), heads(kk[:]), norm_k[:].unsqueeze(2).to_broadcast([P, H, HD]), ALU.mult))
                dve.wait_ge(sig("z_tanh"), t + 1)
                mark(ts(sw[:], sw[:], 0.5, 0.5, ALU.mult, ALU.add), "sw", t + 1)

            def rates(t):
                r, k, v = rkv(t)
                dve.wait_ge(sig("a_tanh"), t + 1)
                link(ts(aa[:], aa[:], 0.5, 0.5, ALU.mult, ALU.add))
                link(stt(out=kp[:], in0=aa[:], scalar=1.0, in1=k_a, op0=ALU.subtract, op1=ALU.mult))
                link(stt(out=kp[:], in0=kp[:], scalar=1.0, in1=k, op0=ALU.add, op1=ALU.mult))
                link(tt(aa[:], aa[:], kk[:], ALU.mult))

            def key_vectors(t):
                r, k, v = rkv(t)
                b = t % 2
                dve.wait_ge(sig("p_ex"), t + 1)
                if t >= 2:
                    dve.wait_ge(sig("state_full"), 2 * (t - 1))
                stt(out=tm[:, b, 0, :], in0=kk[:], scalar=-1.0, in1=p_ex[:], op0=ALU.mult, op1=ALU.mult).then_inc(sig("tm"), 1)
                tt(tm[:, b, 1, :], r, p_in[:], ALU.mult).then_inc(sig("tm"), 1)
                tt(tm[:, b, 2, :], aa[:], p_inv[:], ALU.mult).then_inc(sig("tm"), 1)
                tt(tm[:, b, 3, :], kp[:], p_inv[:], ALU.mult).then_inc(sig("tm"), 1)

            def bonuses(t):
                r, k, v = rkv(t)
                link(tt(tmp[:], r, kp[:], ALU.mult))
                link(tt(tmp[:], tmp[:], r_k, ALU.mult))
                link(nc.vector.tensor_reduce(bonus[:], heads(tmp[:]), AX.X, ALU.add))

            def bonus_values(t):
                r, k, v = rkv(t)
                if t >= 3:
                    dve.wait_ge(sig("tile_done"), t - 2)
                mark(tt(heads(bonus_v[:, t % 3, :]), heads(v), bonus[:].unsqueeze(2).to_broadcast([P, H, HD]), ALU.mult), "bonus_v", t + 1)

            def masked(*hs):
                def piece(t):
                    for h in hs:
                        ps = bank[4 + h % 2].rearrange("p (k a t) -> p k a t", k=2, a=2)
                        dve.wait_ge(sig("gram_full"), H * t + h + 1)
                        if h == 0 and t >= 1:
                            dve.wait_ge(sig("a_off"), 2 * LEVELS * t)
                        for a, dst in enumerate((gram_a[:, h], gram_r[:, t % 2, h])):
                            tt(dst, ps[:, :, a, :], tri[:, a, :].unsqueeze(1).to_broadcast([P, 2, P]), ALU.mult).then_inc(sig("gram"), 1)
                return piece

            ident_h = ident[:].unsqueeze(1).to_broadcast([P, 4, P])

            def first(g):
                def piece(t):
                    hs = slice(4 * g, 4 * g + 4)
                    dve.wait_ge(sig("gram"), 2 * (H * t + 4 * (g + 1)))
                    link(tt(inv_t[:, t % 2, hs], gram_a[:, hs, 0, :], off_t[:, 0, :].unsqueeze(1).to_broadcast([P, 4, P]), ALU.mult))
                    mark(tt(inv_t[:, t % 2, hs], inv_t[:, t % 2, hs], ident_h, ALU.add), "inv_first", 2 * t + g + 1)
                return piece

            def grown(i):
                def piece(t):
                    for g in range(2):
                        dve.wait_ge(sig("grow_full"), 2 * (LEVELS * t + i) + g + 1)
                        tt(grow[:, 4 * g:4 * g + 4], heads(bank[g], P), ident_h, ALU.add).then_inc(sig("grow"), 1)
                return piece

            def advance(ch):
                def piece(t):
                    n = 2 * t + ch
                    dve.wait_ge(sig("state_full"), n + 1)
                    nxt = state[:, 1 - ch]
                    halves = [(slice(h * HD, (h + 1) * HD), slice(h * HD, (h + 1) * HD)) for h in range(2)]
                    for ks, vs in halves:
                        last = tt(nxt[ks, :, vs], heads(bank[7], P)[ks, :, vs], state[ks, ch, :, vs], ALU.add)
                        if ks.start == 0:
                            link(last)
                    mark(last, "state_read", n + 1)
                    for ks, vs in halves:
                        last = tt(nxt[ks, :, vs], nxt[ks, :, vs], p_end[ks, t % 3, :, ch:ch + 1].to_broadcast([HD, PAIRS, HD]), ALU.mult)
                        if ks.start == 0:
                            link(last)
                    mark(last, "state", n + 1)
                return piece

            def y_moments(t):
                yt = y[:, t % 2, :]
                dve.wait_ge(sig("y_sum"), t + 1)
                link(nc.vector.tensor_reduce(norm_y[:], heads(yt), AX.X, ALU.add))
                link(ts(norm_y[:], norm_y[:], 1.0 / HD, None, ALU.mult))
                link(tt(heads(yt), heads(yt), norm_y[:].unsqueeze(2).to_broadcast([P, H, HD]), ALU.subtract))
                link(tt(tmp[:], yt, yt, ALU.mult))
                link(nc.vector.tensor_reduce(norm_y[:], heads(tmp[:]), AX.X, ALU.add))
                ts(norm_y[:], norm_y[:], 1.0 / HD, LN_EPS, ALU.mult, ALU.add).then_inc(sig("y_var"), 1)

            def y_finish(t):
                yt = y[:, t % 2, :]
                dve.wait_ge(sig("y_rstd"), t + 1)
                link(tt(heads(yt), heads(yt), norm_y[:].unsqueeze(2).to_broadcast([P, H, HD]), ALU.mult))
                link(tt(yt, yt, ln_g, ALU.mult))
                mark(tt(yt, yt, ln_b, ALU.add), "y_scaled", t + 1)

            for t in range(-1, TT + 1):
                at(t + 1, gate_half)
                at(t, grown(0))
                at(t + 1, unit_keys, bias)
                at(t, grown(1))
                at(t - 1, advance(0))
                at(t + 1, rates, bonuses, bonus_values)
                at(t, grown(2))
                at(t + 1, key_vectors)
                at(t - 1, advance(1))
                at(t, grown(3))
                at(t - 1, y_moments, y_finish)
                at(t + 1, masked(0, 1))
                at(t, grown(4))
                at(t + 1, masked(2, 3), first(0), masked(4, 5, 6, 7), first(1))


def merge(nc, sig, bank, const, keep, ins, dram, raw):
    with ExitStack() as ctx:
        sb = lambda name, shape: ctx.enter_context(nc.sbuf_tensor(name, shape, F32))
        mixed_t = sb("mg_mixed_t", [P, KT, S])
        blend(nc, sig, bank, const, ins, dram, raw, mixed_t)
        sig.next_stage("blend")
        outward(nc, sig, bank, const, keep, ins, dram, raw, mixed_t)


def load_rows(sp, sig, raw, first, src):
    src = src.rearrange("(k p) n -> p k n", p=P)
    for k in range(0, src.shape[1], 2):
        sp.dma_start(raw[:, first + k:first + k + 2, :], src[:, k:k + 2, :]).then_inc(sig(f"raw_in{(first + k) // 2}"), 16)


def blend(nc, sig, bank, const, ins, dram, raw, mixed_t):
    ident, psum = const["ident"], const["psum"]
    WK = W // P
    with ExitStack() as ctx:
        sb = lambda name, shape, dt=F32: ctx.enter_context(nc.sbuf_tensor(name, shape, dt))
        w_r = sb("bl_w_r", [P, 2, KT, D], F32R)
        gates = sb("bl_gates", [P, 2, 2 * D])
        o_in = sb("bl_o_in", [P, 2, 2, W])
        o_r = sb("bl_o_r", [P, 2, 2, 2, W], F32R)
        mixed = sb("bl_mixed", [P, 2, D])
        block = ctx.enter_context(nc.Block("blend"))

        @block.sync
        def _(sp):
            def load(t):
                b = t % 2
                rows = slice(t * P, (t + 1) * P)
                if t >= 2:
                    sp.wait_ge(sig("o_fox_lo"), t - 1)
                    sp.wait_ge(sig("o_flipped"), t - 1)
                sp.dma_start(o_in[:, b, 1, :], dram["o_rwkv"][rows, :]).then_inc(sig(f"o_rwkv_in{b}"), 16)
                sp.dma_start(o_in[:, b, 0, :].rearrange("p (k t) -> p k t", t=P),
                             dram["o_fox_t"][:, rows].rearrange("(k p) t -> p k t", p=P)).then_inc(sig(f"o_fox_in{b}"), 16)

            def load_gates(t):
                if t >= 2:
                    sp.wait_ge(sig("mixed"), 2 * (t - 1))
                sp.dma_start(gates[:, t % 2, :], dram["gates"][t * P:(t + 1) * P, :]).then_inc(sig(f"gates_in{t % 2}"), 16)

            load(0)
            load_gates(0)
            load(1)
            load_gates(1)
            load(2)
            for t in range(2, TT):
                if t + 1 < TT:
                    load(t + 1)
                load_gates(t)
                if t < 4:
                    sp.wait_ge(sig("w_lo"), KT)
                    load_rows(sp, sig, raw, 4 * (t - 2), ins["w_o"][0][(t - 2) * W:(t - 1) * W])
            for c in range(KT // 2):
                sp.wait_ge(sig(f"raw_in{c}"), 32)

        @block.tensor
        def _(pe):
            def flip(t):
                pe.wait_ge(sig(f"o_rwkv_in{t % 2}"), 16 * (t // 2 + 1))
                if t >= 2:
                    pe.wait_ge(sig("o_rwkv_lo"), t - 1)
                for k in range(WK):
                    last = nc.tensor.transpose(bank[t % 2][:, k * P:(k + 1) * P], o_in[:, t % 2, 1, k * P:(k + 1) * P], ident[:])
                last.then_inc(sig("o_flipped"), 1)

            def branches(t):
                pe.wait_ge(sig("o_fox_lo"), t + 1)
                pe.wait_ge(sig("o_rwkv_lo"), t + 1)
                for half in range(2):
                    cols = slice(half * NC5, (half + 1) * NC5)
                    if t >= 1:
                        pe.wait_ge(sig("branches_read"), 2 * (t - 1) + half + 1)
                    for j in range(2):
                        if t == 0 and half == 0:
                            pe.wait_ge(sig("w_lo"), WK * (j + 1))
                        o = [o_r[:, t % 2, j, i, :] for i in range(2)]
                        last = matmul3(nc, bank[4 + 2 * half + j],
                                       [([o[i][:, k * P:(k + 1) * P] for i in range(2)], [w_r[:, i, j * WK + k, cols] for i in range(2)])
                                        for k in range(WK)])
                    last.then_inc(sig("branches_full"), 1)

            def turn(t):
                pe.wait_ge(sig("mixed"), 2 * (t + 1))
                if t >= 1:
                    pe.wait_ge(sig("mixed_t"), t)
                for k in range(KT):
                    last = nc.tensor.transpose(psum[:, 2 * NC5 + k * P:2 * NC5 + (k + 1) * P], mixed[:, t % 2, k * P:(k + 1) * P], ident[:])
                last.then_inc(sig("mixed_flipped"), 1)

            flip(0)
            for s in range(TT + 1):
                if s + 1 < TT:
                    flip(s + 1)
                if s < TT:
                    branches(s)
                if s >= 1:
                    turn(s - 1)

        @block.scalar
        def _(act):
            def copy(out, src, name):
                nc.scalar.activation(out, src, ACT.Copy).then_inc(sig(name), 1)

            def high(t):
                b = t % 2
                if t >= 2:
                    act.wait_ge(sig("branches_full"), 2 * (t - 1))
                act.wait_ge(sig(f"o_fox_in{b}"), 16 * (t // 2 + 1))
                copy(o_r[:, b, 0, 0, :], o_in[:, b, 0, :], "o_fox_hi")
                act.wait_ge(sig("o_flipped"), t + 1)
                copy(o_r[:, b, 1, 0, :], bank[b], "o_rwkv_hi")

            def weights_high(ks):
                for k in ks:
                    if k % 2 == 0:
                        act.wait_ge(sig(f"raw_in{k // 2}"), 16)
                    copy(w_r[:, 0, k, :], raw[:, k, :], "w_hi")

            weights_high(range(WK))
            high(0)
            weights_high(range(WK, KT))
            for s in range(TT + 1):
                if s + 1 < TT:
                    high(s + 1)
                if s >= 1:
                    act.wait_ge(sig("mixed_flipped"), s)
                    copy(mixed_t[:, :, (s - 1) * P:s * P], psum[:, 2 * NC5:4 * NC5].rearrange("p (k t) -> p k t", t=P), "mixed_t")

        @block.vector
        def _(dve):
            tt = nc.vector.tensor_tensor

            def low(t):
                b = t % 2
                dve.wait_ge(sig("o_fox_hi"), t + 1)
                tt(o_r[:, b, 0, 1, :], o_in[:, b, 0, :], o_r[:, b, 0, 0, :].bitcast(F32), ALU.subtract).then_inc(sig("o_fox_lo"), 1)
                dve.wait_ge(sig("o_rwkv_hi"), t + 1)
                tt(o_r[:, b, 1, 1, :], bank[b], o_r[:, b, 1, 0, :].bitcast(F32), ALU.subtract).then_inc(sig("o_rwkv_lo"), 1)

            def weights_low(ks):
                for k in ks:
                    dve.wait_ge(sig("w_hi"), k + 1)
                    tt(w_r[:, 1, k, :], raw[:, k, :], w_r[:, 0, k, :].bitcast(F32), ALU.subtract).then_inc(sig("w_lo"), 1)

            def gate(t):
                dve.wait_ge(sig(f"gates_in{t % 2}"), 16 * (t // 2 + 1))
                for half in range(2):
                    cols = slice(half * NC5, (half + 1) * NC5)
                    m, g = mixed[:, t % 2, cols], gates[:, t % 2, :]
                    dve.wait_ge(sig("branches_full"), 2 * t + half + 1)
                    if t >= 2:
                        dve.wait_ge(sig("mixed_flipped"), t - 1)
                    tt(m, bank[4 + 2 * half], g[:, cols], ALU.mult).then_inc(sig("fox_gated"), 1)
                    g2 = g[:, D + half * NC5:D + (half + 1) * NC5]
                    tt(g2, bank[5 + 2 * half], g2, ALU.mult).then_inc(sig("branches_read"), 1)
                    dve.wait_ge(sig("branches_read"), 2 * t + half + 1)
                    dve.wait_ge(sig("fox_gated"), 2 * t + half + 1)
                    tt(m, m, g2, ALU.add).then_inc(sig("mixed"), 1)

            weights_low(range(WK))
            low(0)
            weights_low(range(WK, KT))
            for s in range(TT):
                if s + 1 < TT:
                    low(s + 1)
                gate(s)


def outward(nc, sig, bank, const, keep, ins, dram, raw, mixed_t):
    ident, psum = const["ident"], const["psum"]
    mod_bc, logits = keep["mod_bc"], keep["logits"]
    GE = G + E
    with ExitStack() as ctx:
        sb = lambda name, shape, dt=F32: ctx.enter_context(nc.sbuf_tensor(name, shape, dt))
        w_r = sb("ow_w_r", [P, 2, KT, D], F32R)
        m_r = sb("ow_m_r", [P, 2, 2, KT, P], F32R)
        w_route = sb("w_route", [P, KT, GE])
        b_route = sb("b_route", [P, GE])
        x_in = sb("ow_x", [P, 2, D])
        squares = sb("ow_squares", [P, D])
        x_mid = sb("ow_x_mid", [P, 2, D])
        h_mid = sb("ow_h_mid", [P, 2, D])
        h_t = sb("ow_h_t", [P, KT, P])
        logits_t = sb("logits_t", [GE, S])
        ms = sb("ow_ms", [P, TT])
        block = ctx.enter_context(nc.Block("outward"))

        @block.sync
        def _(sp):
            for t in range(TT):
                if t >= 2:
                    sp.wait_ge(sig("x_mid"), t - 1)
                sp.dma_start(x_in[:, t % 2, :], ins["x"][0, t * P:(t + 1) * P, :]).then_inc(sig(f"ow_x_in{t % 2}"), 16)
                if t == 0:
                    sp.dma_start(w_route[:, :, 0:G], ins["router_group_w"][0].rearrange("(k p) n -> p k n", p=P)).then_inc(sig("w_route_in"), 16)
                    sp.dma_start(w_route[:, :, G:GE], ins["router_expert_w"][0].rearrange("(k p) n -> p k n", p=P)).then_inc(sig("w_route_in"), 16)
                    sp.dma_start(b_route[:, 0:G], ins["router_group_b"].partition_broadcast(P).rearrange("p a n -> p (a n)")).then_inc(sig("b_route_in"), 16)
                    sp.dma_start(b_route[:, G:GE], ins["router_expert_b"].partition_broadcast(P).rearrange("p a n -> p (a n)")).then_inc(sig("b_route_in"), 16)

        @block.gpsimd
        def _(pool):
            for t in range(TT):
                pool.wait_ge(sig("ow_ms"), t + 1)
                nc.gpsimd.tensor_tensor(ms[:, t:t + 1], ms[:, t:t + 1], const["neghalf"][:, 0:1], ALU.pow).then_inc(sig("ow_rstd"), 1)
                pool.dma_start(dram["x_mid"][t * P:(t + 1) * P, :], x_mid[:, t % 2, :]).then_inc(sig(f"x_mid_out{t % 2}"), 16)
                pool.wait_ge(sig("h_mid"), t + 1)
                pool.dma_start(dram["h_mid"][t * P:(t + 1) * P, :], h_mid[:, t % 2, :]).then_inc(sig(f"h_mid_out{t % 2}"), 16)
            for b in range(2):
                pool.wait_ge(sig(f"x_mid_out{b}"), 16 * TT // 2)
                pool.wait_ge(sig(f"h_mid_out{b}"), 16 * TT // 2)

        def w_o_banks(t):
            return psum[:, (t % 2) * D:(t % 2 + 1) * D]

        @block.tensor
        def _(pe):
            TURN = 6

            def project_out(t):
                pe.wait_ge(sig("m_lo"), t + 1)
                if t >= 2:
                    pe.wait_ge(sig("w_o_read"), t - 1)
                for k in range(KT):
                    if k == TURN and t >= 1:
                        flip(t - 1)
                    if t == 0:
                        pe.wait_ge(sig("w_lo"), k + 1)
                    m = [m_r[:, t % 2, i, k, :] for i in range(2)]
                    for half in range(2):
                        out = w_o_banks(t)[:, half * NC5:(half + 1) * NC5]
                        w = [w_r[:, i, k, half * NC5:(half + 1) * NC5] for i in range(2)]
                        nc.tensor.matmul(out, m[0], w[0], start=(k == 0), stop=False)
                        nc.tensor.matmul(out, m[0], w[1], start=False, stop=False)
                        last = nc.tensor.matmul(out, m[1], w[0], start=False, stop=(k == KT - 1))
                last.then_inc(sig("w_o_full"), 1)

            def flip(t):
                pe.wait_ge(sig("h_mid"), t + 1)
                if t >= 1:
                    pe.wait_ge(sig("h_t"), t)
                for k in range(KT):
                    last = nc.tensor.transpose(psum[:, 4 * NC5 + k * P:4 * NC5 + (k + 1) * P], h_mid[:, t % 2, k * P:(k + 1) * P], ident[:])
                last.then_inc(sig("h_flipped"), 1)

            def router(t):
                pe.wait_ge(sig("h_t"), t + 1)
                if t == 0:
                    pe.wait_ge(sig("w_route_in"), 32)
                else:
                    pe.wait_ge(sig("logits_t"), t)
                for k in range(KT):
                    last = nc.tensor.matmul(bank[6][0:GE, 0:P], w_route[:, k, :], h_t[:, k, :], start=(k == 0), stop=(k == KT - 1))
                last.then_inc(sig("logits_full"), 1)

            for s in range(TT + 1):
                if s < TT:
                    project_out(s)
                if s == TT:
                    flip(s - 1)
                if s >= 1:
                    router(s - 1)
            pe.wait_ge(sig("logits_t"), TT)
            for t in range(TT):
                last = nc.tensor.transpose(bank[7][:, t * GE:(t + 1) * GE], logits_t[:, t * P:(t + 1) * P], ident[0:GE, 0:GE])
            last.then_inc(sig("logits_flipped"), 1)

        @block.scalar
        def _(act):
            def copy(out, src, name):
                nc.scalar.activation(out, src, ACT.Copy).then_inc(sig(name), 1)

            def high(t):
                if t >= 2:
                    act.wait_ge(sig("w_o_full"), t - 1)
                copy(m_r[:, t % 2, 0], mixed_t[:, :, t * P:(t + 1) * P], "m_hi")

            high(0)
            for k in range(KT):
                copy(w_r[:, 0, k, :], raw[:, k, :], "w_hi")
            for s in range(TT + 1):
                if s + 1 < TT:
                    high(s + 1)
                if s >= 1:
                    act.wait_ge(sig("h_flipped"), s)
                    copy(h_t[:].rearrange("p k t -> p (k t)"), psum[:, 4 * NC5:6 * NC5], "h_t")
                if s < TT:
                    act.wait_ge(sig("x_mid"), s + 1)
                    if s >= 1:
                        act.wait_ge(sig("h_ss"), s)
                    nc.scalar.activation(squares[:], x_mid[:, s % 2, :], ACT.Square, accum_out=ms[:, s:s + 1]).then_inc(sig("h_ss"), 1)
                if s >= 1:
                    act.wait_ge(sig("logits_full"), s)
                    copy(logits_t[:, (s - 1) * P:s * P], bank[6][0:GE, 0:P], "logits_t")

        @block.vector
        def _(dve):
            tt, stt, ts = nc.vector.tensor_tensor, nc.vector.scalar_tensor_tensor, nc.vector.tensor_scalar

            def low(t):
                dve.wait_ge(sig("m_hi"), t + 1)
                tt(m_r[:, t % 2, 1], mixed_t[:, :, t * P:(t + 1) * P], m_r[:, t % 2, 0].bitcast(F32), ALU.subtract).then_inc(sig("m_lo"), 1)

            def residual(t):
                xm, hm = x_mid[:, t % 2, :], h_mid[:, t % 2, :]
                dve.wait_ge(sig("w_o_full"), t + 1)
                dve.wait_ge(sig(f"ow_x_in{t % 2}"), 16 * (t // 2 + 1))
                if t >= 2:
                    dve.wait_ge(sig(f"x_mid_out{t % 2}"), 16 * (t // 2))
                    dve.wait_ge(sig(f"h_mid_out{t % 2}"), 16 * (t // 2))
                    dve.wait_ge(sig("h_flipped"), t - 1)
                tt(xm, w_o_banks(t), mod_bc[:, 0, :], ALU.mult).then_inc(sig("w_o_read"), 1)
                dve.wait_ge(sig("w_o_read"), t + 1)
                tt(xm, xm, x_in[:, t % 2, :], ALU.add).then_inc(sig("x_mid"), 1)
                dve.wait_ge(sig("h_ss"), t + 1)
                ts(ms[:, t:t + 1], ms[:, t:t + 1], 1.0 / D, EPS, ALU.mult, ALU.add).then_inc(sig("ow_ms"), 1)
                dve.wait_ge(sig("ow_rstd"), t + 1)
                stt(out=hm, in0=xm, scalar=ms[:, t:t + 1], in1=mod_bc[:, 2, :], op0=ALU.mult, op1=ALU.mult).then_inc(sig("h_scaled"), 1)
                dve.wait_ge(sig("h_scaled"), t + 1)
                tt(hm, hm, mod_bc[:, 1, :], ALU.add).then_inc(sig("h_mid"), 1)

            low(0)
            for k in range(KT):
                dve.wait_ge(sig("w_hi"), k + 1)
                tt(w_r[:, 1, k, :], raw[:, k, :], w_r[:, 0, k, :].bitcast(F32), ALU.subtract).then_inc(sig("w_lo"), 1)
            for t in range(TT):
                if t + 1 < TT:
                    low(t + 1)
                residual(t)
            dve.wait_ge(sig("b_route_in"), 32)
            dve.wait_ge(sig("logits_flipped"), 1)
            tt(logits, bank[7][:, 0:TT * GE].rearrange("p (t e) -> p t e", e=GE),
               b_route[:].unsqueeze(1).to_broadcast([P, TT, GE]), ALU.add).then_inc(sig("logits"), 1)
            dve.wait_ge(sig("logits"), 1)


def route(nc, sig, bank, const, keep, ins, dram):
    logits, dest, pair_w = keep["logits"], keep["dest"], keep["pair_w"]
    psum = const["psum"]
    BIG = 1024.0
    with ExitStack() as ctx:
        sb = lambda name, shape, dt=F32: ctx.enter_context(nc.sbuf_tensor(name, shape, dt))
        ones = sb("rt_ones", [P, P])
        before = sb("rt_before", [P, P])
        iota_e = sb("iota_e", [P, E])
        iota_g = sb("iota_g", [P, G])
        iota_b = sb("iota_b", [P, OVERFLOW_BLOCKS])
        first_row = sb("first_row", [P, E])
        pair = sb("rt_pair", [P, 2, TT])
        iota_p = sb("iota_p", [P, P])
        iota_blk = sb("iota_blk", [P, BLOCKS])
        base = sb("rt_base", [P, TT + 1, E])
        place_i = sb("rt_place_i", [P, 2, 2, TT], I32)
        place = sb("rt_place", [P, 2, 2, TT])
        of_row = sb("rt_of_row", [P, 2, TT, P], F32R)
        of_block = sb("rt_of_block", [P, 2, TT, BLOCKS], F32R)
        gmax = sb("rt_gmax", [P, TT])
        gexp = sb("rt_gexp", [P, TT, G])
        gsum = sb("rt_gsum", [P, TT])
        ghot = sb("rt_ghot", [P, TT, G])
        el = sb("rt_el", [P, TT, E])
        best = sb("rt_best", [P, 2, TT])
        hot = sb("rt_hot", [P, 2, TT, E])
        both = sb("rt_both", [P, TT, E])
        tmp = sb("rt_tmp", [P, TT, E])
        idx = sb("rt_idx", [P, TT])
        extra = sb("rt_extra", [P, E])
        extra_end = sb("rt_extra_end", [P, E])
        over_row = sb("rt_over_row", [P, E])
        diff = sb("rt_diff", [P, E])
        ones_e = sb("rt_ones_e", [P, E])
        row = sb("rt_row", [P, TT, E])
        destf = sb("rt_destf", [P, TT])
        table = sb("rt_table", [1, BLOCKS, E])
        tablef = sb("rt_tablef", [1, 1 + BLOCKS])
        free_row = sb("rt_free_row", [P, BLOCKS])
        blk_hot = sb("rt_blk_hot", [P, TT, BLOCKS])
        by_block = sb("rt_by_block", [BLOCKS, P])
        pair_f = sb("rt_pair_f", [P, BLOCKS])
        token_f = sb("rt_token_f", [P, BLOCKS])
        block = ctx.enter_context(nc.Block("route"))

        def bt(ap, n):
            return ap.unsqueeze(2).to_broadcast([P, TT, n])

        def be(ap, n):
            return ap.unsqueeze(1).to_broadcast([P, TT, n])

        @block.sync
        def _(sp):
            prefetch_weights(nc, sp, sig, keep, ins)

        @block.gpsimd
        def _(pool):
            link = Link(pool, sig("pool_link_t"))
            link(nc.gpsimd.memset(ones[:], 1.0))
            link(nc.gpsimd.memset(before[:], 1.0))
            link(nc.gpsimd.affine_select(out=before[:], in_=before[:], compare_op=ALU.is_gt, fill=0.0, base=0,
                                         pattern=[[1, P]], channel_multiplier=-1))
            for ap, pattern, cm in ((iota_e, [[1, E]], 0), (iota_g, [[1, G]], 0), (iota_b, [[1, OVERFLOW_BLOCKS]], 0),
                                    (first_row, [[P, E]], 0), (iota_p, [[1, P]], 0), (iota_blk, [[1, BLOCKS]], 0)):
                link(nc.gpsimd.iota(ap[:], pattern, base=0, channel_multiplier=cm, allow_small_or_imprecise_dtypes=True))
            link(nc.gpsimd.iota(pair[:], [[S, 2], [P, TT]], base=1, channel_multiplier=1, allow_small_or_imprecise_dtypes=True))
            link(nc.gpsimd.iota(free_row[:], [[1, BLOCKS]], base=2 * S + 1, channel_multiplier=BLOCKS, allow_small_or_imprecise_dtypes=True))
            nc.gpsimd.nop().then_inc(sig("rt_const"), 1)

        @block.scalar
        def _(act):
            act.wait_ge(sig("rt_gshift"), 1)
            nc.scalar.activation(gexp[:], gexp[:], ACT.Exp).then_inc(sig("rt_gexp"), 1)
            act.wait_ge(sig("rt_ratio"), 1)
            nc.scalar.activation(best[:, 1, :], best[:, 1, :], ACT.Exp).then_inc(sig("rt_ratio_exp"), 1)

        @block.tensor
        def _(pe):
            pe.wait_ge(sig("rt_const"), 1)
            pe.wait_ge(sig("rt_both"), 1)
            all_tiles = both[:].rearrange("p t e -> p (t e)")
            nc.tensor.matmul(bank[0][:, 0:TT * E], before[:], all_tiles, start=True, stop=True).then_inc(sig("ranks"), 1)
            nc.tensor.matmul(bank[1][:, 0:TT * E], ones[:], all_tiles, start=True, stop=True).then_inc(sig("totals"), 1)
            for j in range(2):
                pe.wait_ge(sig("of_place"), 2 * (j + 1))
                for t in range(TT):
                    last = nc.tensor.matmul(bank[2][0:BLOCKS, 0:P], of_block[:, j, t, :], of_row[:, j, t, :],
                                            start=(j == 0 and t == 0), stop=(j == 1 and t == TT - 1))
            last.then_inc(sig("by_block_full"), 1)
            pe.wait_ge(sig("by_block"), 1)
            nc.tensor.transpose(bank[3][:, 0:BLOCKS], by_block[:], const["ident"][0:BLOCKS, 0:BLOCKS]).then_inc(sig("pairs_flipped"), 1)

        @block.vector
        def _(dve):
            link = Link(dve, sig("dve_link_t"))
            tt, stt, ts, red = nc.vector.tensor_tensor, nc.vector.scalar_tensor_tensor, nc.vector.tensor_scalar, nc.vector.tensor_reduce
            gl = logits[:, :, 0:G]
            dve.wait_ge(sig("rt_const"), 1)

            def first_hot(out, vals, top, iota, n):
                link(tt(out, vals, bt(top, n), ALU.is_equal))
                link(stt(out=out, in0=out, scalar=-BIG, in1=be(iota, n), op0=ALU.mult, op1=ALU.add))
                link(red(idx[:], out, AX.X, ALU.min))
                link(ts(idx[:], idx[:], BIG, None, ALU.add))
                link(tt(out, be(iota, n), bt(idx[:], n), ALU.is_equal))

            link(red(gmax[:], gl, AX.X, ALU.max))
            tt(gexp[:], gl, bt(gmax[:], G), ALU.subtract).then_inc(sig("rt_gshift"), 1)
            first_hot(ghot[:], gl, gmax[:], iota_g[:], G)
            link(ts(ghot[:], ghot[:], 1.0, -NEG, ALU.subtract, ALU.mult))
            link(tt(el[:].rearrange("p t (g e) -> p t g e", e=EPG), logits[:, :, G:G + E].rearrange("p t (g e) -> p t g e", e=EPG),
                    ghot[:].unsqueeze(3).to_broadcast([P, TT, G, EPG]), ALU.add))
            link(red(best[:, 0, :], el[:], AX.X, ALU.max))
            first_hot(hot[:, 0], el[:], best[:, 0, :], iota_e[:], E)
            link(stt(out=el[:], in0=hot[:, 0], scalar=2.0 * NEG, in1=el[:], op0=ALU.mult, op1=ALU.add))
            link(red(best[:, 1, :], el[:], AX.X, ALU.max))
            first_hot(hot[:, 1], el[:], best[:, 1, :], iota_e[:], E)
            tt(both[:], hot[:, 0], hot[:, 1], ALU.add).then_inc(sig("rt_both"), 1)
            tt(best[:, 1, :], best[:, 1, :], best[:, 0, :], ALU.subtract).then_inc(sig("rt_ratio"), 1)
            dve.wait_ge(sig("rt_gexp"), 1)
            link(red(gsum[:], gexp[:], AX.X, ALU.add))
            dve.wait_ge(sig("rt_ratio_exp"), 1)
            link(ts(best[:, 0, :], best[:, 1, :], 1.0, None, ALU.add))
            link(tt(gsum[:], gsum[:], best[:, 0, :], ALU.mult))
            link(nc.vector.reciprocal(pair_w[:, :, 0], gsum[:]))
            link(tt(pair_w[:, :, 1], pair_w[:, :, 0], best[:, 1, :], ALU.mult))
            link(nc.vector.memset(base[:, 0, :], 0.0))
            dve.wait_ge(sig("totals"), 1)
            for t in range(TT):
                link(tt(base[:, t + 1, :], base[:, t, :], bank[1][:, t * E:(t + 1) * E], ALU.add))
            dve.wait_ge(sig("ranks"), 1)
            link(nc.vector.memset(extra[:], 0.0))
            link(nc.vector.memset(ones_e[:], 1.0))
            for j in range(1, S // P):
                link(stt(out=extra[:], in0=base[:, TT, :], scalar=float(j * P), in1=extra[:], op0=ALU.is_gt, op1=ALU.add))
            link(nc.vector.tensor_tensor_scan(extra_end[:], ones_e[:], extra[:], 0.0, ALU.mult, ALU.add))
            link(tt(over_row[:], extra_end[:], extra[:], ALU.subtract))
            link(ts(over_row[:], over_row[:], float(P), float(E * P - P), ALU.mult, ALU.add))
            link(tt(diff[:], first_row[:], over_row[:], ALU.subtract))
            rank = bank[0][:, 0:TT * E].rearrange("p (t e) -> p t e", e=E)
            link(tt(tmp[:], rank, base[:, 0:TT, :], ALU.add))
            link(stt(out=row[:], in0=tmp[:], scalar=float(P), in1=be(diff[:], E), op0=ALU.is_lt, op1=ALU.mult))
            link(tt(row[:], row[:], tmp[:], ALU.add))
            link(tt(row[:], row[:], be(over_row[:], E), ALU.add))
            for j in range(2):
                link(tt(tmp[:], row[:], hot[:, j], ALU.mult))
                link(red(destf[:], tmp[:], AX.X, ALU.add))
                nc.vector.tensor_copy(dest[:, :, j], destf[:]).then_inc(sig("dest"), 1)
                dve.wait_ge(sig("dest"), j + 1)
            link(ts(place_i[:, 0], dest[:].rearrange("p t j -> p j t"), P - 1, None, ALU.bitwise_and))
            link(ts(place_i[:, 1], dest[:].rearrange("p t j -> p j t"), P.bit_length() - 1, None, ALU.logical_shift_right))
            link(nc.vector.tensor_copy(place[:], place_i[:]))
            for j in range(2):
                tt(of_row[:, j], iota_p[:].unsqueeze(1).to_broadcast([P, TT, P]), bt(place[:, 0, j, :], P), ALU.is_equal).then_inc(sig("of_place"), 1)
                link(tt(blk_hot[:], iota_blk[:].unsqueeze(1).to_broadcast([P, TT, BLOCKS]), bt(place[:, 1, j, :], BLOCKS), ALU.is_equal))
                tt(of_block[:, j], blk_hot[:], bt(pair[:, j, :], BLOCKS), ALU.mult).then_inc(sig("of_place"), 1)
                dve.wait_ge(sig("of_place"), 2 * (j + 1))
            link(nc.vector.tensor_copy(tablef[0:1, 1:1 + E], iota_e[0:1, :]))
            over = table[0:1, 0:OVERFLOW_BLOCKS, :]
            link(tt(over, extra_end[0:1, :].unsqueeze(1).to_broadcast([1, OVERFLOW_BLOCKS, E]),
                    iota_b[0:1, :].unsqueeze(2).to_broadcast([1, OVERFLOW_BLOCKS, E]), ALU.is_le))
            link(red(tablef[0:1, 1 + E:1 + BLOCKS], over, AX.X, ALU.add))
            link(ts(tablef[0:1, 1 + E:1 + BLOCKS], tablef[0:1, 1 + E:1 + BLOCKS], float(E - 1), None, ALU.min))
            link(ts(table[0:1, 0, 0:OVERFLOW_BLOCKS // 2], iota_b[0:1, 0:OVERFLOW_BLOCKS // 2], 2.0, None, ALU.mult))
            link(tt(table[0:1, 0, 0:OVERFLOW_BLOCKS // 2], table[0:1, 0, 0:OVERFLOW_BLOCKS // 2],
                    extra_end[0:1, E - 1:E].to_broadcast([1, OVERFLOW_BLOCKS // 2]), ALU.is_lt))
            link(red(tablef[0:1, 0:1], table[0:1, 0, 0:OVERFLOW_BLOCKS // 2], AX.X, ALU.add))
            link(ts(tablef[0:1, 0:1], tablef[0:1, 0:1], float(E // 2 - 2), None, ALU.add))
            link(nc.vector.tensor_copy(keep["blocks"][:], tablef[:]))
            dve.wait_ge(sig("by_block_full"), 1)
            nc.vector.tensor_copy(by_block[:], bank[2][0:BLOCKS, 0:P]).then_inc(sig("by_block"), 1)
            dve.wait_ge(sig("pairs_flipped"), 1)
            link(nc.vector.tensor_copy(token_f[:], bank[3][:, 0:BLOCKS]))
            link(stt(out=pair_f[:], in0=token_f[:], scalar=0.0, in1=free_row[:], op0=ALU.is_equal, op1=ALU.mult))
            link(tt(pair_f[:], pair_f[:], token_f[:], ALU.add))
            link(ts(pair_f[:], pair_f[:], 1.0, None, ALU.subtract))
            link(nc.vector.tensor_copy(keep["row_pair"][:], pair_f[:]))
            link(ts(token_f[:], pair_f[:], float(S), float(-S), ALU.is_ge, ALU.mult))
            link(tt(token_f[:], token_f[:], pair_f[:], ALU.add))
            link(nc.vector.tensor_copy(keep["row_token"][:], token_f[:]))


HALF_K = KT // 2


def load_up(nc, sp, sig, keep, ins, par, q, e):
    for j, name in enumerate(("exp_w1", "exp_w3")):
        w = ins[name][0]
        src = w[e] if isinstance(e, int) else w[bass.ds(e, 1)].rearrange("a k n -> (a k) n")
        src = src.rearrange("(k p) n -> p k n", p=P)[:, q * HALF_K:(q + 1) * HALF_K, :]
        sp.dma_start(keep["w13"][:, par, q * HALF_K:(q + 1) * HALF_K, j, :], src).then_inc(sig(f"w13_in{par}{q}"), 16)


def load_down(nc, sp, sig, keep, ins, par, e):
    w = ins["exp_w2"][0]
    src = w[e] if isinstance(e, int) else w[bass.ds(e, 1)].rearrange("a k n -> (a k) n")
    sp.dma_start(keep["w2"][:, par], src.rearrange("(k p) n -> p k n", p=P)).then_inc(sig(f"w2_in{par}"), 16)


def prefetch_weights(nc, sp, sig, keep, ins):
    for b in range(2):
        for q in range(2):
            load_up(nc, sp, sig, keep, ins, b, q, b)
        load_down(nc, sp, sig, keep, ins, b, b)


def experts(nc, sig, bank, const, keep, ins, dram):
    psum, ident = const["psum"], const["ident"]
    blocks, w13, w2 = keep["blocks"], keep["w13"], keep["w2"]
    FK = FE // P
    RING = 4
    with ExitStack() as ctx:
        sb = lambda name, shape, dt=F32: ctx.enter_context(nc.sbuf_tensor(name, shape, dt))
        x_in = sb("ex_x", [P, 2, D])
        x_t = sb("ex_x_t", [P, 2, 2, KT, P], F32R)
        w_r = sb("ex_w_r", [P, RING, 2, D], F32R)
        sigm = sb("ex_sigm", [P, FE])
        hidden = sb("ex_hidden", [P, FE])
        hid_t = sb("ex_hid_t", [P, 2, 2, FK, P], F32R)
        y = sb("ex_y", [P, 2, D])
        idx = sb("ex_idx", [P, 2, 2], I32)
        spare = sb("ex_spare", [P, 1])
        block = ctx.enter_context(nc.Block("experts"))

        def up_count(blk, n):
            return 16 * blk[1] + (8 * blk[0] + n)

        def down_count(blk, n):
            return 8 * blk[1] + (4 * blk[0] + n)

        def slots(eng, slot):
            inner = eng.value_load(blocks[0:1, 0:1], min_val=E // 2 - 2, max_val=BLOCKS // 2 - 2)
            slot((0, 0), None, (1, 0))
            slot((1, 0), (0, 0), (0, 1))
            slot((0, 1), (1, 0), (1, 1))
            with eng.Fori(1, inner + 1) as j:
                slot((1, j), (0, j), (0, j + 1))
                slot((0, j + 1), (1, j), (1, j + 1))
            slot((1, inner + 1), (0, inner + 1), None)

        @block.sync
        def _(sp):
            inner = sp.value_load(blocks[0:1, 0:1], min_val=E // 2 - 2, max_val=BLOCKS // 2 - 2)
            with sp.Fori(0, inner + 1) as i:
                for par in range(2):
                    e = sp.value_load(blocks[0:1, bass.ds(2 * i + par + 3, 1)], min_val=0, max_val=E - 1)
                    for q in range(2):
                        sp.wait_ge(sig("up_lo"), up_count((par, i), HALF_K * (q + 1)))
                        load_up(nc, sp, sig, keep, ins, par, q, e)
                    sp.wait_ge(sig("down_lo"), down_count((par, i), FK))
                    load_down(nc, sp, sig, keep, ins, par, e)

        @block.gpsimd
        def _(pool):
            def index(kind, table, par, pair):
                b = 2 * pair + par
                src = table[:, b:b + 1] if isinstance(b, int) else table[:, bass.ds(b, 1)]
                nc.gpsimd.tensor_copy(idx[:, kind, par:par + 1], src).then_inc(sig(f"idx{kind}{par}"), 1)
                pool.wait_ge(sig(f"idx{kind}{par}"), pair + 1)
                nc.gpsimd.tensor_tensor(spare[:], const["neghalf"][:, 0:1], const["neghalf"][:, 0:1], ALU.mult)
                return bass.IndirectOffsetOnAxis(ap=idx[:, kind, par:par + 1], axis=0)

            def gather(par, pair):
                if not (isinstance(pair, int) and pair == 0):
                    pool.wait_ge(sig(f"x_flipped{par}"), pair)
                at = index(0, keep["row_token"], par, pair)
                pool.indirect_dma_start(x_in[:, par, :], None, dram["h_mid"], at, bounds_check=S - 1,
                                        oob_is_err=False).then_inc(sig(f"x_in_e{par}"), 16)

            def store(par, pair):
                pool.wait_ge(sig(f"y_e{par}"), pair + 1)
                at = index(1, keep["row_pair"], par, pair)
                pool.indirect_dma_start(dram["pair_rows"], at, y[:, par, :], None, bounds_check=2 * S - 1,
                                        oob_is_err=False).then_inc(sig(f"y_out{par}"), 16)

            inner = pool.value_load(blocks[0:1, 0:1], min_val=E // 2 - 2, max_val=BLOCKS // 2 - 2)
            for par in range(2):
                nc.gpsimd.memset(x_in[:, par, :], 0.0).then_inc(sig("x_zero"), 1)
                pool.wait_ge(sig("x_zero"), par + 1)
                gather(par, 0)
            gather(0, 1)
            store(0, 0)
            gather(1, 1)
            with pool.Fori(0, inner) as j:
                gather(0, j + 2)
                store(1, j)
                gather(1, j + 2)
                store(0, j + 1)
            store(1, inner)
            store(0, inner + 1)
            store(1, inner + 1)
            for q in range(2):
                pool.wait_ge(sig(f"y_out{q}"), 16 * (inner + 2))

        @block.tensor
        def _(pe):
            def product(out, lhs, unit, cols, first, last):
                hi, lo = w_r[:, unit % RING, 0, cols], w_r[:, unit % RING, 1, cols]
                nc.tensor.matmul(out, lhs[0], hi, start=first, stop=False)
                nc.tensor.matmul(out, lhs[0], lo, start=False, stop=False)
                return nc.tensor.matmul(out, lhs[1], hi, start=False, stop=last)

            def flip_x(blk, before):
                pe.wait_ge(sig(f"x_in_e{blk[0]}"), 16 * (blk[1] + 1))
                if before:
                    pe.wait_ge(sig(f"x_lo{before[0]}"), before[1] + 1)
                for k in range(KT):
                    last = nc.tensor.transpose(psum[:, k * P:(k + 1) * P], x_in[:, blk[0], k * P:(k + 1) * P], ident[:])
                last.then_inc(sig(f"x_flipped{blk[0]}"), 1)

            def down(blk, y_before):
                par, pair = blk
                pe.wait_ge(sig(f"hid_lo{par}"), pair + 1)
                if y_before:
                    pe.wait_ge(sig(f"y_e{y_before[0]}"), y_before[1])
                for k in range(FK):
                    pe.wait_ge(sig("down_lo"), down_count(blk, k + 1))
                    for half in range(2):
                        last = product(bank[6 + half], [hid_t[:, par, i, k, :] for i in range(2)], k,
                                       slice(half * NC5, (half + 1) * NC5), k == 0, k == FK - 1)
                    last.then_inc(sig("down_used"), 1)

            def slot(blk, before, behind):
                par, pair = blk
                if not before:
                    flip_x(blk, None)
                pe.wait_ge(sig(f"x_lo{par}"), pair + 1)
                if before:
                    pe.wait_ge(sig(f"hidden{before[0]}"), before[1] + 1)
                for k in range(KT):
                    pe.wait_ge(sig("up_lo"), up_count(blk, k + 1))
                    for j in range(2):
                        last = product(bank[2 + j], [x_t[:, par, i, k, :] for i in range(2)], k,
                                       slice(j * FE, (j + 1) * FE), k == 0, k == KT - 1)
                    last.then_inc(sig("up_used"), 1)
                if behind:
                    flip_x(behind, blk)
                if before:
                    first = isinstance(pair, int) and pair == 0
                    down(before, None if first else (par, pair))
                pe.wait_ge(sig(f"hidden{par}"), pair + 1)
                if before:
                    pe.wait_ge(sig(f"hid_lo{before[0]}"), before[1] + 1)
                for k in range(FK):
                    last = nc.tensor.transpose(bank[4][:, k * P:(k + 1) * P], hidden[:, k * P:(k + 1) * P], ident[:])
                last.then_inc(sig(f"hid_flipped{par}"), 1)
                if not behind:
                    down(blk, (before[0], before[1] + 1))

            slots(pe, slot)

        @block.scalar
        def _(act):
            def copy(out, src):
                return nc.scalar.activation(out, src, ACT.Copy)

            def x_hi(par, pair):
                act.wait_ge(sig(f"x_flipped{par}"), pair + 1)
                copy(x_t[:, par, 0].rearrange("p k t -> p (k t)"), psum[:, 0:D]).then_inc(sig(f"x_hi{par}"), 1)

            def up_hi(blk, units, used):
                for u in units:
                    if u % HALF_K == 0:
                        act.wait_ge(sig(f"w13_in{blk[0]}{u // HALF_K}"), 32 * (blk[1] + 1))
                    if used:
                        act.wait_ge(*used(u))
                    copy(w_r[:, u % RING, 0, :], w13[:, blk[0], u].rearrange("p j n -> p (j n)")).then_inc(sig("up_hi"), 1)

            def down_hi(blk, used):
                act.wait_ge(sig(f"w2_in{blk[0]}"), 16 * (blk[1] + 1))
                for u in range(FK):
                    act.wait_ge(*used(u))
                    copy(w_r[:, u, 0, :], w2[:, blk[0], u, :]).then_inc(sig("down_hi"), 1)

            def move_y(blk):
                par, pair = blk
                act.wait_ge(sig("down_used"), down_count(blk, FK))
                if not (isinstance(pair, int) and pair == 0):
                    act.wait_ge(sig(f"y_out{par}"), 16 * pair)
                copy(y[:, par, :], psum[:, 6 * NC5:8 * NC5]).then_inc(sig(f"y_e{par}"), 1)

            def slot(blk, before, behind):
                par, pair = blk
                if not before:
                    up_hi(blk, range(RING), None)
                    x_hi(*blk)
                up_hi(blk, range(RING, KT), lambda u: (sig("up_used"), up_count(blk, u - RING + 1)))
                if before:
                    down_hi(before, lambda u: (sig("up_used"), up_count(blk, u + RING + 1)))
                act.wait_ge(sig("up_used"), up_count(blk, KT))
                nc.scalar.activation(sigm[:], bank[2], ACT.Sigmoid).then_inc(sig(f"sigm{par}"), 1)
                if behind:
                    x_hi(*behind)
                    if before:
                        up_hi(behind, range(RING), lambda u: (sig("down_used"), down_count(before, u + 1)))
                    else:
                        up_hi(behind, range(RING), lambda u: (sig("up_used"), up_count(blk, u + RING + 1)))
                if before:
                    move_y(before)
                act.wait_ge(sig(f"hid_flipped{par}"), pair + 1)
                copy(hid_t[:, par, 0].rearrange("p k t -> p (k t)"), bank[4]).then_inc(sig(f"hid_hi{par}"), 1)
                if not behind:
                    down_hi(blk, lambda u: (sig("down_used"), down_count(before, u + 1)))
                    move_y(blk)

            slots(act, slot)

        @block.vector
        def _(dve):
            def low(out, whole, high):
                return nc.vector.tensor_tensor(out, whole, high.bitcast(F32), ALU.subtract)

            def x_lo(par, pair):
                dve.wait_ge(sig(f"x_hi{par}"), pair + 1)
                parts = [x_t[:, par, i].rearrange("p k t -> p (k t)") for i in range(2)]
                low(parts[1], psum[:, 0:D], parts[0]).then_inc(sig(f"x_lo{par}"), 1)

            def up_lo(blk, units):
                for u in units:
                    dve.wait_ge(sig("up_hi"), up_count(blk, u + 1))
                    low(w_r[:, u % RING, 1, :], w13[:, blk[0], u].rearrange("p j n -> p (j n)"), w_r[:, u % RING, 0, :]).then_inc(sig("up_lo"), 1)

            def down_lo(blk):
                for u in range(FK):
                    dve.wait_ge(sig("down_hi"), down_count(blk, u + 1))
                    low(w_r[:, u, 1, :], w2[:, blk[0], u, :], w_r[:, u, 0, :]).then_inc(sig("down_lo"), 1)

            def slot(blk, before, behind):
                par, pair = blk
                if not before:
                    up_lo(blk, range(RING))
                    x_lo(*blk)
                up_lo(blk, range(RING, KT))
                if before:
                    down_lo(before)
                dve.wait_ge(sig(f"sigm{par}"), pair + 1)
                nc.vector.tensor_tensor(sigm[:], bank[2], sigm[:], ALU.mult).then_inc(sig(f"silu{par}"), 1)
                dve.wait_ge(sig(f"silu{par}"), pair + 1)
                nc.vector.tensor_tensor(hidden[:], bank[3], sigm[:], ALU.mult).then_inc(sig(f"hidden{par}"), 1)
                if behind:
                    x_lo(*behind)
                    up_lo(behind, range(RING))
                dve.wait_ge(sig(f"hid_hi{par}"), pair + 1)
                parts = [hid_t[:, par, i].rearrange("p k t -> p (k t)") for i in range(2)]
                low(parts[1], bank[4], parts[0]).then_inc(sig(f"hid_lo{par}"), 1)
                if not behind:
                    down_lo(blk)

            slots(dve, slot)


def combine(nc, sig, bank, const, keep, ins, dram, out):
    mod_bc, pair_w = keep["mod_bc"], keep["pair_w"]
    rows = keep["w13"][:].rearrange("p a k j n -> p (a k j n)").rearrange("p (t j n) -> p t j n", t=TT, j=2)
    x_in = keep["w2"][:].rearrange("p a k n -> p (a k) n")
    with ExitStack() as ctx:
        sb = lambda name, shape: ctx.enter_context(nc.sbuf_tensor(name, shape, F32))
        squares = sb("cb_squares", [P, D])
        ms = sb("cb_ms", [P, TT])
        block = ctx.enter_context(nc.Block("combine"))

        @block.sync
        def _(sp):
            for t in range(TT):
                tile = slice(t * P, (t + 1) * P)
                sp.dma_start(rows[:, t], dram["pair_rows"].rearrange("(j s) n -> s j n", j=2)[tile]).then_inc(sig(f"cb_rows_in{t}"), 16)
                sp.dma_start(x_in[:, t, :], dram["x_mid"][tile, :]).then_inc(sig(f"cb_x_in{t}"), 16)
                if t == 0:
                    sp.dma_start(mod_bc[:, 4, :], ins["final_g"].rearrange("(a n) -> a n", a=1).partition_broadcast(P).rearrange("p a n -> p (a n)")).then_inc(sig("fg_in"), 16)
            for t in range(TT):
                sp.wait_ge(sig("cb_out"), t + 1)
                sp.dma_start(out[0, t * P:(t + 1) * P, :], x_in[:, t, :]).then_inc(sig("out_done"), 16)
            sp.wait_ge(sig("out_done"), 16 * TT)

        @block.gpsimd
        def _(pool):
            for s in range(TT + 1):
                if s < TT:
                    pool.wait_ge(sig("cb_sum"), s + 1)
                    nc.gpsimd.tensor_tensor(rows[:, s, 0, :], rows[:, s, 0, :], mod_bc[:, 3, :], ALU.mult).then_inc(sig("cb_gated"), 1)
                if s >= 1:
                    pool.wait_ge(sig("cb_ms"), s)
                    nc.gpsimd.tensor_tensor(ms[:, s - 1:s], ms[:, s - 1:s], const["neghalf"][:, 0:1], ALU.pow).then_inc(sig("cb_rstd"), 1)

        @block.scalar
        def _(act):
            for s in range(TT + 1):
                if s < TT:
                    act.wait_ge(sig(f"cb_rows_in{s}"), 16)
                    nc.scalar.activation(rows[:, s, 0, :], rows[:, s, 0, :], ACT.Copy, scale=pair_w[:, s, 0:1]).then_inc(sig("cb_first"), 1)
                if s >= 1:
                    act.wait_ge(sig("cb_x"), s)
                    if s >= 2:
                        act.wait_ge(sig("cb_ss"), s - 1)
                    nc.scalar.activation(squares[:], x_in[:, s - 1, :], ACT.Square, accum_out=ms[:, s - 1:s]).then_inc(sig("cb_ss"), 1)

        @block.vector
        def _(dve):
            tt, stt, ts = nc.vector.tensor_tensor, nc.vector.scalar_tensor_tensor, nc.vector.tensor_scalar
            for s in range(TT + 2):
                if s < TT:
                    dve.wait_ge(sig("cb_first"), s + 1)
                    a = rows[:, s, 0, :]
                    stt(out=a, in0=rows[:, s, 1, :], scalar=pair_w[:, s, 1:2], in1=a, op0=ALU.mult, op1=ALU.add).then_inc(sig("cb_sum"), 1)
                if 1 <= s <= TT:
                    t = s - 1
                    dve.wait_ge(sig(f"cb_x_in{t}"), 16)
                    dve.wait_ge(sig("cb_gated"), t + 1)
                    tt(x_in[:, t, :], x_in[:, t, :], rows[:, t, 0, :], ALU.add).then_inc(sig("cb_x"), 1)
                if s >= 2:
                    t = s - 2
                    if t == 0:
                        dve.wait_ge(sig("fg_in"), 16)
                    dve.wait_ge(sig("cb_rstd"), t + 1)
                    stt(out=x_in[:, t, :], in0=x_in[:, t, :], scalar=ms[:, t:t + 1], in1=mod_bc[:, 4, :], op0=ALU.mult, op1=ALU.mult).then_inc(sig("cb_out"), 1)
                if 1 <= s <= TT:
                    dve.wait_ge(sig("cb_ss"), s)
                    ts(ms[:, s - 1:s], ms[:, s - 1:s], 1.0 / D, EPS, ALU.mult, ALU.add).then_inc(sig("cb_ms"), 1)


def constants(nc, sig, const):
    with nc.Block("constants") as block:
        @block.gpsimd
        def _(pool):
            nc.gpsimd.memset(const["ident"][:], 0.0).then_inc(sig("const_set"), 1)
            nc.gpsimd.memset(const["ones"][:], 1.0).then_inc(sig("const_set"), 1)
            nc.gpsimd.memset(const["neghalf"][:], -0.5).then_inc(sig("const_set"), 1)
            pool.wait_ge(sig("const_set"), 1)
            nc.gpsimd.affine_select(out=const["ident"][:], in_=const["ident"][:], compare_op=ALU.not_equal, fill=1.0,
                                    base=0, pattern=[[-1, P]], channel_multiplier=1).then_inc(sig("const_set"), 1)
            pool.wait_ge(sig("const_set"), 4)


def build(nc, ins, out):
    dram = {
        "p_rwkv": nc.dram_tensor("p_rwkv", (S + 1, SHIFT), F32, kind="Internal").ap(),
        "qk": nc.dram_tensor("qk", (2, 2, W, S), F32, kind="Internal").ap(),
        "v": nc.dram_tensor("v", (S, W), F32, kind="Internal").ap(),
        "ncum": nc.dram_tensor("ncum", (H, S), F32, kind="Internal").ap(),
        "o_fox_t": nc.dram_tensor("o_fox_t", (W, S), F32, kind="Internal").ap(),
        "o_rwkv": nc.dram_tensor("o_rwkv", (S, W), F32, kind="Internal").ap(),
        "gates": nc.dram_tensor("gates", (S, 2 * D), F32, kind="Internal").ap(),
        "x_mid": nc.dram_tensor("x_mid", (S, D), F32, kind="Internal").ap(),
        "h_mid": nc.dram_tensor("h_mid", (S, D), F32, kind="Internal").ap(),
        "pair_rows": nc.dram_tensor("pair_rows", (2 * S, D), F32, kind="Internal").ap(),
    }
    with ExitStack() as ctx:
        sig = Signals(nc, ctx)
        psum = ctx.enter_context(nc.psum_tensor("psum", [P, 8 * NC5], F32))
        bank = [psum[:, i * NC5:(i + 1) * NC5] for i in range(8)]
        sb = lambda name, shape, dt=F32: ctx.enter_context(nc.sbuf_tensor(name, shape, dt))
        const = {"ident": sb("ident", [P, P]), "ones": sb("ones", [P, P]), "neghalf": sb("neghalf", [P, H]), "psum": psum}
        keep = {"mod_bc": sb("mod_bc", [P, 5, D])}
        keep["logits"] = keep["mod_bc"][:, 4, 0:TT * (G + E)].rearrange("p (t e) -> p t e", e=G + E)
        constants(nc, sig, const)
        sig.next_stage("constants")
        with ExitStack() as early:
            sbe = lambda name, shape, dt=F32: early.enter_context(nc.sbuf_tensor(name, shape, dt))
            keep["ring"] = sbe("w_ring", [P, 2, KT, NC5])
            keep["h_hi"] = sbe("h_hi", [P, KT, S], F32R)
            keep["h_lo"] = sbe("h_lo", [P, KT, S], F32R)
            keep["c_silu"] = sbe("c_silu", [P, KT])
            keep["w_f"] = sbe("w_f", [P, KT, H])
            weights = Ring(sig, keep["ring"], ins)
            modulate(nc, sig, bank, const, keep, ins, dram, weights)
            sig.next_stage("modulate")
            project(nc, sig, bank, const, keep, ins, dram, weights)
            sig.next_stage("project")
        with ExitStack() as mid:
            raw = mid.enter_context(nc.sbuf_tensor("raw", [P, KT, D], F32))
            with ExitStack() as inner:
                ready = recur_buffers(nc, inner, raw)
                attend(nc, sig, bank, const, keep, ins, dram, ready)
                sig.next_stage("attend")
                recur(nc, sig, bank, const, keep, ins, ready, raw, dram)
                sig.next_stage("recur")
            merge(nc, sig, bank, const, keep, ins, dram, raw)
            sig.next_stage("merge")
        with ExitStack() as late:
            sbl = lambda name, shape, dt=F32: late.enter_context(nc.sbuf_tensor(name, shape, dt))
            keep["dest"] = sbl("dest", [P, TT, 2], I32)
            keep["pair_w"] = sbl("pair_w", [P, TT, 2])
            keep["blocks"] = sbl("blocks", [1, 1 + BLOCKS], I32)
            keep["row_token"] = sbl("row_token", [P, BLOCKS], I32)
            keep["row_pair"] = sbl("row_pair", [P, BLOCKS], I32)
            keep["w13"] = sbl("w13", [P, 2, KT, 2, FE])
            keep["w2"] = sbl("w2", [P, 2, FE // P, D])
            route(nc, sig, bank, const, keep, ins, dram)
            sig.next_stage("route")
            experts(nc, sig, bank, const, keep, ins, dram)
            sig.next_stage("experts")
            combine(nc, sig, bank, const, keep, ins, dram, out)


INPUTS = ["x", "c", "ada_w", "ada_b", "norm1_g", "w_in", "fox_forget_b", "shift_mu", "rwkv_w0", "rwkv_w2", "rwkv_a0",
          "rwkv_a2", "rwkv_g2", "rwkv_k_k", "rwkv_k_a", "rwkv_r_k", "ln_x_g", "ln_x_b", "w_out_fox", "w_out_rwkv",
          "w_o", "norm2_g", "router_group_w", "router_group_b", "router_expert_w", "router_expert_b", "exp_w1",
          "exp_w3", "exp_w2", "final_g"]


def kernel(**inputs):
    import numpy as _np
    import concourse.bacc as _bacc
    from concourse import mybir as _mybir
    from concourse.bass_utils import run_bass_kernel_spmd as _run

    nc = _bacc.Bacc("TRN2", target_bir_lowering=False, num_devices=1)
    arrays, aps = {}, {}
    for name in INPUTS:
        a = _np.ascontiguousarray(inputs[name])
        arrays[f"in_{name}"] = a
        aps[name] = nc.dram_tensor(f"in_{name}", a.shape, _mybir.dt.from_np(a.dtype), kind="ExternalInput").ap()
    out = nc.dram_tensor("out", (1, S, D), F32, kind="ExternalOutput").ap()
    build(nc, aps, out)
    r = _run(nc, [arrays], core_ids=[0])
    return r.results[0]["out"]
```
